# Optimizing a Trainium2 kernel written in Bass

```python
import math
import jax
import jax.numpy as jnp
from jax import lax
import numpy as np

D_MODEL = 1024
BATCH = 1
SEQ = 512
DEPTH = 1

PLE_DIM = 256
NSA_HEADS = 8
NSA_KV_GROUPS = 2
NSA_REP = NSA_HEADS // NSA_KV_GROUPS
NSA_HEAD_DIM = 64
NSA_WIDTH = NSA_HEADS * NSA_HEAD_DIM
CMP_BLOCK = 32
CMP_STRIDE = 16
SEL_BLOCK = 64
N_SEL = 16
WINDOW = 512
SEL_Q_CHUNK = 16
MLA_HEADS = 8
Q_LORA = 256
KV_LORA = 128
QK_NOPE = 64
QK_ROPE = 32
V_DIM = 64
MLA_WIDTH = MLA_HEADS * V_DIM
ROPE_THETA = 10000.0
MAX_POS_OFFSET = 4096
D_FF = 2816
CONV_WIDTH = 3
Q_BLOCK = 128
EPS = 1e-6
NEG = -1e30
BIG = 1e9
IN_SIZES = (NSA_WIDTH, 6 * NSA_KV_GROUPS * NSA_HEAD_DIM, 3 * NSA_HEADS, Q_LORA, KV_LORA, QK_ROPE, 2 * D_MODEL)
N_IN = NSA_WIDTH + 6 * NSA_KV_GROUPS * NSA_HEAD_DIM + 3 * NSA_HEADS + Q_LORA + KV_LORA + QK_ROPE + 2 * D_MODEL


def _rmsnorm(x, g):
    xf = x.astype(jnp.float32)
    y = xf * lax.rsqrt(jnp.mean(xf * xf, axis=-1, keepdims=True) + EPS)
    return (y * g.astype(jnp.float32)).astype(x.dtype)

def _masked_softmax(s, mask):
    p = jax.nn.softmax(jnp.where(mask, s, NEG), axis=-1)
    return p * mask.astype(p.dtype)

def _alibi_slopes(n):
    return jnp.asarray(np.array([2.0 ** (-8.0 * (i + 1) / n) for i in range(n)], dtype=np.float32))

def _rope(x, cos, sin):
    half = x.shape[-1] // 2
    x1, x2 = x[..., :half], x[..., half:]
    return jnp.concatenate([x1 * cos - x2 * sin, x2 * cos + x1 * sin], axis=-1)

def _causal_dwconv(u, w, b):
    c = u.shape[-1]
    y = lax.conv_general_dilated(u, w[:, None, :].astype(u.dtype), window_strides=(1,), padding=[(CONV_WIDTH - 1, 0)], dimension_numbers=('NWC', 'WIO', 'NWC'), feature_group_count=c)
    return y + b

def _nsa_mixer(q, kc, vc, ks, vs, kw, vw, gates, pos_k, pos_v, ck_w1, ck_b1, ck_w2, cv_w1, cv_b1, cv_w2):
    B, T = q.shape[0], q.shape[1]
    G, R, dh = NSA_KV_GROUPS, NSA_REP, NSA_HEAD_DIM
    scale = dh ** -0.5
    slopes = _alibi_slopes(NSA_HEADS).reshape(G, R)
    t_idx = jnp.arange(T)

    n_cmp = (T - CMP_BLOCK) // CMP_STRIDE + 1
    blk = jnp.arange(n_cmp)[:, None] * CMP_STRIDE + jnp.arange(CMP_BLOCK)[None, :]

    def compress(k, pos, w1, b1, w2):
        kb = k[:, blk] + pos[None, None, :, None, :]
        kb = kb.transpose(0, 1, 3, 2, 4).reshape(B, n_cmp, G, CMP_BLOCK * dh)
        return jax.nn.gelu(kb @ w1 + b1) @ w2

    k_cmp = compress(kc, pos_k, ck_w1, ck_b1, ck_w2)
    v_cmp = compress(vc, pos_v, cv_w1, cv_b1, cv_w2)
    blk_end = jnp.arange(n_cmp) * CMP_STRIDE + CMP_BLOCK - 1
    dist_c = (t_idx[:, None] - blk_end[None, :]).astype(jnp.float32)
    s_c = jnp.einsum('btgrd,bjgd->bgrtj', q, k_cmp, preferred_element_type=jnp.float32) * scale
    s_c = s_c - slopes[:, :, None, None] * dist_c
    p_cmp = _masked_softmax(s_c, dist_c >= 0)
    o_cmp = jnp.einsum('bgrtj,bjgd->btgrd', p_cmp.astype(v_cmp.dtype), v_cmp)

    n_sb = T // SEL_BLOCK
    per = SEL_BLOCK // CMP_STRIDE
    imp = p_cmp.sum(axis=2)
    imp = jnp.pad(imp, ((0, 0), (0, 0), (0, 0), (0, n_sb * per - n_cmp)))
    imp = imp.reshape(B, G, T, n_sb, per).sum(axis=-1)
    cur = t_idx // SEL_BLOCK
    sb = jnp.arange(n_sb)
    forced = (sb[None, :] == 0) | (sb[None, :] == cur[:, None]) | (sb[None, :] == cur[:, None] - 1)
    future = sb[None, :] > cur[:, None]
    score = jnp.where(forced, BIG, jnp.where(future, -BIG, imp))
    k_sel = min(N_SEL, n_sb)
    _, sel_idx = lax.top_k(score, k_sel)

    ksb = ks.reshape(B, n_sb, SEL_BLOCK, G, dh).transpose(0, 3, 1, 2, 4)
    vsb = vs.reshape(B, n_sb, SEL_BLOCK, G, dh).transpose(0, 3, 1, 2, 4)
    C = SEL_Q_CHUNK
    n_ch = T // C
    q_ch = q.reshape(B, n_ch, C, G, R, dh).transpose(1, 0, 2, 3, 4, 5)
    idx_ch = sel_idx.reshape(B, G, n_ch, C, k_sel).transpose(2, 0, 1, 3, 4)
    t_ch = t_idx.reshape(n_ch, C)
    gather = jax.vmap(jax.vmap(lambda kb, ix: kb[ix]))

    def sel_step(args):
        qc, ic, tc = args
        kg = gather(ksb, ic)
        vg = gather(vsb, ic)
        s = jnp.einsum('bcgrd,bgckld->bgrckl', qc, kg, preferred_element_type=jnp.float32) * scale
        spos = ic[..., None] * SEL_BLOCK + jnp.arange(SEL_BLOCK)
        dist = (tc[None, None, :, None, None] - spos).astype(jnp.float32)
        s = s - slopes[None, :, :, None, None, None] * dist[:, :, None]
        s = s.reshape(B, G, R, C, k_sel * SEL_BLOCK)
        mask = (dist >= 0).reshape(B, G, 1, C, k_sel * SEL_BLOCK)
        pr = _masked_softmax(s, mask).reshape(B, G, R, C, k_sel, SEL_BLOCK)
        return jnp.einsum('bgrckl,bgckld->bcgrd', pr.astype(vg.dtype), vg)

    o_sel = lax.map(sel_step, (q_ch, idx_ch, t_ch))
    o_sel = o_sel.transpose(1, 0, 2, 3, 4, 5).reshape(B, T, G, R, dh)

    n_qb = T // Q_BLOCK
    span = WINDOW + Q_BLOCK
    kw_p = jnp.pad(kw, ((0, 0), (WINDOW, 0), (0, 0), (0, 0)))
    vw_p = jnp.pad(vw, ((0, 0), (WINDOW, 0), (0, 0), (0, 0)))
    q_blk = q.reshape(B, n_qb, Q_BLOCK, G, R, dh).transpose(1, 0, 2, 3, 4, 5)

    def win_step(args):
        qb, i = args
        start = i * Q_BLOCK
        kblk = lax.dynamic_slice_in_dim(kw_p, start, span, axis=1)
        vblk = lax.dynamic_slice_in_dim(vw_p, start, span, axis=1)
        tq = start + jnp.arange(Q_BLOCK)
        sk = start - WINDOW + jnp.arange(span)
        dist = (tq[:, None] - sk[None, :]).astype(jnp.float32)
        mask = (dist >= 0) & (dist < WINDOW) & (sk[None, :] >= 0)
        s = jnp.einsum('bqgrd,bsgd->bgrqs', qb, kblk, preferred_element_type=jnp.float32) * scale
        s = s - slopes[:, :, None, None] * dist
        pr = _masked_softmax(s, mask)
        return jnp.einsum('bgrqs,bsgd->bqgrd', pr.astype(vblk.dtype), vblk)

    o_win = lax.map(win_step, (q_blk, jnp.arange(n_qb, dtype=jnp.int32)))
    o_win = o_win.transpose(1, 0, 2, 3, 4, 5).reshape(B, T, G, R, dh)

    g = jax.nn.sigmoid(gates.astype(jnp.float32)).astype(q.dtype).reshape(B, T, 3, G, R, 1)
    o = g[:, :, 0] * o_cmp + g[:, :, 1] * o_sel + g[:, :, 2] * o_win
    return o.reshape(B, T, NSA_WIDTH)

def _mla_mixer(c_q, c_kv, k_rope, cos, sin, g_q, w_uq, g_kv, w_ukv):
    B, T = c_q.shape[0], c_q.shape[1]
    H = MLA_HEADS
    q = (_rmsnorm(c_q, g_q) @ w_uq).reshape(B, T, H, QK_NOPE + QK_ROPE)
    q_nope = q[..., :QK_NOPE]
    q_rope = _rope(q[..., QK_NOPE:], cos[:, :, None, :], sin[:, :, None, :])
    kv = (_rmsnorm(c_kv, g_kv) @ w_ukv).reshape(B, T, H, QK_NOPE + V_DIM)
    k_nope = kv[..., :QK_NOPE]
    v = kv[..., QK_NOPE:]
    k_r = _rope(k_rope, cos, sin)
    scale = (QK_NOPE + QK_ROPE) ** -0.5
    n_qb = T // Q_BLOCK
    qn_b = q_nope.reshape(B, n_qb, Q_BLOCK, H, QK_NOPE).transpose(1, 0, 2, 3, 4)
    qr_b = q_rope.reshape(B, n_qb, Q_BLOCK, H, QK_ROPE).transpose(1, 0, 2, 3, 4)
    s_idx = jnp.arange(T)

    def step(args):
        qn, qr, i = args
        s = (jnp.einsum('bqhd,bshd->bhqs', qn, k_nope, preferred_element_type=jnp.float32) + jnp.einsum('bqhd,bsd->bhqs', qr, k_r, preferred_element_type=jnp.float32)) * scale
        tq = i * Q_BLOCK + jnp.arange(Q_BLOCK)
        pr = _masked_softmax(s, s_idx[None, :] <= tq[:, None])
        return jnp.einsum('bhqs,bshd->bqhd', pr.astype(v.dtype), v)

    o = lax.map(step, (qn_b, qr_b, jnp.arange(n_qb, dtype=jnp.int32)))
    return o.transpose(1, 0, 2, 3, 4).reshape(B, T, MLA_WIDTH)

def first_inputs(seed: int = 0) -> dict:
    key = jax.random.key(seed)
    ks = jax.random.split(key, 40)
    f32 = jnp.float32

    def nrm(k, shape, fan_in):
        return jax.random.normal(k, shape, f32) * (fan_in ** -0.5)

    def gain(k, n):
        return 1.0 + 0.05 * jax.random.normal(k, (DEPTH, n), f32)

    def small(k, shape, s):
        return s * jax.random.normal(k, shape, f32)

    L = DEPTH
    dh = NSA_HEAD_DIM
    offs = jax.random.randint(ks[2], (BATCH, 1), 0, MAX_POS_OFFSET, dtype=jnp.int32)
    return {
        'x': jax.random.normal(ks[0], (BATCH, SEQ, D_MODEL), f32),
        'p': jax.random.normal(ks[1], (DEPTH, BATCH, SEQ, PLE_DIM), f32),
        'positions': offs + jnp.arange(SEQ, dtype=jnp.int32)[None, :],
        'g_pre_mix': gain(ks[3], D_MODEL),
        'w_in': nrm(ks[4], (L, D_MODEL, N_IN), D_MODEL),
        'nsa_pos_k': small(ks[5], (L, CMP_BLOCK, dh), 0.1),
        'nsa_pos_v': small(ks[6], (L, CMP_BLOCK, dh), 0.1),
        'nsa_ck_w1': nrm(ks[7], (L, CMP_BLOCK * dh, dh), CMP_BLOCK * dh),
        'nsa_ck_b1': small(ks[8], (L, dh), 0.02),
        'nsa_ck_w2': nrm(ks[9], (L, dh, dh), dh),
        'nsa_cv_w1': nrm(ks[10], (L, CMP_BLOCK * dh, dh), CMP_BLOCK * dh),
        'nsa_cv_b1': small(ks[11], (L, dh), 0.02),
        'nsa_cv_w2': nrm(ks[12], (L, dh, dh), dh),
        'mla_g_q': gain(ks[13], Q_LORA),
        'mla_w_uq': nrm(ks[14], (L, Q_LORA, MLA_HEADS * (QK_NOPE + QK_ROPE)), Q_LORA),
        'mla_g_kv': gain(ks[15], KV_LORA),
        'mla_w_ukv': nrm(ks[16], (L, KV_LORA, MLA_HEADS * (QK_NOPE + V_DIM)), KV_LORA),
        'w_br_nsa': nrm(ks[17], (L, NSA_WIDTH, D_MODEL), NSA_WIDTH),
        'w_br_mla': nrm(ks[18], (L, MLA_WIDTH, D_MODEL), MLA_WIDTH),
        'w_o': nrm(ks[19], (L, D_MODEL, D_MODEL), D_MODEL),
        'g_post_mix': gain(ks[20], D_MODEL),
        'g_pre_ffn': gain(ks[21], D_MODEL),
        'w_up': nrm(ks[22], (L, D_MODEL, 2 * D_FF), D_MODEL),
        'w_conv': nrm(ks[23], (L, CONV_WIDTH, 2 * D_FF), CONV_WIDTH),
        'b_conv': small(ks[24], (L, 2 * D_FF), 0.02),
        'w_down': nrm(ks[25], (L, D_FF, D_MODEL), D_FF),
        'g_post_ffn': gain(ks[26], D_MODEL),
        'w_ple': nrm(ks[27], (L, PLE_DIM, D_MODEL), PLE_DIM),
        'w_ple_gate': nrm(ks[28], (L, D_MODEL, D_MODEL), D_MODEL),
        'g_ple': gain(ks[29], D_MODEL),
    }

def first_block(x, p, positions, g_pre_mix, w_in, nsa_pos_k, nsa_pos_v, nsa_ck_w1, nsa_ck_b1, nsa_ck_w2, nsa_cv_w1, nsa_cv_b1, nsa_cv_w2, mla_g_q, mla_w_uq, mla_g_kv, mla_w_ukv, w_br_nsa, w_br_mla, w_o, g_post_mix, g_pre_ffn, w_up, w_conv, b_conv, w_down, g_post_ffn, w_ple, w_ple_gate, g_ple):
    B, T, D = x.shape
    G, R, dh = NSA_KV_GROUPS, NSA_REP, NSA_HEAD_DIM
    offsets = [int(v) for v in np.cumsum(np.array(IN_SIZES))[:-1]]
    inv_freq = ROPE_THETA ** (-jnp.arange(0, QK_ROPE, 2, dtype=jnp.float32) / QK_ROPE)
    ang = positions.astype(jnp.float32)[..., None] * inv_freq
    cos = jnp.cos(ang).astype(x.dtype)
    sin = jnp.sin(ang).astype(x.dtype)
    for i in range(DEPTH):
        h = _rmsnorm(x, g_pre_mix[i])
        proj = h @ w_in[i]
        q_n, kv_n, gate_n, c_q, c_kv, k_r, merge = jnp.split(proj, offsets, axis=-1)
        q_n = q_n.reshape(B, T, G, R, dh)
        kv_n = kv_n.reshape(B, T, 6, G, dh)
        o_nsa = _nsa_mixer(q_n, kv_n[:, :, 0], kv_n[:, :, 1], kv_n[:, :, 2], kv_n[:, :, 3], kv_n[:, :, 4], kv_n[:, :, 5], gate_n, nsa_pos_k[i], nsa_pos_v[i], nsa_ck_w1[i], nsa_ck_b1[i], nsa_ck_w2[i], nsa_cv_w1[i], nsa_cv_b1[i], nsa_cv_w2[i])
        o_mla = _mla_mixer(c_q, c_kv, k_r, cos, sin, mla_g_q[i], mla_w_uq[i], mla_g_kv[i], mla_w_ukv[i])
        gm = jax.nn.sigmoid(merge.astype(jnp.float32)).astype(x.dtype).reshape(B, T, 2, D)
        merged = gm[:, :, 0] * (o_nsa @ w_br_nsa[i]) + gm[:, :, 1] * (o_mla @ w_br_mla[i])
        x = x + _rmsnorm(merged @ w_o[i], g_post_mix[i])
        h = _rmsnorm(x, g_pre_ffn[i])
        u = _causal_dwconv(h @ w_up[i], w_conv[i], b_conv[i])
        a, v = u[..., :D_FF], u[..., D_FF:]
        x = x + _rmsnorm((jax.nn.gelu(a) * v) @ w_down[i], g_post_ffn[i])
        e = p[i] @ w_ple[i]
        gate = jax.nn.sigmoid((x @ w_ple_gate[i]).astype(jnp.float32)).astype(x.dtype)
        x = x + _rmsnorm(e * gate, g_ple[i])
    return x


D_MIX = D_MODEL
HEAD_DIM = 64
D_HYENA = D_MIX // 2
D_FOURIER = D_MIX - D_HYENA
N_HYENA_HEADS = D_HYENA // HEAD_DIM
N_FOURIER_GROUPS = D_FOURIER // HEAD_DIM
N_MIX_HEADS = N_HYENA_HEADS + N_FOURIER_GROUPS
D_IN_PROJ = 3 * D_HYENA + D_FOURIER
SHORT_CONV = 3
FILTER_EMB = 33
FILTER_BANDS = (FILTER_EMB - 1) // 2
FILTER_ORDER = 64
N_INNER_MLPS = 2
DECAY_FAST_PCT = 0.3
DECAY_SLOW_PCT = 1.5
DECAY_TARGET = 1e-2
N_GROUPS = 4
EXPERTS_PER_GROUP = 8
N_EXPERTS = N_GROUPS * EXPERTS_PER_GROUP
TOP_K = 2
D_EXPERT = D_MODEL // 2
MOE_BLOCK = 128


def rmsnorm(x, g):
    xf = x.astype(jnp.float32)
    y = xf * lax.rsqrt(jnp.mean(xf * xf, axis=-1, keepdims=True) + EPS)
    return (y * g.astype(jnp.float32)).astype(x.dtype)

def short_conv_centred(u, w, b):
    L = u.shape[1]
    half = SHORT_CONV // 2
    up = jnp.pad(u, ((0, 0), (half, half), (0, 0)))
    y = b
    for k in range(SHORT_CONV):
        y = y + up[:, k:k + L] * w[k]
    return y

def hyena_filters(L, f_w_in, f_b_in, f_w_mid, f_b_mid, f_freq, f_w_out):
    t = jnp.linspace(0.0, 1.0, L, dtype=jnp.float32)[:, None]
    w = (2.0 * math.pi / L) * jnp.arange(L, dtype=jnp.float32)[:, None]
    f = jnp.linspace(1e-4, FILTER_BANDS - 1, FILTER_BANDS, dtype=jnp.float32)[None, :]
    z = jnp.concatenate([t, jnp.cos(f * w), -jnp.sin(f * w)], axis=-1)
    h = jnp.sin(f_freq[0] * (z @ f_w_in + f_b_in))
    for i in range(N_INNER_MLPS):
        h = jnp.sin(f_freq[i + 1] * (h @ f_w_mid[i] + f_b_mid[i]))
    h = (h @ f_w_out).astype(jnp.float32).reshape(L, 2, D_HYENA)
    max_decay = math.log(DECAY_TARGET) / DECAY_FAST_PCT
    min_decay = math.log(DECAY_TARGET) / DECAY_SLOW_PCT
    deltas = jnp.abs(jnp.linspace(min_decay, max_decay, D_HYENA, dtype=jnp.float32))
    decay = jnp.exp(-t * deltas)
    h = h * decay[:, None, :]
    return h[:, 0], h[:, 1]

def bidirectional_long_conv(u, h_fwd, h_bwd):
    L = u.shape[1]
    k = jnp.concatenate([h_fwd, jnp.zeros_like(h_fwd[:1]), h_bwd[:0:-1]], axis=0)
    k = k / jnp.sum(jnp.abs(k), axis=0, keepdims=True)
    k_f = jnp.fft.rfft(k, n=2 * L, axis=0)
    u_f = jnp.fft.rfft(u, n=2 * L, axis=1)
    return jnp.fft.irfft(u_f * k_f[None], n=2 * L, axis=1)[:, :L]

def hyena_mixer(u, conv_w, conv_b, f_w_in, f_b_in, f_w_mid, f_b_mid, f_freq, f_w_out, f_bias):
    uc = short_conv_centred(u, conv_w, conv_b).astype(jnp.float32)
    x0, x1, v = jnp.split(uc, 3, axis=-1)
    h_fwd, h_bwd = hyena_filters(u.shape[1], f_w_in, f_b_in, f_w_mid, f_b_mid, f_freq, f_w_out)
    z = x1 * v
    z = bidirectional_long_conv(z, h_fwd, h_bwd) + z * f_bias.astype(jnp.float32)
    return x0 * z

def fourier_mixer(u):
    B, L, _ = u.shape
    ug = u.astype(jnp.float32).reshape(B, L, N_FOURIER_GROUPS, HEAD_DIM)
    y = jnp.fft.fftn(ug, axes=(1, 3), norm='ortho').real
    return y.reshape(B, L, D_FOURIER)

def head_rmsnorm(y, g):
    B, L, _ = y.shape
    yh = y.reshape(B, L, N_MIX_HEADS, HEAD_DIM)
    yh = yh * lax.rsqrt(jnp.mean(yh * yh, axis=-1, keepdims=True) + EPS)
    return yh.reshape(B, L, D_MIX) * g.astype(jnp.float32)

def mixer_sublayer(x, norm_g, w_in, conv_w, conv_b, f_w_in, f_b_in, f_w_mid, f_b_mid, f_freq, f_w_out,
                   f_bias, mix_g, w_out):
    h = rmsnorm(x, norm_g)
    proj = h @ w_in
    y_hyena = hyena_mixer(proj[..., :3 * D_HYENA], conv_w, conv_b, f_w_in, f_b_in, f_w_mid, f_b_mid,
                          f_freq, f_w_out, f_bias)
    y_fourier = fourier_mixer(proj[..., 3 * D_HYENA:])
    y = head_rmsnorm(jnp.concatenate([y_hyena, y_fourier], axis=-1), mix_g).astype(x.dtype)
    return x + y @ w_out

def hierarchical_moe(h, w_group, b_group, w_router, b_router, w_gate, w_up, w_down):
    B, L, D = h.shape
    T = B * L
    tok = h.reshape(T, D)
    g_logits = (tok @ w_group).astype(jnp.float32) + b_group.astype(jnp.float32)
    g_sel = jnp.argmax(g_logits, axis=-1)
    p_group = jnp.take_along_axis(jax.nn.softmax(g_logits, axis=-1), g_sel[:, None], axis=-1)[:, 0]
    e_logits = jnp.einsum('td,gde->tge', tok, w_router).astype(jnp.float32) + b_router.astype(jnp.float32)
    e_logits = jnp.take_along_axis(e_logits, g_sel[:, None, None], axis=1)[:, 0]
    top_l, top_i = lax.top_k(e_logits, TOP_K)
    weight = p_group[:, None] * jax.nn.softmax(top_l, axis=-1)
    expert = (g_sel[:, None] * EXPERTS_PER_GROUP + top_i).astype(jnp.int32)

    P = T * TOP_K
    flat_e = expert.reshape(P)
    flat_t = jnp.repeat(jnp.arange(T, dtype=jnp.int32), TOP_K)
    flat_w = weight.reshape(P)
    order = jnp.argsort(flat_e)
    se = flat_e[order]
    counts = jnp.bincount(flat_e, length=N_EXPERTS).astype(jnp.int32)
    starts = jnp.cumsum(counts) - counts
    padded = ((counts + MOE_BLOCK - 1) // MOE_BLOCK) * MOE_BLOCK
    pad_ends = jnp.cumsum(padded)
    pad_starts = pad_ends - padded
    dest = pad_starts[se] + (jnp.arange(P, dtype=jnp.int32) - starts[se])
    n_blocks = -(-P // MOE_BLOCK) + N_EXPERTS
    n_rows = n_blocks * MOE_BLOCK
    row_tok = jnp.zeros((n_rows,), jnp.int32).at[dest].set(flat_t[order])
    row_w = jnp.zeros((n_rows,), jnp.float32).at[dest].set(flat_w[order])
    block_start = jnp.arange(n_blocks, dtype=jnp.int32) * MOE_BLOCK
    block_e = jnp.minimum(jnp.searchsorted(pad_ends, block_start, side='right'), N_EXPERTS - 1)

    def expert_block(args):
        e, rows_tok, rows_w = args
        xb = tok[rows_tok]
        a = xb @ w_gate[e]
        u = xb @ w_up[e]
        y = (jax.nn.silu(a) * u) @ w_down[e]
        return (y * rows_w[:, None].astype(y.dtype)).astype(tok.dtype)

    ys = lax.map(expert_block, (block_e, row_tok.reshape(n_blocks, MOE_BLOCK), row_w.reshape(n_blocks, MOE_BLOCK)))
    out = jnp.zeros((T, D), tok.dtype).at[row_tok].add(ys.reshape(n_rows, D))
    return out.reshape(B, L, D)

def second_inputs(seed: int = 0) -> dict:
    key = jax.random.key(seed)
    ks = jax.random.split(key, 24)
    f32 = jnp.float32
    n = lambda k, shape, s: (jax.random.normal(k, shape, f32) * s)
    return {
        'x': n(ks[0], (BATCH, SEQ, D_MODEL), 1.0),
        'norm1_g': 1.0 + n(ks[1], (DEPTH, D_MODEL), 0.02),
        'w_in': n(ks[2], (DEPTH, D_MODEL, D_IN_PROJ), D_MODEL ** -0.5),
        'conv_w': n(ks[3], (DEPTH, SHORT_CONV, 3 * D_HYENA), SHORT_CONV ** -0.5),
        'conv_b': n(ks[4], (DEPTH, 3 * D_HYENA), 0.02),
        'f_w_in': n(ks[5], (DEPTH, FILTER_EMB, FILTER_ORDER), FILTER_EMB ** -0.5),
        'f_b_in': n(ks[6], (DEPTH, FILTER_ORDER), 0.1),
        'f_w_mid': n(ks[7], (DEPTH, N_INNER_MLPS, FILTER_ORDER, FILTER_ORDER), FILTER_ORDER ** -0.5),
        'f_b_mid': n(ks[8], (DEPTH, N_INNER_MLPS, FILTER_ORDER), 0.1),
        'f_freq': 1.0 + n(ks[9], (DEPTH, N_INNER_MLPS + 1, FILTER_ORDER), 0.1),
        'f_w_out': n(ks[10], (DEPTH, FILTER_ORDER, 2 * D_HYENA), FILTER_ORDER ** -0.5),
        'f_bias': n(ks[11], (DEPTH, D_HYENA), 1.0),
        'mix_g': 1.0 + n(ks[12], (DEPTH, D_MIX), 0.02),
        'w_out': n(ks[13], (DEPTH, D_MIX, D_MODEL), D_MIX ** -0.5),
        'norm2_g': 1.0 + n(ks[14], (DEPTH, D_MODEL), 0.02),
        'w_group': n(ks[15], (DEPTH, D_MODEL, N_GROUPS), D_MODEL ** -0.5),
        'b_group': n(ks[16], (DEPTH, N_GROUPS), 0.01),
        'w_router': n(ks[17], (DEPTH, N_GROUPS, D_MODEL, EXPERTS_PER_GROUP), D_MODEL ** -0.5),
        'b_router': n(ks[18], (DEPTH, N_GROUPS, EXPERTS_PER_GROUP), 0.01),
        'w_gate': n(ks[19], (DEPTH, N_EXPERTS, D_MODEL, D_EXPERT), D_MODEL ** -0.5),
        'w_up': n(ks[20], (DEPTH, N_EXPERTS, D_MODEL, D_EXPERT), D_MODEL ** -0.5),
        'w_down': n(ks[21], (DEPTH, N_EXPERTS, D_EXPERT, D_MODEL), D_EXPERT ** -0.5),
        'final_g': 1.0 + n(ks[22], (D_MODEL,), 0.02),
    }

def second_block(x, norm1_g, w_in, conv_w, conv_b, f_w_in, f_b_in, f_w_mid, f_b_mid, f_freq, f_w_out, f_bias,
              mix_g, w_out, norm2_g, w_group, b_group, w_router, b_router, w_gate, w_up, w_down, final_g):
    for i in range(DEPTH):
        x = mixer_sublayer(x, norm1_g[i], w_in[i], conv_w[i], conv_b[i], f_w_in[i], f_b_in[i], f_w_mid[i],
                           f_b_mid[i], f_freq[i], f_w_out[i], f_bias[i], mix_g[i], w_out[i])
        x = x + hierarchical_moe(rmsnorm(x, norm2_g[i]), w_group[i], b_group[i], w_router[i], b_router[i],
                                 w_gate[i], w_up[i], w_down[i])
    return rmsnorm(x, final_g)


def setup_inputs(seed=0):
    out = dict(first_inputs(seed))
    for name, value in second_inputs(seed + 1).items():
        if name != "x":
            out[name + "_2"] = value
    return out


def reference(
    x, p, positions, g_pre_mix, w_in, nsa_pos_k, nsa_pos_v, nsa_ck_w1, nsa_ck_b1, nsa_ck_w2,
    nsa_cv_w1, nsa_cv_b1, nsa_cv_w2, mla_g_q, mla_w_uq, mla_g_kv, mla_w_ukv, w_br_nsa, w_br_mla,
    w_o, g_post_mix, g_pre_ffn, w_up, w_conv, b_conv, w_down, g_post_ffn, w_ple, w_ple_gate,
    g_ple, norm1_g_2, w_in_2, conv_w_2, conv_b_2, f_w_in_2, f_b_in_2, f_w_mid_2, f_b_mid_2,
    f_freq_2, f_w_out_2, f_bias_2, mix_g_2, w_out_2, norm2_g_2, w_group_2, b_group_2,
    w_router_2, b_router_2, w_gate_2, w_up_2, w_down_2, final_g_2,
):
    x = first_block(
        x, p, positions, g_pre_mix, w_in, nsa_pos_k, nsa_pos_v, nsa_ck_w1, nsa_ck_b1, nsa_ck_w2,
        nsa_cv_w1, nsa_cv_b1, nsa_cv_w2, mla_g_q, mla_w_uq, mla_g_kv, mla_w_ukv, w_br_nsa,
        w_br_mla, w_o, g_post_mix, g_pre_ffn, w_up, w_conv, b_conv, w_down, g_post_ffn, w_ple,
        w_ple_gate, g_ple,
    )
    return second_block(
        x, norm1_g_2, w_in_2, conv_w_2, conv_b_2, f_w_in_2, f_b_in_2, f_w_mid_2, f_b_mid_2,
        f_freq_2, f_w_out_2, f_bias_2, mix_g_2, w_out_2, norm2_g_2, w_group_2, b_group_2,
        w_router_2, b_router_2, w_gate_2, w_up_2, w_down_2, final_g_2,
    )


_drawn_inputs = setup_inputs


def setup_inputs(seed=0):
    import zlib

    import numpy as np

    out = dict(_drawn_inputs(seed))
    spreads = {}
    factors = {'nsa_pos_k': 5.247,
     'nsa_ck_b1': 8.0,
     'nsa_cv_b1': 3.381,
     'b_conv': 2.717,
     'norm1_g_2': 3.368,
     'conv_b_2': 3.219,
     'f_b_in_2': 4.641,
     'f_b_mid_2': 3.717,
     'f_freq_2': 5.31,
     'mix_g_2': 4.229,
     'norm2_g_2': 4.277,
     'b_group_2': 4.987,
     'b_router_2': 7.997,
     'final_g_2': 2.947}
    for name, (base, spread) in spreads.items():
        noise = np.random.default_rng([zlib.crc32(name.encode()), seed]).standard_normal(out[name].shape)
        drawn = base * np.exp(spread * noise) if base else spread * noise
        out[name] = jnp.asarray(drawn.astype(out[name].dtype))
    for name, factor in factors.items():
        out[name] = (out[name] * factor).astype(out[name].dtype)
    return out
```

```python
from contextlib import ExitStack

import numpy as np
import concourse.bass as bass
from concourse import mybir

F32 = mybir.dt.float32
I32 = mybir.dt.int32
ALU = mybir.AluOpType
ACT = mybir.ActivationFunctionType
AX = mybir.AxisListType

P = 128
T = 512
NT = T // P
D = 1024
ND = D // P
EPS = 1e-6
NEG = -1e30
HEADS = 8
DH = 64
N_CMP = (T - 32) // 16 + 1
QK = 96
QK_SCALE = float(QK) ** -0.5
D_FF = 2816
NF = D_FF // P
N_EXP = 32
CH = 512
RING = 12

W_PROJ_FM = 0
W_PROJ_MLA = W_PROJ_FM + 8
W_PROJ_V = W_PROJ_MLA + 4
W_CMP = W_PROJ_V + 3
W_UQ = W_CMP + 4
W_UKV = W_UQ + 2
W_MERGE = W_UKV + 1
W_O = W_MERGE + 24
W_UP = W_O + 8
W_DOWN = W_UP + 2 * NF
W_PLE = W_DOWN + NF
W_PGATE = W_PLE + 2
W_IN2 = W_PGATE + 8
W_DFT = W_IN2 + 16
W_IDFT = W_DFT + 5
W_FFT = W_IDFT + 4
W_OUT2 = W_FFT + 4
W_ROUTE = W_OUT2 + 8
W_EXP = W_ROUTE + 1
N_TILES = W_EXP + 12 * N_EXP
assert W_EXP % RING == 0 and N_TILES % RING == 0

COLS = [("g_pre_mix", 8), ("g_pre_ffn", 8), ("norm1", 8), ("norm2", 8), ("mix_g", 8), ("g_q", 2), ("g_kv", 1),
        ("w_conv", 3 * 2 * NF), ("b_conv", 2 * NF), ("conv_w", 3 * 12), ("conv_b", 12), ("b1k", 1), ("b1v", 1),
        ("w2k", 64), ("w2v", 64), ("pos_k", 32), ("pos_v", 32), ("f_b_in", 1), ("f_freq", 3), ("f_b_mid", 2),
        ("f_w_in", 64), ("f_w_mid", 128), ("r_bias", 36)]
COL = {}
_at = 0
for _n, _w in COLS:
    COL[_n] = (_at, _at + _w)
    _at += _w
N_COLS = _at

CSTS = [("ident", 128), ("ones", 128), ("diag", 128), ("alibi", 512), ("inv_freq", 16), ("row_ok", 1),
        ("dft64", 256), ("giota", 4), ("eiota", 32)]
CST = {}
_at = 0
for _n, _w in CSTS:
    CST[_n] = (_at, _at + _w)
    _at += _w
N_CST = _at

SLOPES = [2.0 ** (-(h + 1)) for h in range(HEADS)]

SEMS = """p3_prod norm_ss norm_ms norm_rt norm_xn post_mm post_ss post_ms post_rt post_x turned copied_dve copied_act w_used small_in x_in tab_in pos_in g_in p_in decay_in out_st dve_chain
proj_fm_ev proj_mla_ev proj_v_ev
cmp_blocks cmp_gelu cmp_kv cmp_ready
ang_ready sin_ready mla_ms mla_rt mla_norm mla_tr mla_tr_ev mla_up q_ev kv_ev q_raw qk_tr qk_ev_act qk_ev_dve
cs_mm cs_max cs_exp cs_tr cs_tr_ev cs_pv cs_o
at_s at_max at_exp at_tr at_ev_dve at_ev_act at_pv at_o
mg_sig mg_ev
up_conv up_dve up_gelu up_g
ple_mm ple_ev pg_mm pg_sig
in2_lin in2_conv in2_f z_ready f_in fb_in
fm_mm fm_arg fm_sin fo_mm fo_ev habs hs_mm hs_ready pm_ready
kf_mm kf_ev y_ready yo_ev fd_mm fd_ev fo2_ev hn_sq hn_ms hn_rt hn_y wo2_mm wo2_x
rt_lg rt_g rt_d rt_exp ex_sig ex_hid ex_dn ex_acc fin_y""".split()
NORMS = ["n1", "n2", "n3", "n4", "n5"]
POSTS = ["p1", "p2", "p3"]
TURNS = {}
_at = 0
for _n, _w in (("n1", 8), ("o_nsa", 4), ("o_mla", 4), ("n2", 8), ("x2", 8), ("n3", 8), ("z", 4), ("x0", 4), ("y2", 8), ("n4", 8)):
    TURNS[_n] = (_at, _w)
    _at += _w


def build(nc, last_stage, N_STREAM, W, x, cols, csts, cmp_tab, pos, grows, pT, fconst, fwout, decay, frow, out):
    ctx = ExitStack()
    with ctx:
        def sem(name):
            return ctx.enter_context(nc.semaphore(name))

        def sb(name, shape, dt=F32):
            return ctx.enter_context(nc.sbuf_tensor(name, shape, dt))

        S = {n: sem(n) for n in SEMS}
        landed = [sem(f"w_landed{s}") for s in range(RING)]

        pb = ctx.enter_context(nc.psum_tensor("banks", [P, 8, 512], F32))
        ring = sb("ring", [P, RING, 1024])
        X = sb("resid", [P, NT, D])
        hT = sb("hT", [P, ND, T])
        colt = sb("colt", [P, N_COLS])
        cst = sb("cst", [P, N_CST])
        grow = sb("grow", [P, D])
        junk = sb("junk", [P, 1024])
        st = sb("st", [P, 640])
        posi = sb("posi", [P, NT], I32)
        arena = sb("arena", [P, 28100])

        def col(name, a=0, w=1):
            o = COL[name][0] + a
            return colt[:, o:o + w]

        def cs(name):
            return cst[:, CST[name][0]:CST[name][1]]

        def ar(off, n):
            return arena[:, off:off + n]

        def ar3(off, a, b):
            return arena[:, off:off + a * b].rearrange("p (a b) -> p a b", a=a)

        ident = cs("ident")
        ss = st[:, 0:4]
        ms = st[:, 4:8]
        rt = st[:, 8:12]
        rstd = st[:, 12:16]
        sums = st[:, 16:112].rearrange("p (w h) -> p w h", w=12)
        nm = st[:, 112:116].rearrange("p (u h) -> p u h", u=2)
        fac = st[:, 116:148]
        csum = st[:, 148:180]
        cmaxn = st[:, 180:212]
        mss = st[:, 212:220]
        mrt = st[:, 220:228]
        mrs = st[:, 228:236]
        hns = st[:, 236:300]
        hnr = st[:, 300:364]
        hni = st[:, 364:428]

        xn = ar3(0, NT, D)
        qT = ar3(0, 4, T)
        kvT = ar3(2048, 4, T)
        Vsw = ar3(4096, NT, 256)
        cqkv = ar3(5120, NT, 416)
        gates = ar3(6784, NT, 24)
        qTm = ar3(6880, HEADS, T)
        kTm = ar3(10976, HEADS, T)
        Vm = ar3(15072, NT, 512)
        O_nsa = ar3(17120, NT, 512)
        O_mla = ar3(19168, NT, 512)
        cqT = ar3(17120, 3, T)
        chat = ar3(18656, NT, 384)
        Pr = ar(21216, 2048).rearrange("p (u h k) -> p u h k", u=2, h=2)
        PTs = ar(23264, 2048).rearrange("p (u h k) -> p u h k", u=2, h=2)
        qkt = ar(21216, 3072).rearrange("p (u w c) -> p u w c", u=2, w=2)
        ropet = ar(24300, 1000)
        cmpt = ar(25312, 992)
        kb = ar(21216, 1984).rearrange("p (w l j) -> p w l j", w=2, l=32)
        Pc = ar(21216, 1024).rearrange("p (i h j) -> p i h j", i=NT, h=HEADS)
        PcT = ar(22240, 1024).rearrange("p (i c) -> p i c", i=NT)
        Vbd = ar(26304, 512).rearrange("p (g c) -> p g c", g=2)
        kcT = ar(26816, 32)
        gk = ar(26848, 32)
        gv4 = ar(26880, 128)
        oTn = ar3(6880, 4, T)
        oTm = ar3(8928, 4, T)
        mT = ar3(10976, ND, T)
        mgt = ar(0, 4096).rearrange("p (u k c) -> p u k c", u=2, k=4)
        ptmp = ar3(21216, 2, 1024)
        gT = ar3(4096, NF, T)
        cva = ar(15360, 2048).rearrange("p (u k c) -> p u k c", u=2, k=2)
        ga = ar3(17408, 2, T)
        pTs = ar3(24000, 2, T)
        E = ar3(0, NT, D)
        Gs = ar3(4096, NT, D)

        def tile(n):
            return ring[:, n % RING, :]

        def arrived(pe, n):
            pe.wait_ge(landed[n % RING], 16 * (n // RING + 1))


        uc = ar3(0, 12, T)
        uF = ar3(6144, 4, T)
        zt = ar3(8192, NT, CH)
        x0t = ar3(10240, NT, CH)
        Pk = ar3(12288, NT, CH)
        Mk = ar3(14336, NT, CH)
        HF = ar3(16384, NT, CH)
        HB = ar3(18432, NT, CH)
        prod = ar3(16384, 4, CH)
        Y = ar3(16384, NT, D)
        decs = ar3(20480, NT, CH)
        absb = ar(22528, 2048).rearrange("p (u c) -> p u c", u=2)
        vCS = ar(20480, 4096).rearrange("p (i w c) -> p i w c", i=NT, w=2)
        Kt = ar(24576, 2048).rearrange("p (u w c) -> p u w c", u=2, w=2)
        Kn = ar(26624, 512)
        YA = ar3(0, 4, CH)
        YB = ar3(2048, 4, CH)
        ysq = ar3(0, NT, D)
        yt = ar(4096, 2048).rearrange("p (u w c) -> p u w c", u=2, w=2)
        fws = ar(6144, 1024)
        fzs = ar(26624, 512)
        farg, fturn, fred, fh = [ar(24576 + 512 * q, 512)[0:64, :] for q in range(4)]
        hid = ar3(0, 4, T)
        sil = ar3(4096, 2, T)
        xo = ar3(8192, NT, D)
        fbias, rsum_b = grow[:, 0:512], grow[:, 512:1024]
        RT = ar(5120, 2000)
        lg = RT[:, 0:144].rearrange("p (i c) -> p i c", i=NT)
        gate_w = RT[:, 144:272].rearrange("p (i e) -> p i e", i=NT)

        def second_pool(pool):
            pool.wait_ge(S["p3_prod"], NT)
            pool.dma_start(fws[0:64, :], fwout).then_inc(S["f_in"], 16)
            pool.dma_start(fzs, fconst).then_inc(S["f_in"], 16)
            pool.wait_ge(S["post_x"], 3 * NT)
            pool.dma_start(ar(20480, 2048), decay).then_inc(S["decay_in"], 16)
            pool.dma_start(fbias, frow).then_inc(S["fb_in"], 16)
            pool.wait_ge(S["yo_ev"], NT)
            pool.dma_start(grow[:, :], grows[3, :, :]).then_inc(S["g_in"], 16)
            for i in range(NT):
                pool.wait_ge(S["fin_y"], i + 1)
                pool.dma_start(out[i * P:(i + 1) * P, :], xo[:, i, :]).then_inc(S["out_st"], 16)
            pool.wait_ge(S["out_st"], 16 * NT)

        def second_pe(pe):
            used = S["w_used"]
            pe.wait_ge(S["pg_sig"], NT)
            pe.wait_ge(S["f_in"], 32)
            nc.tensor.matmul(pb[0:64, 0, :], col("f_w_in", 0, 64)[0:33, :], fzs[0:33, :], start=True, stop=True)\
                .then_inc(S["fm_mm"], 1)
            for q in range(2):
                pe.wait_ge(S["fm_sin"], q + 1)
                nc.tensor.matmul(pb[0:64, q + 1, :], col("f_w_mid", 64 * q, 64)[0:64, :], fh, start=True, stop=True)\
                    .then_inc(S["fm_mm"], 1)
            pe.wait_ge(S["fm_sin"], 3)
            for i in range(NT):
                for h in range(2):
                    last = nc.tensor.matmul(pb[:, 2 * i + h, :], fh[:, i * P:(i + 1) * P], fws[0:64, h * 512:(h + 1) * 512],
                                            start=True, stop=True)
                last.then_inc(S["fo_mm"], 1)
            pe.wait_ge(S["fo_ev"], NT)
            for i in range(NT):
                pe.wait_ge(S["habs"], i + 1)
                for h in range(2):
                    last = nc.tensor.matmul(pb[:, 0, :], cs("ones"), absb[:, i % 2, h * 512:(h + 1) * 512],
                                            start=(i == 0 and h == 0), stop=(i == NT - 1 and h == 1))
                last.then_inc(S["hs_mm"], 1)
            pe.wait_ge(S["norm_xn"], 3 * NT)
            pe.wait_ge(S["hs_ready"], 1)
            tr_pe(pe, "n3", xn, NT, ND)
            tr_wait(pe, "n3")
            for m in range(16):
                n = W_IN2 + m
                arrived(pe, n)
                if m >= 8:
                    pe.wait_ge(S["in2_conv"], m - 7)
                for k in range(ND):
                    last = nc.tensor.matmul(pb[:, m % 8, :], tile(n)[:, k * P:(k + 1) * P], hT[:, k, :],
                                            start=(k == 0), stop=(k == ND - 1))
                last.then_inc(used, 1)
            pe.wait_ge(S["in2_conv"], 12)
            pe.wait_ge(S["in2_f"], 4)
            for i in range(NT):
                for w in range(2):
                    for m in range(4):
                        last = nc.tensor.matmul(pb[:, 2 * i + w, m * P:(m + 1) * P], uF[:, m, i * P:(i + 1) * P],
                                                cs("dft64")[:, w * P:(w + 1) * P], start=True, stop=True)
                last.then_inc(S["fd_mm"], 1)
            pe.wait_ge(S["fd_ev"], NT)
            pe.wait_ge(S["z_ready"], 4)
            tr_pe(pe, "z", uc[:, 4:8, :], 4, NT)
            tr_pe(pe, "x0", uc[:, 0:4, :], 4, NT, bank0=4)
            tr_wait(pe, "z")
            tr_wait(pe, "x0")
            pe.wait_ge(S["pm_ready"], 1)
            arrived(pe, W_DFT)
            for m in range(4):
                b = 4 * (m % 2)
                n = W_DFT + 1 + m
                arrived(pe, n)
                if m == 1:
                    pe.wait_ge(S["kf_ev"], 3)
                if m >= 2:
                    pe.wait_ge(S["y_ready"], m - 1)
                for w, src in ((0, Pk), (1, Mk)):
                    for k in range(NT):
                        last = nc.tensor.matmul(pb[:, b + w, :], tile(n)[:, (4 * w + k) * P:(4 * w + k + 1) * P], src[:, k, :],
                                                start=(k == 0), stop=(k == NT - 1))
                    last.then_inc(S["kf_mm"], 1)
                if m == 0:
                    for k in range(NT):
                        last = nc.tensor.matmul(pb[:, 4, :], tile(W_DFT)[:, k * P:(k + 1) * P], Pk[:, k, :],
                                                start=(k == 0), stop=(k == NT - 1))
                    last.then_inc(S["kf_mm"], 1)
                for w in range(2):
                    basis = tile(W_DFT) if m == 0 and w == 1 else tile(n)
                    for k in range(NT):
                        last = nc.tensor.matmul(pb[:, b + 2 + w, :], basis[:, (4 * w + k) * P:(4 * w + k + 1) * P], zt[:, k, :],
                                                start=(k == 0), stop=(k == NT - 1))
                last.then_inc(used, 2 if m == 0 else 1)
            pe.wait_ge(S["y_ready"], 4)
            for i in range(NT):
                n = W_IDFT + i
                arrived(pe, n)
                for w, src in ((0, YA), (1, YB)):
                    for k in range(NT):
                        last = nc.tensor.matmul(pb[:, i, :], tile(n)[:, (4 * w + k) * P:(4 * w + k + 1) * P], src[:, k, :],
                                                start=(w == 0 and k == 0), stop=(w == 1 and k == NT - 1))
                last.then_inc(used, 1)
            for i in range(NT):
                n = W_FFT + i
                arrived(pe, n)
                for w in range(2):
                    for k in range(NT):
                        last = nc.tensor.matmul(pb[:, 4 + i, :], tile(n)[:, (4 * w + k) * P:(4 * w + k + 1) * P], vCS[:, k, w, :],
                                                start=(w == 0 and k == 0), stop=(w == 1 and k == NT - 1))
                last.then_inc(used, 1)
            pe.wait_ge(S["hn_y"], NT)
            tr_pe(pe, "y2", Y, NT, ND)
            tr_wait(pe, "y2")
            tokens_pe(pe, W_OUT2, ND, hT, S["wo2_mm"])
            pe.wait_ge(S["norm_xn"], 4 * NT)
            tr_pe(pe, "n4", xn, NT, ND)
            tr_wait(pe, "n4")
            arrived(pe, W_ROUTE)
            for i in range(NT):
                for k in range(ND):
                    last = nc.tensor.matmul(pb[:, i, 0:36], hT[:, k, i * P:(i + 1) * P], tile(W_ROUTE)[:, 36 * k:36 * k + 36],
                                            start=(k == 0), stop=(k == ND - 1))
            last.then_inc(used, 1)
            pe.wait_ge(S["rt_lg"], 1)
            with pe.Fori(0, N_EXP) as e:
                for f in range(4):
                    if f >= 2:
                        pe.wait_ge(S["ex_hid"], e * 4 + (f - 1))
                    for w in range(2):
                        s = 2 * f + w
                        pe.wait_ge(landed[s], e * 16 + 16 * (W_EXP // RING + 1))
                        for k in range(ND):
                            last = nc.tensor.matmul(pb[:, 2 * (f % 2) + w, :], ring[:, s, k * P:(k + 1) * P], hT[:, k, :],
                                                    start=(k == 0), stop=(k == ND - 1))
                        last.then_inc(used, 1)
                pe.wait_ge(S["ex_hid"], e * 4 + 4)
                for s in range(8, 12):
                    pe.wait_ge(landed[s], e * 16 + 16 * (W_EXP // RING + 1))
                for i in range(NT):
                    if i != 1:
                        pe.wait_ge(S["ex_acc"], e * 4 + (max(i - 1, 0) + 1))
                    for h in range(2):
                        for k in range(4):
                            last = nc.tensor.matmul(pb[:, 4 + 2 * (i % 2) + h, :], hid[:, k, i * P:(i + 1) * P],
                                                    ring[:, 8 + k, h * 512:(h + 1) * 512], start=(k == 0), stop=(k == 3))
                    if i < NT - 1:
                        last.then_inc(S["ex_dn"], 1)
                last.then_inc(used, 4)

        def second_act(act):
            for q in range(3):
                act.wait_ge(S["fm_arg"], q + 1)
                nc.scalar.activation(fh, fred, ACT.Sin).then_inc(S["fm_sin"], 1)
            for i in range(NT):
                act.wait_ge(S["fo_ev"], i + 1)
                if i >= 2:
                    act.wait_ge(S["hs_mm"], i - 1)
                nc.scalar.activation(absb[:, i % 2, 0:512], HF[:, i, :], ACT.Abs)
                nc.scalar.activation(absb[:, i % 2, 512:1024], HB[:, i, :], ACT.Abs).then_inc(S["habs"], 1)
            norm_act(act, "n3", S["post_x"], 3 * NT)
            tr_act(act, "n3", hT, ND, "norm1")
            for m in range(16):
                act.wait_ge(S["w_used"], W_IN2 + m + 1)
                if m < 12:
                    nc.scalar.activation(uc[:, m, :], pb[:, m % 8, :], ACT.Identity, scale=col("conv_w", 12 + m),
                                         bias=col("conv_b", m)).then_inc(S["in2_lin"], 1)
                else:
                    nc.scalar.activation(uF[:, m - 12, :], pb[:, m % 8, :], ACT.Copy).then_inc(S["in2_f"], 1)
            for i in range(NT):
                act.wait_ge(S["fd_mm"], i + 1)
                nc.scalar.activation(vCS[:, i, :, :], pb[:, 2 * i:2 * i + 2, :], ACT.Copy).then_inc(S["fd_ev"], 1)
            tr_act(act, "z", zt, NT)
            tr_act(act, "x0", x0t, NT, bank0=4)
            count = 0
            for m in range(4):
                if m >= 2:
                    act.wait_ge(S["y_ready"], m - 1)
                for w in range(3 if m == 0 else 2):
                    count += 1
                    act.wait_ge(S["kf_mm"], count)
                    src = pb[:, 4, :] if w == 2 else pb[:, 4 * (m % 2) + w, :]
                    nc.scalar.activation(Kn if w == 2 else Kt[:, m % 2, w, :], src, ACT.Copy).then_inc(S["kf_ev"], 1)
            for i in range(NT):
                act.wait_ge(S["w_used"], W_FFT + i + 1)
                act.wait_ge(S["y_ready"], 4)
                nc.scalar.activation(Y[:, i, 512:1024], pb[:, 4 + i, :], ACT.Copy).then_inc(S["fo2_ev"], 1)
            for i in range(NT):
                act.wait_ge(S["yo_ev"], i + 1)
                act.wait_ge(S["fo2_ev"], i + 1)
                nc.scalar.activation(ysq[:, i, :], Y[:, i, :], ACT.Square).then_inc(S["hn_sq"], 1)
            act.wait_ge(S["hn_ms"], 1)
            nc.scalar.activation(hnr, hns, ACT.Sqrt).then_inc(S["hn_rt"], 1)
            tr_act(act, "y2", hT, ND, "mix_g")
            norm_act(act, "n4", S["wo2_x"], NT)
            tr_act(act, "n4", hT, ND, "norm2")
            act.wait_ge(S["rt_g"], 1)
            nc.scalar.activation(RT[:, 288:304], RT[:, 272:288], ACT.Exp).then_inc(S["rt_exp"], 1)
            act.wait_ge(S["rt_d"], 1)
            nc.scalar.activation(RT[:, 308:312], RT[:, 304:308], ACT.Exp).then_inc(S["rt_exp"], 1)
            with act.Fori(0, N_EXP) as e:
                for f in range(4):
                    act.wait_ge(S["w_used"], e * 12 + (W_EXP + 2 * f + 1))
                    nc.scalar.activation(sil[:, f % 2, :], pb[:, 2 * (f % 2), :], ACT.Silu).then_inc(S["ex_sig"], 1)
            norm_act(act, "n5", S["ex_acc"], NT * N_EXP + 1)

        def second_dve(dve, chain):
            def L(ins):
                link(dve, chain, ins)

            TT, TS, STT = nc.vector.tensor_tensor, nc.vector.tensor_scalar, nc.vector.scalar_tensor_tensor
            for q in range(3):
                dve.wait_ge(S["fm_mm"], q + 1)
                b = col("f_b_in") if q == 0 else col("f_b_mid", q - 1)
                L(TS(farg, pb[0:64, q, :], b[0:64, :], col("f_freq", q)[0:64, :], ALU.add, ALU.mult))
                reduce_angle(L, nc, farg, fturn, fred)
                TS(fred, fred, PI_LOW, -PI_LOW, ALU.min, ALU.max).then_inc(S["fm_arg"], 1)
            dve.wait_ge(S["decay_in"], 16)
            for i in range(NT):
                dve.wait_ge(S["fo_mm"], i + 1)
                TT(HF[:, i, :], pb[:, 2 * i, :], decs[:, i, :], ALU.mult)
                ins = TT(HB[:, i, :], pb[:, 2 * i + 1, :], decs[:, i, :], ALU.mult)
                if i == 0:
                    L(ins)
                    ins = nc.vector.memset(HB[0:1, 0, :], 0.0)
                ins.then_inc(S["fo_ev"], 1)
                dve.wait_ge(S["fo_ev"], i + 1)
            for i in range(NT):
                TT(Pk[:, i, :], HF[:, i, :], HB[:, i, :], ALU.add)
                last = TT(Mk[:, i, :], HF[:, i, :], HB[:, i, :], ALU.subtract)
            last.then_inc(S["pm_ready"], 1)
            dve.wait_ge(S["hs_mm"], NT)
            dve.wait_ge(S["fb_in"], 16)
            L(nc.vector.reciprocal(rsum_b, pb[:, 0, :]))
            TS(rsum_b, rsum_b, 2.0 / (2 * T), None, ALU.mult).then_inc(S["hs_ready"], 1)
            norm_dve(dve, chain, "n3")
            tr_dve(dve, "n3", hT, ND, "norm1")
            for m in range(12):
                dve.wait_ge(S["in2_lin"], m + 1)
                u = pb[:, m % 8, :]
                L(STT(out=uc[:, m, 1:T], in0=u[:, 0:T - 1], scalar=col("conv_w", m), in1=uc[:, m, 1:T],
                      op0=ALU.mult, op1=ALU.add))
                STT(out=uc[:, m, 0:T - 1], in0=u[:, 1:T], scalar=col("conv_w", 24 + m), in1=uc[:, m, 0:T - 1],
                    op0=ALU.mult, op1=ALU.add).then_inc(S["in2_conv"], 1)
                if m >= 8:
                    dve.wait_ge(S["in2_conv"], m + 1)
                    TT(uc[:, m - 4, :], uc[:, m - 4, :], uc[:, m, :], ALU.mult).then_inc(S["z_ready"], 1)
            tr_dve(dve, "z", zt, NT)
            tr_dve(dve, "x0", x0t, NT, bank0=4)
            for m in range(4):
                b = 4 * (m % 2)
                dve.wait_ge(S["kf_ev"], 3 + 2 * m)
                dve.wait_ge(S["w_used"], W_DFT + 2 + m)
                if m:
                    dve.wait_ge(S["y_ready"], m)
                KA, KB = Kt[:, m % 2, 0, :], Kt[:, m % 2, 1, :]
                ZA, ZB = pb[:, b + 2, :], pb[:, b + 3, :]
                TT(prod[:, 0, :], ZA, KA, ALU.mult)
                TT(prod[:, 1, :], ZB, KB, ALU.mult)
                TT(prod[:, 2, :], ZA, KB, ALU.mult)
                L(TT(prod[:, 3, :], ZB, Kn if m == 0 else KA, ALU.mult))
                TT(YA[:, m, :], prod[:, 0, :], prod[:, 1, :], ALU.subtract)
                TT(YB[:, m, :], prod[:, 2, :], prod[:, 3, :], ALU.add).then_inc(S["y_ready"], 1)
            dve.wait_ge(S["y_ready"], 4)
            for i in range(NT):
                dve.wait_ge(S["w_used"], W_IDFT + i + 1)
                TT(yt[:, i % 2, 0, :], pb[:, i, :], rsum_b, ALU.mult)
                L(TT(yt[:, i % 2, 1, :], zt[:, i, :], fbias, ALU.mult))
                L(TT(yt[:, i % 2, 0, :], yt[:, i % 2, 0, :], yt[:, i % 2, 1, :], ALU.add))
                TT(Y[:, i, 0:512], yt[:, i % 2, 0, :], x0t[:, i, :], ALU.mult).then_inc(S["yo_ev"], 1)
                dve.wait_ge(S["yo_ev"], i + 1)
            for i in range(NT):
                dve.wait_ge(S["hn_sq"], i + 1)
                ins = nc.vector.tensor_reduce(hni[:, 16 * i:16 * i + 16], ysq[:, i, :].rearrange("p (h c) -> p h c", c=64),
                                              AX.X, ALU.add)
            L(ins)
            TS(hns, hni, 1.0 / 64, EPS, ALU.mult, ALU.add).then_inc(S["hn_ms"], 1)
            dve.wait_ge(S["hn_rt"], 1)
            L(nc.vector.reciprocal(hni, hnr))
            for i in range(NT):
                y = Y[:, i, :].rearrange("p (h c) -> p h c", c=64)
                TT(y, y, hni[:, 16 * i:16 * i + 16].unsqueeze(2).broadcast_to([P, 16, 64]), ALU.mult).then_inc(S["hn_y"], 1)
            tr_dve(dve, "y2", hT, ND, "mix_g")
            for i in range(NT):
                product(dve, S["wo2_mm"], 0, i, W_ROUTE - 1)
                TT(X[:, i, :], X[:, i, :], pair(i), ALU.add).then_inc(S["wo2_x"], 1)
            dve.wait_ge(S["wo2_x"], NT)
            norm_dve(dve, chain, "n4")
            tr_dve(dve, "n4", hT, ND, "norm2")
            dve.wait_ge(S["w_used"], W_EXP)
            b4 = [P, NT, 4]
            TT(lg, pb[:, 0:4, 0:36], col("r_bias", 0, 36).unsqueeze(1).broadcast_to([P, NT, 36]), ALU.add)\
                .then_inc(S["rt_lg"], 1)
            dve.wait_ge(S["rt_lg"], 1)
            glog = lg[:, :, 0:4]
            elog = lg[:, :, 4:36]

            def by_t(a, n):
                return RT[:, a:a + NT * n].rearrange("p (i c) -> p i c", i=NT)

            def first_of(src, n, iota, best, mark, low, hot):
                L(nc.vector.tensor_reduce(best, src, AX.X, ALU.max))
                L(TT(mark, src, best.unsqueeze(2).broadcast_to([P, NT, n]), ALU.is_equal))
                L(STT(out=mark, in0=mark, scalar=-64.0, in1=iota.unsqueeze(1).broadcast_to([P, NT, n]), op0=ALU.mult, op1=ALU.add))
                L(nc.vector.tensor_reduce(low, mark, AX.X, ALU.min))
                L(TT(hot, mark, low.unsqueeze(2).broadcast_to([P, NT, n]), ALU.is_equal))

            gbest, low, ghot, gmark = RT[:, 312:316], RT[:, 316:320], by_t(320, 4), by_t(336, 4)
            first_of(glog, 4, cs("giota"), gbest, gmark, low, ghot)
            TT(by_t(272, 4), glog, gbest.unsqueeze(2).broadcast_to(b4), ALU.subtract).then_inc(S["rt_g"], 1)
            L(TS(gmark, ghot, -NEG, NEG, ALU.mult, ALU.add))
            masked, mark, hot1, hot2 = by_t(352, 32), by_t(480, 32), by_t(608, 32), by_t(736, 32)
            for i in range(NT):
                ins = TT(masked[:, i, :].rearrange("p (g c) -> p g c", g=4), elog[:, i, :].rearrange("p (g c) -> p g c", g=4),
                         gmark[:, i, :].unsqueeze(2).broadcast_to([P, 4, 8]), ALU.add)
            L(ins)
            best1, best2 = RT[:, 864:868], RT[:, 868:872]
            first_of(masked, 32, cs("eiota"), best1, mark, low, hot1)
            L(STT(out=masked, in0=hot1, scalar=2 * NEG, in1=masked, op0=ALU.mult, op1=ALU.add))
            first_of(masked, 32, cs("eiota"), best2, mark, low, hot2)
            TT(RT[:, 304:308], best2, best1, ALU.subtract).then_inc(S["rt_d"], 1)
            dve.wait_ge(S["rt_exp"], 2)
            L(nc.vector.tensor_reduce(RT[:, 872:876], by_t(288, 4), AX.X, ALU.add))
            L(TS(RT[:, 876:880], RT[:, 308:312], 1.0, None, ALU.add))
            L(TT(RT[:, 872:876], RT[:, 872:876], RT[:, 876:880], ALU.mult))
            L(nc.vector.reciprocal(RT[:, 880:884], RT[:, 872:876]))
            L(TT(RT[:, 884:888], RT[:, 880:884], RT[:, 308:312], ALU.mult))
            L(TT(hot1, hot1, RT[:, 880:884].unsqueeze(2).broadcast_to([P, NT, 32]), ALU.mult))
            L(TT(hot2, hot2, RT[:, 884:888].unsqueeze(2).broadcast_to([P, NT, 32]), ALU.mult))
            TT(gate_w, hot1, hot2, ALU.add).then_inc(S["ex_acc"], 1)
            with dve.Fori(0, N_EXP) as e:
                for f in range(4):
                    dve.wait_ge(S["w_used"], e * 12 + (W_EXP + 2 * f + 2))
                    dve.wait_ge(S["ex_sig"], e * 4 + (f + 1))
                    TT(hid[:, f, :], sil[:, f % 2, :], pb[:, 2 * (f % 2) + 1, :], ALU.mult).then_inc(S["ex_hid"], 1)
                for i in range(NT):
                    if i < NT - 1:
                        dve.wait_ge(S["ex_dn"], e * 3 + (i + 1))
                    else:
                        dve.wait_ge(S["w_used"], e * 12 + (W_EXP + 12))
                    dve.wait_ge(S["ex_acc"], e * 4 + 1)
                    STT(out=X[:, i, :], in0=pb[:, 4 + 2 * (i % 2):6 + 2 * (i % 2), :].rearrange("p b c -> p (b c)"),
                        scalar=RT[:, bass.ds(e + (144 + 32 * i), 1)], in1=X[:, i, :], op0=ALU.mult, op1=ALU.add)\
                        .then_inc(S["ex_acc"], 1)
            dve.wait_ge(S["norm_ss"], 5 * NT)
            TS(ms, ss, 1.0 / D, EPS, ALU.mult, ALU.add).then_inc(S["norm_ms"], 1)
            dve.wait_ge(S["norm_rt"], 5)
            dve.wait_ge(S["g_in"], 64)
            L(nc.vector.reciprocal(rstd, rt))
            for i in range(NT):
                STT(out=xo[:, i, :], in0=X[:, i, :], scalar=rstd[:, i:i + 1], in1=grow[:, :], op0=ALU.mult, op1=ALU.mult)\
                    .then_inc(S["fin_y"], 1)

        block = ctx.enter_context(nc.Block())

        @block.sync
        def _(sp):
            for s in range(RING):
                sp.dma_start(ring[:, s, :], W[s, :, :]).then_inc(landed[s], 16)
            with sp.Fori(1, N_STREAM // RING) as turn:
                for s in range(RING):
                    sp.wait_ge(S["w_used"], turn * RING + (s + 1 - RING))
                    sp.dma_start(ring[:, s, :], W[turn * RING + s, :, :]).then_inc(landed[s], 16)
            if last_stage < 8:
                for s in range(RING):
                    sp.wait_ge(landed[s], 16 * (N_STREAM // RING))

        @block.gpsimd
        def _(pool):
            pool.dma_start(colt[:, :], cols).then_inc(S["small_in"], 16)
            pool.dma_start(cst[:, :], csts).then_inc(S["small_in"], 16)
            pool.dma_start(posi[:, :], pos).then_inc(S["pos_in"], 16)
            pool.dma_start(cmpt, cmp_tab).then_inc(S["tab_in"], 16)
            pool.dma_start(grow[:, :], grows[0, :, :]).then_inc(S["g_in"], 16)
            if last_stage >= 5:
                pool.wait_ge(S["post_x"], 1 * NT)
                pool.dma_start(ar(24000, 1024), pT).then_inc(S["p_in"], 16)
                pool.dma_start(grow[:, :], grows[1, :, :]).then_inc(S["g_in"], 16)
            if last_stage >= 7:
                pool.wait_ge(S["post_x"], 2 * NT)
                pool.dma_start(grow[:, :], grows[2, :, :]).then_inc(S["g_in"], 16)
            if last_stage >= 8:
                second_pool(pool)

        def norm_act(act, n, ready, count):
            act.wait_ge(ready, count)
            for i in range(NT):
                if NT * NORMS.index(n) + i:
                    act.wait_ge(S["norm_ss"], NT * NORMS.index(n) + i)
                nc.scalar.activation(junk[:, :], X[:, i, :], ACT.Square, accum_out=ss[:, i:i + 1])\
                    .then_inc(S["norm_ss"], 1)
            act.wait_ge(S["norm_ms"], NORMS.index(n) + 1)
            nc.scalar.activation(rt, ms, ACT.Sqrt).then_inc(S["norm_rt"], 1)

        def link(dve, chain, ins):
            chain[0] += 1
            ins.then_inc(S["dve_chain"], 1)
            dve.wait_ge(S["dve_chain"], chain[0])

        def norm_dve(dve, chain, n):
            at = NORMS.index(n)
            dve.wait_ge(S["norm_ss"], NT * (at + 1))
            nc.vector.tensor_scalar(ms, ss, 1.0 / D, EPS, ALU.mult, ALU.add).then_inc(S["norm_ms"], 1)
            dve.wait_ge(S["norm_rt"], at + 1)
            link(dve, chain, nc.vector.reciprocal(rstd, rt))
            for i in range(NT):
                nc.vector.tensor_scalar(xn[:, i, :], X[:, i, :], rstd[:, i:i + 1], None, ALU.mult)\
                    .then_inc(S["norm_xn"], 1)

        def tr_pe(pe, n, src, A, B, bank0=0):
            for b in range(B):
                for a in range(A):
                    last = nc.tensor.transpose(pb[:, bank0 + b, a * P:(a + 1) * P], src[:, a, b * P:(b + 1) * P], ident)
                last.then_inc(S["turned"], 1)

        def tr_dve(dve, n, dst, B, gain=None, bank0=0):
            for b in range(0, B, 2):
                dve.wait_ge(S["turned"], TURNS[n][0] + b + 1)
                if gain:
                    ins = nc.vector.tensor_scalar(dst[:, b, :], pb[:, bank0 + b, :], col(gain, b), None, ALU.mult)
                else:
                    ins = nc.vector.tensor_copy(dst[:, b, :], pb[:, bank0 + b, :])
                ins.then_inc(S["copied_dve"], 1)

        def tr_act(act, n, dst, B, gain=None, bank0=0):
            for b in range(1, B, 2):
                act.wait_ge(S["turned"], TURNS[n][0] + b + 1)
                nc.scalar.activation(dst[:, b, :], pb[:, bank0 + b, :], ACT.Copy, scale=col(gain, b) if gain else 1.0)\
                    .then_inc(S["copied_act"], 1)

        def tr_wait(eng, n):
            eng.wait_ge(S["copied_dve"], sum(TURNS[n]) // 2)
            eng.wait_ge(S["copied_act"], sum(TURNS[n]) // 2)

        def tokens_pe(pe, base, K, src, done):
            for k in range(K):
                arrived(pe, base + k)
                for i in range(NT):
                    for h in range(2):
                        last = nc.tensor.matmul(pb[:, 2 * i + h, :], src[:, k, i * P:(i + 1) * P],
                                                tile(base + k)[:, h * 512:(h + 1) * 512],
                                                start=(k == 0), stop=(k == K - 1))
                    if k == K - 1 and i < NT - 1:
                        last.then_inc(done, 1)
                last.then_inc(S["w_used"], 1)

        def product(eng, sem, before, i, last_tile):
            if i < NT - 1:
                eng.wait_ge(sem, (NT - 1) * before + i + 1)
            else:
                eng.wait_ge(S["w_used"], last_tile + 1)

        def pair(i):
            return pb[:, 2 * i:2 * i + 2, :].rearrange("p b c -> p (b c)")

        def post_act(act, n, src, last_tile=None):
            at = POSTS.index(n)
            for i in range(NT):
                if last_tile is None:
                    act.wait_ge(S["p3_prod"], i + 1)
                else:
                    product(act, S["post_mm"], at, i, last_tile)
                if i:
                    act.wait_ge(S["post_ss"], NT * at + i)
                nc.scalar.activation(junk[:, :], src(i), ACT.Square, accum_out=ss[:, i:i + 1])\
                    .then_inc(S["post_ss"], 1)
            act.wait_ge(S["post_ms"], at + 1)
            nc.scalar.activation(rt, ms, ACT.Sqrt).then_inc(S["post_rt"], 1)

        def post_dve(dve, chain, n, src, load):
            at = POSTS.index(n)
            dve.wait_ge(S["post_ss"], NT * (at + 1))
            nc.vector.tensor_scalar(ms, ss, 1.0 / D, EPS, ALU.mult, ALU.add).then_inc(S["post_ms"], 1)
            dve.wait_ge(S["g_in"], 16 * load)
            dve.wait_ge(S["post_rt"], at + 1)
            link(dve, chain, nc.vector.reciprocal(rstd, rt))
            for i in range(NT):
                link(dve, chain, nc.vector.scalar_tensor_tensor(out=ptmp[:, i % 2, :], in0=src(i), scalar=rstd[:, i:i + 1],
                                                                in1=grow[:, :], op0=ALU.mult, op1=ALU.mult))
                nc.vector.tensor_tensor(X[:, i, :], X[:, i, :], ptmp[:, i % 2, :], ALU.add).then_inc(S["post_x"], 1)

        UNITS = [(i, kind, pr) for i in range(NT) for kind in range(3) for pr in range(4)]

        @block.tensor
        def _(pe):
            used = S["w_used"]
            pe.wait_ge(S["small_in"], 32)
            pe.wait_ge(S["norm_xn"], 1 * NT)
            tr_pe(pe, "n1", xn, NT, ND)
            tr_wait(pe, "n1")
            for m in range(8):
                arrived(pe, W_PROJ_FM + m)
                for k in range(ND):
                    last = nc.tensor.matmul(pb[:, m, :], tile(W_PROJ_FM + m)[:, k * P:(k + 1) * P], hT[:, k, :],
                                            start=(k == 0), stop=(k == ND - 1))
                last.then_inc(used, 1)
            pe.wait_ge(S["proj_fm_ev"], 4)
            for k in range(ND):
                n = W_PROJ_MLA + k // 2
                arrived(pe, n)
                for i in range(NT):
                    last = nc.tensor.matmul(pb[:, i, 0:416], hT[:, k, i * P:(i + 1) * P],
                                            tile(n)[:, (k % 2) * 416:(k % 2 + 1) * 416], start=(k == 0), stop=(k == ND - 1))
                if k % 2:
                    last.then_inc(used, 1)
            pe.wait_ge(S["proj_fm_ev"], 8)
            for k in range(ND):
                n = W_PROJ_V + k // 3
                arrived(pe, n)
                for i in range(NT):
                    last = nc.tensor.matmul(pb[:, 4 + i, 0:280], hT[:, k, i * P:(i + 1) * P],
                                            tile(n)[:, (k % 3) * 280:(k % 3 + 1) * 280], start=(k == 0), stop=(k == ND - 1))
                if k % 3 == 2 or k == ND - 1:
                    last.then_inc(used, 1)
            pe.wait_ge(S["cmp_blocks"], 4)
            pe.wait_ge(S["proj_mla_ev"], NT)
            for w in range(2):
                for half in range(2):
                    n = W_CMP + 2 * w + half
                    arrived(pe, n)
                    for l in range(16 * half, 16 * half + 16):
                        for g in range(2):
                            last = nc.tensor.matmul(pb[g * 64:g * 64 + 64, w, 0:31],
                                                    tile(n)[g * 64:g * 64 + 64, (l % 16) * 64:(l % 16 + 1) * 64],
                                                    kb[g * 64:g * 64 + 64, w, l, :], start=(l == 0), stop=(l == 31))
                    last.then_inc(used, 1)
            pe.wait_ge(S["cmp_gelu"], 5)
            for g in range(2):
                r = slice(g * 64, g * 64 + 64)
                nc.tensor.matmul(pb[r, 2, 0:31], col("w2k", 0, 64)[r, :], gk[r, 0:31], start=True, stop=True)
                last = nc.tensor.matmul(pb[:, 3 * (1 - g), 0:64], gv4[r, :], col("w2v", 0, 64)[r, :], start=True, stop=True)
            last.then_inc(S["cmp_kv"], 1)
            pe.wait_ge(S["proj_v_ev"], 2)
            pe.wait_ge(S["mla_norm"], 1)
            for b in range(3):
                for i in range(NT):
                    last = nc.tensor.transpose(pb[:, 4 + b, i * P:(i + 1) * P], chat[:, i, b * P:(b + 1) * P], ident)
                last.then_inc(S["mla_tr"], 1)
            pe.wait_ge(S["mla_tr_ev"], 3)
            pe.wait_ge(S["cmp_ready"], 1)
            for n in (W_UQ, W_UQ + 1, W_UKV):
                arrived(pe, n)
            for i in range(NT):
                if i:
                    pe.wait_ge(S["q_ev"], i)
                    pe.wait_ge(S["kv_ev"], i)
                for h in range(2):
                    for k in range(2):
                        nc.tensor.matmul(pb[:, h, 0:384], cqT[:, k, i * P:(i + 1) * P],
                                         tile(W_UQ + k)[:, h * 384:(h + 1) * 384], start=(k == 0), stop=(k == 1))
                for h in range(2):
                    last = nc.tensor.matmul(pb[:, 2 + h, :], cqT[:, 2, i * P:(i + 1) * P],
                                            tile(W_UKV)[:, h * 512:(h + 1) * 512], start=True, stop=True)
                last.then_inc(S["mla_up"], 1)
                pe.wait_ge(S["q_ev"], i + 1)
                pe.wait_ge(S["kv_ev"], i + 1)
                if i:
                    pe.wait_ge(S["qk_ev_act"], 2 * i)
                    pe.wait_ge(S["qk_ev_dve"], 2 * i)
                for w in range(2):
                    for b in range(2):
                        for h in range(4):
                            last = nc.tensor.transpose(pb[0:QK, 4 + 2 * w + b, h * P:(h + 1) * P],
                                                       qkt[:, i % 2, w, (4 * b + h) * QK:(4 * b + h + 1) * QK], ident)
                        last.then_inc(S["qk_tr"], 1)
            pe.wait_ge(S["qk_ev_act"], 2 * NT)
            pe.wait_ge(S["qk_ev_dve"], 2 * NT)
            pe.wait_ge(S["cmp_ready"], 1)
            for i in range(NT):
                for h in range(HEADS):
                    r = slice((h // 4) * 64, (h // 4) * 64 + 64)
                    last = nc.tensor.matmul(pb[:, 4 * (h // 4) + i, (h % 4) * 32:(h % 4) * 32 + 31], qT[r, h % 4, i * P:(i + 1) * P], kcT[r, 0:31],
                                            start=True, stop=True)
                if i == 0:
                    last.then_inc(used, 3)
            last.then_inc(S["cs_mm"], 1)
            pe.wait_ge(S["cs_exp"], 1)
            for i in range(NT):
                for g in range(2):
                    last = nc.tensor.transpose(pb[:, 4 + i, g * P:(g + 1) * P],
                                               Pc[:, i, 4 * g:4 * g + 4, :].rearrange("p h j -> p (h j)"), ident)
            last.then_inc(S["cs_tr"], 1)
            pe.wait_ge(S["cs_tr_ev"], 1)
            for i in range(NT):
                for g in range(2):
                    last = nc.tensor.matmul(pb[:, i, g * 256:(g + 1) * 256], PcT[:, i, g * P:(g + 1) * P], Vbd[:, g, :],
                                            start=True, stop=True)
            last.then_inc(S["cs_pv"], 1)

            pe.wait_ge(S["cs_o"], 1)

            def scores(u):
                i, kind, pr = UNITS[u]
                nk = (i + 1) * P
                if u >= 2:
                    pe.wait_ge(S["at_exp"], 2 * (u - 1))
                for hh in range(2):
                    h = 2 * pr + hh
                    dst = pb[:, 2 * (u % 2) + hh, 0:nk]
                    if kind == 2:
                        last = nc.tensor.matmul(dst, qTm[0:QK, h, i * P:(i + 1) * P], kTm[0:QK, h, 0:nk], start=True, stop=True)
                    else:
                        r = slice((h // 4) * 64, (h // 4) * 64 + 64)
                        last = nc.tensor.matmul(dst, qT[r, h % 4, i * P:(i + 1) * P], kvT[r, 2 + kind, 0:nk], start=True, stop=True)
                last.then_inc(S["at_s"], 1)

            def turn_probs(u):
                i, kind, pr = UNITS[u]
                for hh in range(2):
                    pe.wait_ge(S["at_exp"], 2 * u + hh + 1)
                    if u:
                        pe.wait_ge(S["at_ev_dve"] if hh == 0 else S["at_ev_act"], u)
                    for kt in range(i + 1):
                        last = nc.tensor.transpose(pb[:, 4 + hh, kt * P:(kt + 1) * P], Pr[:, u % 2, hh, kt * P:(kt + 1) * P], ident)
                    last.then_inc(S["at_tr"], 1)

            def values(u):
                i, kind, pr = UNITS[u]
                w = u // 4
                if pr == 0 and w >= 2:
                    pe.wait_ge(S["at_o"], w - 1)
                for hh in range(2):
                    h = 2 * pr + hh
                    pe.wait_ge(S["at_ev_dve"] if hh == 0 else S["at_ev_act"], u + 1)
                    for kt in range(i + 1):
                        v = Vm[:, kt, h * DH:(h + 1) * DH] if kind == 2 else \
                            Vsw[:, kt, kind * P + (h // 4) * DH:kind * P + (h // 4) * DH + DH]
                        last = nc.tensor.matmul(pb[:, 6 + w % 2, h * DH:(h + 1) * DH], PTs[:, u % 2, hh, kt * P:(kt + 1) * P], v,
                                                start=(kt == 0), stop=(kt == i))
                    last.then_inc(S["at_pv"], 1)

            scores(0)
            for u in range(len(UNITS)):
                if u + 1 < len(UNITS):
                    scores(u + 1)
                turn_probs(u)
                if u:
                    values(u - 1)
            values(len(UNITS) - 1)
            if last_stage < 4:
                return
            pe.wait_ge(S["at_o"], 12)
            tr_pe(pe, "o_nsa", O_nsa, NT, 4)
            tr_pe(pe, "o_mla", O_mla, NT, 4, bank0=4)
            tr_wait(pe, "o_nsa")
            tr_wait(pe, "o_mla")
            for m in range(ND):
                n = W_MERGE + 3 * m
                b = 4 * (m % 2)
                if m >= 2:
                    pe.wait_ge(S["mg_ev"], m - 1)
                for w in range(2):
                    arrived(pe, n + w)
                    for k in range(ND):
                        last = nc.tensor.matmul(pb[:, b + w, :], tile(n + w)[:, k * P:(k + 1) * P], hT[:, k, :],
                                                start=(k == 0), stop=(k == ND - 1))
                    last.then_inc(used, 1)
                arrived(pe, n + 2)
                for w, src in ((0, oTn), (1, oTm)):
                    for k in range(4):
                        last = nc.tensor.matmul(pb[:, b + 2 + w, :], tile(n + 2)[:, (4 * w + k) * P:(4 * w + k + 1) * P],
                                                src[:, k, :], start=(k == 0), stop=(k == 3))
                last.then_inc(used, 1)
            pe.wait_ge(S["mg_ev"], ND)
            tokens_pe(pe, W_O, ND, mT, S["post_mm"])
            if last_stage < 5:
                return
            pe.wait_ge(S["norm_xn"], 2 * NT)
            tr_pe(pe, "n2", xn, NT, ND)
            tr_wait(pe, "n2")
            for j in range(NF):
                if j >= 4:
                    pe.wait_ge(S["up_dve"], 2 * (j - 3))
                for w in range(2):
                    n = W_UP + 2 * j + w
                    arrived(pe, n)
                    for k in range(ND):
                        last = nc.tensor.matmul(pb[:, 2 * (j % 4) + w, :], tile(n)[:, k * P:(k + 1) * P], hT[:, k, :],
                                                start=(k == 0), stop=(k == ND - 1))
                    last.then_inc(used, 1)
            pe.wait_ge(S["up_g"], NF)
            tokens_pe(pe, W_DOWN, NF, gT, S["post_mm"])
            if last_stage < 7:
                return
            pe.wait_ge(S["post_x"], 2 * NT)
            pe.wait_ge(S["p_in"], 16)
            tokens_pe(pe, W_PLE, 2, pTs, S["ple_mm"])
            pe.wait_ge(S["ple_ev"], NT)
            tr_pe(pe, "x2", X, NT, ND)
            tr_wait(pe, "x2")
            tokens_pe(pe, W_PGATE, ND, hT, S["pg_mm"])
            if last_stage >= 8:
                second_pe(pe)

        @block.scalar
        def _(act):
            for i in range(NT):
                act.dma_start(X[:, i, :], x[i * P:(i + 1) * P, :]).then_inc(S["x_in"], 16)
            norm_act(act, "n1", S["x_in"], 16 * NT)
            act.wait_ge(S["small_in"], 32)
            tr_act(act, "n1", hT, ND, "g_pre_mix")
            for m in range(8):
                act.wait_ge(S["w_used"], W_PROJ_FM + m + 1)
                dst = qT[:, m, :] if m < 4 else kvT[:, m - 4, :]
                nc.scalar.activation(dst, pb[:, m, :], ACT.Copy, scale=DH ** -0.5 if m < 4 else 1.0)\
                    .then_inc(S["proj_fm_ev"], 1)
            for i in range(NT):
                act.wait_ge(S["w_used"], W_PROJ_V)
                nc.scalar.activation(cqkv[:, i, :], pb[:, i, 0:416], ACT.Copy).then_inc(S["proj_mla_ev"], 1)
            act.wait_ge(S["w_used"], W_CMP)
            nc.scalar.activation(Vsw[:, :, :], pb[:, 4:8, 0:256], ACT.Copy).then_inc(S["proj_v_ev"], 1)
            nc.scalar.activation(gates[:, :, :], pb[:, 4:8, 256:280], ACT.Sigmoid).then_inc(S["proj_v_ev"], 1)
            act.wait_ge(S["ang_ready"], 1)
            nc.scalar.activation(ropet[:, 0:128], ropet[:, 128:256], ACT.Sin).then_inc(S["sin_ready"], 1)
            act.wait_ge(S["mla_ms"], 1)
            nc.scalar.activation(mrt, mss, ACT.Sqrt).then_inc(S["mla_rt"], 1)
            act.wait_ge(S["w_used"], W_CMP + 2)
            nc.scalar.activation(gk[:, 0:31], pb[:, 0, 0:31], ACT.Gelu_apprx_tanh, bias=col("b1k")).then_inc(S["cmp_gelu"], 1)
            act.wait_ge(S["w_used"], W_CMP + 4)
            act.wait_ge(S["cmp_blocks"], 5)
            for q in range(4):
                nc.scalar.activation(gv4[:, 32 * q:32 * q + 31], pb[:, 1, 0:31], ACT.Gelu_apprx_tanh, bias=col("b1v"))\
                    .then_inc(S["cmp_gelu"], 1)
            for b in range(3):
                act.wait_ge(S["mla_tr"], b + 1)
                nc.scalar.activation(cqT[:, b, :], pb[:, 4 + b, :], ACT.Copy,
                                     scale=col("g_q", b) if b < 2 else col("g_kv")).then_inc(S["mla_tr_ev"], 1)
            for i in range(NT):
                act.wait_ge(S["mla_up"], i + 1)
                if i >= 2:
                    act.wait_ge(S["qk_tr"], 4 * (i - 1))
                nc.scalar.activation(qkt[:, i % 2, 0, :].rearrange("p (b c) -> p b c", b=2), pb[:, 0:2, 0:384], ACT.Copy,
                                     scale=QK_SCALE).then_inc(S["q_raw"], 1)
                for w, dst in ((0, qTm), (1, kTm)):
                    act.wait_ge(S["qk_tr"], 4 * i + 2 * w + 2)
                    nc.scalar.activation(dst[0:QK, 4:8, i * P:(i + 1) * P],
                                         pb[0:QK, 5 + 2 * w, :].rearrange("p (h c) -> p h c", h=4), ACT.Copy)\
                        .then_inc(S["qk_ev_act"], 1)
            act.wait_ge(S["cs_max"], 1)
            nc.scalar.activation(Pc[:, :, :, 0:31], Pc[:, :, :, 0:31], ACT.Exp).then_inc(S["cs_exp"], 1)

            def exps(u):
                i, kind, pr = UNITS[u]
                nk = (i + 1) * P
                act.wait_ge(S["at_max"], u + 1)
                for hh in range(2):
                    if u >= 2:
                        act.wait_ge(S["at_tr"], 2 * (u - 2) + hh + 1)
                    nc.scalar.activation(Pr[:, u % 2, hh, 0:nk], pb[:, 2 * (u % 2) + hh, 0:nk], ACT.Exp,
                                         bias=nm[:, u % 2, hh:hh + 1],
                                         accum_out=sums[:, u // 4, 2 * pr + hh:2 * pr + hh + 1]).then_inc(S["at_exp"], 1)

            def copy_turned(u):
                nk = (UNITS[u][0] + 1) * P
                act.wait_ge(S["at_tr"], 2 * u + 2)
                if u >= 2:
                    act.wait_ge(S["at_pv"], 2 * (u - 2) + 2)
                nc.scalar.activation(PTs[:, u % 2, 1, 0:nk], pb[:, 5, 0:nk], ACT.Copy).then_inc(S["at_ev_act"], 1)

            for u in range(len(UNITS)):
                exps(u)
                if u:
                    copy_turned(u - 1)
            copy_turned(len(UNITS) - 1)
            if last_stage < 4:
                return
            tr_act(act, "o_nsa", oTn, 4)
            tr_act(act, "o_mla", oTm, 4, bank0=4)
            for m in range(ND):
                b = 4 * (m % 2)
                for w in range(2):
                    act.wait_ge(S["w_used"], W_MERGE + 3 * m + w + 1)
                    if m >= 2:
                        act.wait_ge(S["mg_ev"], m - 1)
                    nc.scalar.activation(mgt[:, m % 2, w, :], pb[:, b + w, :], ACT.Sigmoid).then_inc(S["mg_sig"], 1)
            post_act(act, "p1", pair, W_UP - 1)
            if last_stage < 5:
                return
            norm_act(act, "n2", S["post_x"], 1 * NT)
            tr_act(act, "n2", hT, ND, "g_pre_ffn")

            def conv_last(j, w):
                m = w * NF + j
                act.wait_ge(S["w_used"], W_UP + 2 * j + w + 1)
                if j >= 2:
                    act.wait_ge(S["up_g"], j - 1)
                nc.scalar.activation(cva[:, j % 2, w, :], pb[:, 2 * (j % 4) + w, :], ACT.Identity,
                                     scale=col("w_conv", 2 * 2 * NF + m), bias=col("b_conv", m)).then_inc(S["up_conv"], 1)

            for j in range(NF):
                for w in range(2):
                    conv_last(j, w)
                act.wait_ge(S["up_dve"], 2 * j + 1)
                nc.scalar.activation(ga[:, j % 2, :], cva[:, j % 2, 0, :], ACT.Gelu_apprx_tanh).then_inc(S["up_gelu"], 1)
            post_act(act, "p2", pair, W_PLE - 1)
            if last_stage < 7:
                return
            for i in range(NT):
                product(act, S["ple_mm"], 0, i, W_PGATE - 1)
                nc.scalar.activation(E[:, i, :], pair(i), ACT.Copy).then_inc(S["ple_ev"], 1)
            tr_act(act, "x2", hT, ND)
            for i in range(NT):
                product(act, S["pg_mm"], 0, i, W_IN2 - 1)
                nc.scalar.activation(Gs[:, i, :], pair(i), ACT.Sigmoid).then_inc(S["pg_sig"], 1)
            post_act(act, "p3", lambda i: E[:, i, :])
            if last_stage >= 8:
                second_act(act)
            else:
                act.wait_ge(S["post_x"], 3 * NT)

        @block.vector
        def _(dve):
            chain = [0]

            def L(ins):
                link(dve, chain, ins)

            norm_dve(dve, chain, "n1")
            dve.wait_ge(S["small_in"], 32)
            tr_dve(dve, "n1", hT, ND, "g_pre_mix")
            dve.wait_ge(S["pos_in"], 16)
            posf = ropet[:, 256:260]
            ang = ropet[:, 264:328]
            turns = ropet[:, 328:392]
            red = ropet[:, 128:192]
            redc = ropet[:, 192:256]
            L(nc.vector.tensor_copy(posf, posi[:, :]))
            L(nc.vector.tensor_tensor(ang.rearrange("p (i f) -> p i f", i=NT), posf.unsqueeze(2).broadcast_to([P, NT, 16]),
                                      cs("inv_freq").unsqueeze(1).broadcast_to([P, NT, 16]), ALU.mult))
            reduce_angle(L, nc, ang, turns, red)
            L(nc.vector.tensor_scalar(red, red, PI_LOW, -PI_LOW, ALU.min, ALU.max))
            L(nc.vector.scalar_tensor_tensor(out=redc, in0=red, scalar=-1.0, in1=red, op0=ALU.mult, op1=ALU.max))
            nc.vector.tensor_scalar(redc, redc, -1.0, PI_HALF, ALU.mult, ALU.add).then_inc(S["ang_ready"], 1)
            dve.wait_ge(S["proj_fm_ev"], 6)
            for w in range(2):
                src = kvT[:, w, :].rearrange("p (b l) -> p l b", l=16)
                for half in range(2):
                    nc.vector.tensor_tensor(
                        kb[:, w, 16 * half:16 * half + 16, :], src[:, :, half:half + 31],
                        col("pos_k" if w == 0 else "pos_v", 16 * half, 16).unsqueeze(2).broadcast_to([P, 16, 31]), ALU.add)\
                        .then_inc(S["cmp_blocks"], 1)
            nc.vector.memset(gv4, 0.0).then_inc(S["cmp_blocks"], 1)
            nc.vector.memset(ar(26304, 512), 0.0)
            dve.wait_ge(S["proj_mla_ev"], NT)
            L(nc.vector.tensor_tensor(chat[:, :, :], cqkv[:, :, 0:384], cqkv[:, :, 0:384], ALU.mult))
            L(nc.vector.tensor_reduce(mrs[:, 0:4], chat[:, :, 0:256], AX.X, ALU.add))
            L(nc.vector.tensor_reduce(mrs[:, 4:8], chat[:, :, 256:384], AX.X, ALU.add))
            nc.vector.tensor_scalar(mss[:, 0:4], mrs[:, 0:4], 1.0 / 256, EPS, ALU.mult, ALU.add)
            nc.vector.tensor_scalar(mss[:, 4:8], mrs[:, 4:8], 1.0 / 128, EPS, ALU.mult, ALU.add).then_inc(S["mla_ms"], 1)
            dve.wait_ge(S["mla_rt"], 1)
            L(nc.vector.reciprocal(mrs, mrt))
            nc.vector.tensor_tensor(chat[:, :, 0:256], cqkv[:, :, 0:256], mrs[:, 0:4].unsqueeze(2).broadcast_to([P, NT, 256]), ALU.mult)
            nc.vector.tensor_tensor(chat[:, :, 256:384], cqkv[:, :, 256:384], mrs[:, 4:8].unsqueeze(2).broadcast_to([P, NT, 128]), ALU.mult)\
                .then_inc(S["mla_norm"], 1)
            dve.wait_ge(S["sin_ready"], 1)
            sin, cos = ropet[:, 0:64], ropet[:, 64:128]

            def by_tile(t):
                return t.rearrange("p (i f) -> p i f", i=NT)

            krr = ropet[:, 520:648].rearrange("p (i c) -> p i c", i=NT)
            r1, r2 = ropet[:, 648:712], ropet[:, 712:776]
            x1, x2 = cqkv[:, :, 384:400], cqkv[:, :, 400:416]
            L(nc.vector.tensor_tensor(by_tile(r1), x1, by_tile(cos), ALU.mult))
            L(nc.vector.tensor_tensor(by_tile(r2), x2, by_tile(sin), ALU.mult))
            L(nc.vector.tensor_tensor(krr[:, :, 0:16], by_tile(r1), by_tile(r2), ALU.subtract))
            L(nc.vector.tensor_tensor(by_tile(r1), x2, by_tile(cos), ALU.mult))
            L(nc.vector.tensor_tensor(by_tile(r2), x1, by_tile(sin), ALU.mult))
            L(nc.vector.tensor_tensor(krr[:, :, 16:32], by_tile(r1), by_tile(r2), ALU.add))
            dve.wait_ge(S["cmp_kv"], 1)
            nc.vector.tensor_copy(kcT[:, 0:31], pb[:, 2, 0:31])
            for g in range(2):
                for q in range(4):
                    last = nc.vector.tensor_copy(Vbd[32 * q:32 * q + 32, g, q * DH:(q + 1) * DH],
                                                 pb[32 * q:32 * q + 32, 3 * (1 - g), 0:64])
            last.then_inc(S["cmp_ready"], 1)
            q1, q2, q3, q4 = [t.rearrange("p (h c) -> p h c", h=HEADS)
                              for t in (ropet[:, 776:904], ropet[:, 264:392], ropet[:, 392:520], ropet[:, 128:256])]
            for i in range(NT):
                dve.wait_ge(S["mla_up"], i + 1)
                if i >= 2:
                    dve.wait_ge(S["qk_tr"], 4 * (i - 1))
                kvv = pb[:, 2:4, :].rearrange("p b (h c) -> p (b h) c", c=P)
                qd = qkt[:, i % 2, 0, :].rearrange("p (h c) -> p h c", c=QK)
                kd = qkt[:, i % 2, 1, :].rearrange("p (h c) -> p h c", c=QK)
                nc.vector.tensor_copy(kd[:, :, 64:96], krr[:, i, :].unsqueeze(1).broadcast_to([P, HEADS, 32]))
                nc.vector.tensor_copy(Vm[:, i, :].rearrange("p (h c) -> p h c", c=DH), kvv[:, :, 64:128])
                nc.vector.tensor_copy(kd[:, :, 0:64], kvv[:, :, 0:64]).then_inc(S["kv_ev"], 1)
                dve.wait_ge(S["q_raw"], i + 1)
                y1, y2 = qd[:, :, 64:80], qd[:, :, 80:96]
                ci = cos[:, 16 * i:16 * i + 16].unsqueeze(1).broadcast_to([P, HEADS, 16])
                si = sin[:, 16 * i:16 * i + 16].unsqueeze(1).broadcast_to([P, HEADS, 16])
                if i:
                    dve.wait_ge(S["q_ev"], i)
                nc.vector.tensor_tensor(q1, y1, ci, ALU.mult)
                nc.vector.tensor_tensor(q2, y2, si, ALU.mult)
                nc.vector.tensor_tensor(q3, y2, ci, ALU.mult)
                L(nc.vector.tensor_tensor(q4, y1, si, ALU.mult))
                nc.vector.tensor_tensor(y1, q1, q2, ALU.subtract)
                nc.vector.tensor_tensor(y2, q3, q4, ALU.add).then_inc(S["q_ev"], 1)
                for w, dst in ((0, qTm), (1, kTm)):
                    dve.wait_ge(S["qk_tr"], 4 * i + 2 * w + 1)
                    nc.vector.tensor_copy(dst[0:QK, 0:4, i * P:(i + 1) * P],
                                          pb[0:QK, 4 + 2 * w, :].rearrange("p (h c) -> p h c", h=4))\
                        .then_inc(S["qk_ev_dve"], 1)
            dve.wait_ge(S["tab_in"], 16)
            dve.wait_ge(S["cs_mm"], 1)
            L(nc.vector.memset(ar(21216, 1024), 0.0))
            for g in range(2):
                sc = pb[:, 4 * g:4 * g + 4, 0:128].rearrange("p i (h j) -> p i h j", j=32)
                ins = nc.vector.tensor_tensor(Pc[:, :, 4 * g:4 * g + 4, 0:31], sc[:, :, :, 0:31],
                                              cmpt.rearrange("p (i h j) -> p i h j", i=NT, j=31)[:, :, 4 * g:4 * g + 4, :],
                                              ALU.add)
            L(ins)
            L(nc.vector.tensor_reduce(cmaxn.rearrange("p (i h) -> p i h", i=NT), Pc[:, :, :, 0:31], AX.X, ALU.max))
            nc.vector.tensor_tensor(Pc[:, :, :, 0:31], Pc[:, :, :, 0:31],
                                    cmaxn.rearrange("p (i h) -> p i h", i=NT).unsqueeze(3).broadcast_to([P, NT, HEADS, 31]),
                                    ALU.subtract).then_inc(S["cs_max"], 1)
            dve.wait_ge(S["cs_exp"], 1)
            L(nc.vector.tensor_reduce(csum.rearrange("p (i h) -> p i h", i=NT), Pc[:, :, :, 0:31], AX.X, ALU.add))
            L(nc.vector.reciprocal(csum, csum))
            f3 = fac.rearrange("p (i h) -> p i h", i=NT)
            dve.wait_ge(S["proj_v_ev"], 2)
            L(nc.vector.tensor_tensor(f3, csum.rearrange("p (i h) -> p i h", i=NT), gates[:, :, 0:8], ALU.mult))
            L(nc.vector.tensor_scalar(fac[:, 0:8], fac[:, 0:8], cs("row_ok"), None, ALU.mult))
            dve.wait_ge(S["cs_tr"], 1)
            nc.vector.tensor_copy(PcT[:, :, :], pb[:, 4:8, 0:256]).then_inc(S["cs_tr_ev"], 1)
            dve.wait_ge(S["cs_pv"], 1)
            nc.vector.tensor_tensor(ar(17120, 2048).rearrange("p (a c) -> p a c", c=DH),
                                    pb[:, 0:4, :].rearrange("p i (h c) -> p (i h) c", c=DH),
                                    fac.unsqueeze(2).broadcast_to([P, 32, DH]), ALU.mult).then_inc(S["cs_o"], 1)
            dve.wait_ge(S["cs_o"], 1)

            alibi = cs("alibi")
            rinv = st[:, 428:436]
            otmp = junk[:, 0:512]

            def mask_max(u):
                i, kind, pr = UNITS[u]
                nk = (i + 1) * P
                b = 2 * (u % 2)
                dve.wait_ge(S["at_s"], u + 1)
                if kind == 2:
                    L(nc.vector.tensor_tensor(pb[:, b:b + 2, nk - P:nk], pb[:, b:b + 2, nk - P:nk],
                                              cs("diag").unsqueeze(1).broadcast_to([P, 2, P]), ALU.add))
                else:
                    for hh in range(2):
                        ins = nc.vector.scalar_tensor_tensor(out=pb[:, b + hh, 0:nk], in0=alibi[:, 512 - nk:512],
                                                             scalar=SLOPES[2 * pr + hh], in1=pb[:, b + hh, 0:nk],
                                                             op0=ALU.mult, op1=ALU.add)
                    L(ins)
                nc.vector.tensor_reduce(nm[:, u % 2, :], pb[:, b:b + 2, 0:nk], AX.X, ALU.max, negate=True)\
                    .then_inc(S["at_max"], 1)

            def copy_turned(u):
                nk = (UNITS[u][0] + 1) * P
                dve.wait_ge(S["at_tr"], 2 * u + 1)
                if u >= 2:
                    dve.wait_ge(S["at_pv"], 2 * (u - 2) + 1)
                nc.vector.tensor_copy(PTs[:, u % 2, 0, 0:nk], pb[:, 4, 0:nk]).then_inc(S["at_ev_dve"], 1)

            def combine(w):
                i, kind = w // 3, w % 3
                dve.wait_ge(S["at_pv"], 8 * (w + 1))
                L(nc.vector.reciprocal(rinv, sums[:, w, :]))
                if kind < 2:
                    L(nc.vector.tensor_tensor(rinv, rinv, gates[:, i, 8 * (kind + 1):8 * (kind + 2)], ALU.mult))
                dst = O_mla[:, i, :] if kind == 2 else otmp
                ins = nc.vector.tensor_tensor(dst.rearrange("p (h c) -> p h c", c=DH),
                                              pb[:, 6 + w % 2, :].rearrange("p (h c) -> p h c", c=DH),
                                              rinv.unsqueeze(2).broadcast_to([P, HEADS, DH]), ALU.mult)
                if kind < 2:
                    L(ins)
                    ins = nc.vector.tensor_tensor(O_nsa[:, i, :], O_nsa[:, i, :], otmp, ALU.add)
                ins.then_inc(S["at_o"], 1)
                dve.wait_ge(S["at_o"], w + 1)

            for u in range(len(UNITS)):
                mask_max(u)
                if u:
                    copy_turned(u - 1)
                if u % 4 == 1 and u >= 5:
                    combine((u - 5) // 4)
            copy_turned(len(UNITS) - 1)
            combine(11)
            if last_stage < 4:
                return
            tr_dve(dve, "o_nsa", oTn, 4)
            tr_dve(dve, "o_mla", oTm, 4, bank0=4)
            for m in range(ND):
                b = 4 * (m % 2)
                dve.wait_ge(S["mg_sig"], 2 * m + 2)
                dve.wait_ge(S["w_used"], W_MERGE + 3 * m + 3)
                for w in range(2):
                    ins = nc.vector.tensor_tensor(mgt[:, m % 2, 2 + w, :], mgt[:, m % 2, w, :], pb[:, b + 2 + w, :], ALU.mult)
                L(ins)
                nc.vector.tensor_tensor(mT[:, m, :], mgt[:, m % 2, 2, :], mgt[:, m % 2, 3, :], ALU.add).then_inc(S["mg_ev"], 1)
            post_dve(dve, chain, "p1", pair, 1)
            if last_stage < 5:
                return
            dve.wait_ge(S["post_x"], 1 * NT)
            norm_dve(dve, chain, "n2")
            tr_dve(dve, "n2", hT, ND, "g_pre_ffn")
            for j in range(NF):
                for w in range(2):
                    m = w * NF + j
                    dve.wait_ge(S["up_conv"], 2 * j + w + 1)
                    c = cva[:, j % 2, w, :]
                    u = pb[:, 2 * (j % 4) + w, :]
                    L(nc.vector.scalar_tensor_tensor(out=c[:, 1:T], in0=u[:, 0:T - 1], scalar=col("w_conv", 2 * NF + m),
                                                     in1=c[:, 1:T], op0=ALU.mult, op1=ALU.add))
                    nc.vector.scalar_tensor_tensor(out=c[:, 2:T], in0=u[:, 0:T - 2], scalar=col("w_conv", m),
                                                   in1=c[:, 2:T], op0=ALU.mult, op1=ALU.add).then_inc(S["up_dve"], 1)
                dve.wait_ge(S["up_dve"], 2 * j + 2)
                dve.wait_ge(S["up_gelu"], j + 1)
                nc.vector.tensor_tensor(gT[:, j, :], ga[:, j % 2, :], cva[:, j % 2, 1, :], ALU.mult).then_inc(S["up_g"], 1)
            post_dve(dve, chain, "p2", pair, 2)
            if last_stage < 7:
                return
            dve.wait_ge(S["post_x"], 2 * NT)
            tr_dve(dve, "x2", hT, ND)
            for i in range(NT):
                dve.wait_ge(S["pg_sig"], i + 1)
                nc.vector.tensor_tensor(E[:, i, :], E[:, i, :], Gs[:, i, :], ALU.mult).then_inc(S["p3_prod"], 1)
            dve.wait_ge(S["p3_prod"], NT)
            post_dve(dve, chain, "p3", lambda i: E[:, i, :], 3)
            if last_stage >= 8:
                dve.wait_ge(S["post_x"], 3 * NT)
                second_dve(dve, chain)



TWO_PI = 6.283185307179586
PI_HALF = 1.5707963267948966
TWO_PI_A = 6.28125
TWO_PI_B = float(np.float32(np.round((TWO_PI - 6.28125) * 2.0 ** 21) / 2.0 ** 21))
TWO_PI_C = TWO_PI - TWO_PI_A - TWO_PI_B
ROUND = 12582912.0


def reduce_angle(L, nc, ang, turns, red):
    L(nc.vector.tensor_scalar(turns, ang, 1.0 / TWO_PI, ROUND, ALU.mult, ALU.add))
    L(nc.vector.tensor_scalar(turns, turns, ROUND, None, ALU.subtract))
    L(nc.vector.scalar_tensor_tensor(out=red, in0=turns, scalar=-TWO_PI_A, in1=ang, op0=ALU.mult, op1=ALU.add))
    L(nc.vector.scalar_tensor_tensor(out=red, in0=turns, scalar=-TWO_PI_B, in1=red, op0=ALU.mult, op1=ALU.add))
    L(nc.vector.scalar_tensor_tensor(out=red, in0=turns, scalar=-TWO_PI_C, in1=red, op0=ALU.mult, op1=ALU.add))


PI_LOW = 3.1415925025939941


def constants():
    f32 = np.float32
    p = np.arange(P)
    c = {"ident": np.eye(P), "ones": np.ones((P, P)), "diag": np.where(p[None, :] <= p[:, None], 0.0, NEG)}
    dist = p[:, None] - (np.arange(512)[None, :] - 384)
    c["alibi"] = np.where(dist >= 0, -dist, NEG)
    inv = (np.float32(10000.0) ** (-np.arange(0, 32, 2, dtype=f32) / f32(32))).astype(f32)
    c["inv_freq"] = np.broadcast_to(inv, (P, 16))
    c["row_ok"] = (p >= 31)[:, None]
    a = 2 * np.pi * np.outer(np.arange(64), np.arange(64)) / 64
    z = np.zeros((64, 64))
    c["dft64"] = np.block([[np.cos(a), z, -np.sin(a), z], [z, np.cos(a), z, -np.sin(a)]])
    c["giota"] = np.broadcast_to(np.arange(4), (P, 4))
    c["eiota"] = np.broadcast_to(np.arange(32), (P, 32))
    csts = np.concatenate([c[n].astype(f32) for n, _ in CSTS], axis=1)
    t = np.arange(T).reshape(NT, P).T
    dist = t[:, :, None] - (np.arange(N_CMP) * 16 + 31)[None, None, :]
    slopes = np.array(SLOPES)
    tab = np.where(dist[:, :, None, :] >= 0, -slopes[None, None, :, None] * dist[:, :, None, :], NEG)
    return csts, tab.astype(f32).reshape(P, -1)


def transforms():
    n = np.arange(T)
    a = 2 * np.pi * (np.outer(n, n) % (2 * T)) / (2 * T)
    C, Sn, alt = np.cos(a), np.sin(a), (-1.0) ** n

    def blocks(c, s, m):
        cols = slice(m * P, (m + 1) * P)
        return np.concatenate([by_rows(c[:, cols]), by_rows(s[:, cols])], axis=1).astype(np.float32)

    Cn, Sa = C.copy(), Sn.copy()
    Cn[:, 0] = alt
    Sa[:, 0] = alt
    forward = [blocks(Cn, Sa, 0)] + [blocks(C, Sn, m) for m in range(4)]
    Ci, Si = C.copy(), Sn.copy()
    Ci[0, :] = 0.5
    Si[0, :] = 0.5 * alt
    inverse = [blocks(Ci, Si, i) for i in range(NT)]
    b = 2 * np.pi * (np.outer(n, n) % T) / T
    scale = 1.0 / np.sqrt(64.0 * T)
    time = [blocks(np.cos(b) * scale, np.sin(b) * scale, i) for i in range(NT)]
    return (W_DFT, forward), (W_IDFT, inverse), (W_FFT, time)


def filter_tables():
    f32 = np.float32
    t = np.linspace(0.0, 1.0, T, dtype=f32)[:, None]
    w = (f32(2.0 * np.pi / T) * np.arange(T, dtype=f32))[:, None]
    f = np.linspace(1e-4, 15, 16, dtype=f32)[None, :]
    z = np.concatenate([t, np.cos(f * w), -np.sin(f * w)], axis=-1)
    deltas = np.abs(np.linspace(np.log(1e-2) / 1.5, np.log(1e-2) / 0.3, CH, dtype=f32))
    zp = np.zeros((P, T), f32)
    zp[:33] = z.T
    return zp, by_rows(np.exp(-t * deltas).astype(f32)).reshape(P, -1)


def by_rows(w):
    return w.reshape(-1, P, w.shape[-1]).transpose(1, 0, 2)


def pack(tiles, dest, at, m):
    flat = tiles.reshape(P, -1)
    dest[at + m, :, :flat.shape[1]] = flat


def kernel(**a):
    import concourse.bacc as bacc
    from concourse.bass_utils import run_bass_kernel_spmd

    last_stage = LAST
    a = {k: np.asarray(v) for k, v in a.items()}
    f32 = np.float32
    n_used = {3: W_MERGE, 4: W_UP, 5: W_PLE, 7: W_IN2}.get(last_stage, N_TILES)
    n_stream = -(-n_used // RING) * RING
    W = np.zeros((n_stream, P, 1024), f32)
    w_in = a["w_in"][0]
    put = lambda tiles, at, m: pack(tiles, W, at, m) if at + m < n_stream else None
    for m in range(4):
        cols = [*range(m * 64, m * 64 + 64), *range((m + 4) * 64, (m + 4) * 64 + 64)]
        put(by_rows(w_in[:, cols]), W_PROJ_FM, m)
    for m, part in enumerate((0, 1, 2, 4)):
        put(by_rows(w_in[:, 512 + part * 128:512 + part * 128 + 128]), W_PROJ_FM, 4 + m)
    mla = by_rows(w_in[:, 1304:1720])
    for m in range(4):
        put(mla[:, 2 * m:2 * m + 2], W_PROJ_MLA, m)
    vv = by_rows(np.concatenate([w_in[:, 896:1024], w_in[:, 1152:1304]], axis=1))
    for m in range(3):
        put(vv[:, 3 * m:3 * m + 3], W_PROJ_V, m)
    for w, name in enumerate(("nsa_ck_w1", "nsa_cv_w1")):
        w1 = a[name][0].reshape(32, 64, 64).transpose(1, 0, 2)
        w1 = np.concatenate([w1, w1], axis=0)
        for half in range(2):
            put(w1[:, 16 * half:16 * half + 16], W_CMP, 2 * w + half)
    uq = by_rows(a["mla_w_uq"][0])
    put(uq[:, 0], W_UQ, 0)
    put(uq[:, 1], W_UQ, 1)
    put(a["mla_w_ukv"][0], W_UKV, 0)
    for m in range(ND):
        s = slice(m * P, m * P + P)
        put(by_rows(w_in[:, 1720:2744][:, s]), W_MERGE, 3 * m)
        put(by_rows(w_in[:, 2744:3768][:, s]), W_MERGE, 3 * m + 1)
        put(np.concatenate([by_rows(a["w_br_nsa"][0][:, s]), by_rows(a["w_br_mla"][0][:, s])], axis=1), W_MERGE, 3 * m + 2)
    for name, at in (("w_o", W_O), ("w_down", W_DOWN), ("w_ple", W_PLE), ("w_ple_gate", W_PGATE), ("w_out_2", W_OUT2)):
        w = by_rows(a[name][0])
        for k in range(w.shape[1]):
            put(w[:, k], at, k)
    w_up = a["w_up"][0]
    for j in range(NF):
        for w in range(2):
            o = w * D_FF + j * P
            put(by_rows(w_up[:, o:o + P]), W_UP, 2 * j + w)
    w_in2 = a["w_in_2"][0]
    for m in range(16):
        put(by_rows(w_in2[:, m * P:(m + 1) * P]), W_IN2, m)
    if last_stage >= 8:
        for at, tiles in transforms():
            for m, t in enumerate(tiles):
                put(t, at, m)
        put(by_rows(np.concatenate([a["w_group_2"][0], a["w_router_2"][0].transpose(1, 0, 2).reshape(D, 32)], axis=1)), W_ROUTE, 0)
        for w, name in enumerate(("w_gate_2", "w_up_2")):
            v = a[name][0].reshape(N_EXP, ND, P, 4, P).transpose(0, 3, 2, 1, 4)
            W[W_EXP:].reshape(N_EXP, 12, P, 1024)[:, w:8:2] = v.reshape(N_EXP, 4, P, 1024)
        W[W_EXP:].reshape(N_EXP, 12, P, 1024)[:, 8:12] = a["w_down_2"][0].reshape(N_EXP, 4, P, 1024)
    vec = lambda v: v.reshape(-1, P).T
    twice = lambda v: np.concatenate([v, v], axis=0)
    low = lambda v: np.concatenate([v, np.zeros((P - v.shape[0], v.shape[1]), f32)], axis=0)
    c = {"g_pre_mix": vec(a["g_pre_mix"][0]), "g_pre_ffn": vec(a["g_pre_ffn"][0]), "norm1": vec(a["norm1_g_2"][0]),
         "norm2": vec(a["norm2_g_2"][0]), "mix_g": vec(a["mix_g_2"][0]), "g_q": vec(a["mla_g_q"][0]),
         "g_kv": vec(a["mla_g_kv"][0]), "w_conv": vec(a["w_conv"][0].reshape(-1)), "b_conv": vec(a["b_conv"][0]),
         "conv_w": vec(a["conv_w_2"][0].reshape(-1)), "conv_b": vec(a["conv_b_2"][0]),
         "b1k": twice(a["nsa_ck_b1"][0][:, None]), "b1v": twice(a["nsa_cv_b1"][0][:, None]),
         "w2k": twice(a["nsa_ck_w2"][0]), "w2v": twice(a["nsa_cv_w2"][0]),
         "pos_k": twice(a["nsa_pos_k"][0].T), "pos_v": twice(a["nsa_pos_v"][0].T),
         "f_b_in": low(a["f_b_in_2"][0][:, None]), "f_freq": low(a["f_freq_2"][0].T), "f_b_mid": low(a["f_b_mid_2"][0].T),
         "f_w_in": low(a["f_w_in_2"][0]), "r_bias": np.broadcast_to(np.concatenate([a["b_group_2"][0], a["b_router_2"][0].reshape(-1)]), (P, 36)),
         "f_w_mid": low(a["f_w_mid_2"][0].transpose(1, 0, 2).reshape(64, 128))}
    cols = np.concatenate([c[n] for n, _ in COLS], axis=1)
    csts, cmp_tab = constants()
    ins = {"stream": W, "x": a["x"][0], "cols": cols, "csts": csts, "cmp_tab": cmp_tab,
           "pos": np.ascontiguousarray(a["positions"][0].reshape(NT, P).T),
           "grows": np.stack([np.broadcast_to(v, (P, D)) for v in (a["g_post_mix"][0], a["g_post_ffn"][0], a["g_ple"][0], a["final_g_2"])]),
           "pT": np.ascontiguousarray(by_rows(np.ascontiguousarray(a["p"][0, 0].T))).reshape(P, -1)}
    ins["fconst"], ins["decay"] = filter_tables()
    ins["fwout"] = a["f_w_out_2"][0]
    ins["frow"] = np.broadcast_to(a["f_bias_2"][0], (P, CH))
    nc = bacc.Bacc("TRN2", target_bir_lowering=False, num_devices=1)
    ap = {}
    for n, v in ins.items():
        v = ins[n] = np.ascontiguousarray(v)
        ap[n] = nc.dram_tensor(n, v.shape, mybir.dt.from_np(v.dtype), kind="ExternalInput").ap()
    out = nc.dram_tensor("out", (T, D), F32, kind="ExternalOutput").ap()
    build(nc, last_stage, n_stream, ap["stream"], ap["x"], ap["cols"], ap["csts"], ap["cmp_tab"], ap["pos"], ap["grows"],
          ap["pT"], ap["fconst"], ap["fwout"], ap["decay"], ap["frow"], out)
    r = run_bass_kernel_spmd(nc, [ins], core_ids=[0])
    return r.results[0]["out"].reshape(1, T, D)


LAST = 8
```

```python
from contextlib import ExitStack

import numpy as np
import concourse.bass as bass
from concourse import mybir

F32 = mybir.dt.float32
I32 = mybir.dt.int32
ALU = mybir.AluOpType
ACT = mybir.ActivationFunctionType
AX = mybir.AxisListType

P = 128
T = 512
NT = T // P
D = 1024
ND = D // P
EPS = 1e-6
NEG = -1e30
HEADS = 8
DH = 64
N_CMP = (T - 32) // 16 + 1
QK = 96
QK_SCALE = float(QK) ** -0.5
D_FF = 2816
NF = D_FF // P
N_EXP = 32
CH = 512
RING = 12
N_SLOTS = N_EXP * T
EXTRA = 2 * T // P - 1
N_OVER = EXTRA + 1

W_PROJ_FM = 0
W_PROJ_MLA = W_PROJ_FM + 8
W_PROJ_V = W_PROJ_MLA + 4
W_CMP = W_PROJ_V + 3
W_UQ = W_CMP + 4
W_UKV = W_UQ + 2
W_MERGE = W_UKV + 1
W_O = W_MERGE + 24
W_UP = W_O + 8
W_DOWN = W_UP + 2 * NF
W_PLE = W_DOWN + NF
W_PGATE = W_PLE + 2
W_IN2 = W_PGATE + 8
W_DFT = W_IN2 + 16
W_IDFT = W_DFT + 5
W_FFT = W_IDFT + 4
W_OUT2 = W_FFT + 4
W_ROUTE = W_OUT2 + 8
W_EXP = W_ROUTE + 1
N_TILES = W_EXP + 12 * N_EXP
assert W_EXP % RING == 0 and N_TILES % RING == 0

COLS = [("g_pre_mix", 8), ("g_pre_ffn", 8), ("norm1", 8), ("norm2", 8), ("mix_g", 8), ("g_q", 2), ("g_kv", 1),
        ("w_conv", 3 * 2 * NF), ("b_conv", 2 * NF), ("conv_w", 3 * 12), ("conv_b", 12), ("b1k", 1), ("b1v", 1),
        ("w2k", 64), ("w2v", 64), ("pos_k", 32), ("pos_v", 32), ("f_b_in", 1), ("f_freq", 3), ("f_b_mid", 2),
        ("f_w_in", 64), ("f_w_mid", 128), ("r_bias", 36)]
COL = {}
_at = 0
for _n, _w in COLS:
    COL[_n] = (_at, _at + _w)
    _at += _w
N_COLS = _at

CSTS = [("ident", 128), ("ones", 128), ("diag", 128), ("alibi", 512), ("inv_freq", 16), ("row_ok", 1),
        ("dft64", 256), ("giota", 4), ("eiota", 32), ("tri", 128), ("choice", 8)]
CST = {}
_at = 0
for _n, _w in CSTS:
    CST[_n] = (_at, _at + _w)
    _at += _w
N_CST = _at

SLOPES = [2.0 ** (-(h + 1)) for h in range(HEADS)]

SEMS = """p3_prod norm_ss norm_ms norm_rt norm_xn post_mm post_ss post_ms post_rt post_x turned copied_dve copied_act w_used small_in x_in tab_in pos_in g_in p_in decay_in out_st dve_chain
proj_fm_ev proj_mla_ev proj_v_ev
cmp_blocks cmp_gelu cmp_kv cmp_ready
ang_ready sin_ready mla_ms mla_rt mla_norm mla_tr mla_tr_ev mla_up q_ev kv_ev q_raw qk_tr qk_ev_act qk_ev_dve
cs_mm cs_max cs_exp cs_tr cs_tr_ev cs_pv cs_o
at_s at_max at_exp at_tr at_ev_dve at_ev_act at_pv at_o
mg_sig mg_ev
up_conv up_dve up_gelu up_g
ple_mm ple_ev pg_mm pg_sig
in2_lin in2_conv in2_f z_ready f_in fb_in
fm_mm fm_arg fm_sin fo_mm fo_ev habs hs_mm hs_ready pm_ready
kf_mm kf_ev y_ready yo_ev fd_mm fd_ev fo2_ev hn_sq hn_ms hn_rt hn_y wo2_mm wo2_x
rt_lg rt_g rt_d rt_exp past_set slots_set rows_st xg_zero dest_ready slots_st sel_ready rank_mm over_ready x_tr x_ev_dve x_ev_act
ex_sig ex_hid ex_mul h_tr h_ev y_ev_dve y_ev_act xg_in0 xg_in1 idx_in at_in at_out gathers scatters y_st0 y_st1
back0 back1 back2 back3 moe_x fin_y""".split()
NORMS = ["n1", "n2", "n3", "n4", "n5"]
POSTS = ["p1", "p2", "p3"]
TURNS = {}
_at = 0
for _n, _w in (("n1", 8), ("o_nsa", 4), ("o_mla", 4), ("n2", 8), ("x2", 8), ("n3", 8), ("z", 4), ("x0", 4), ("y2", 8), ("n4", 8)):
    TURNS[_n] = (_at, _w)
    _at += _w


def build(nc, W, x, cols, csts, cmp_tab, pos, grows, pT, fconst, fwout, decay, frow, free, out):
    ctx = ExitStack()
    with ctx:
        def sem(name):
            return ctx.enter_context(nc.semaphore(name))

        def sb(name, shape, dt=F32):
            return ctx.enter_context(nc.sbuf_tensor(name, shape, dt))

        S = {n: sem(n) for n in SEMS}
        landed = [sem(f"w_landed{s}") for s in range(RING)]

        pb = ctx.enter_context(nc.psum_tensor("banks", [P, 8, 512], F32))
        ring = sb("ring", [P, RING, 1024])
        X = sb("resid", [P, NT, D])
        hT = sb("hT", [P, ND, T])
        colt = sb("colt", [P, N_COLS])
        cst = sb("cst", [P, N_CST])
        grow = sb("grow", [P, D])
        junk = sb("junk", [P, 1024])
        st = sb("st", [P, 640])
        posi = sb("posi", [P, NT], I32)
        arena = sb("arena", [P, 27300])
        idx = sb("idx", [P, N_SLOTS // P], I32)
        dest = sb("dest", [P, 2 * NT], I32)
        choice = sb("choice", [P, 2 * NT], I32)
        over = sb("over", [1, 3 * N_OVER], I32)
        at_in = [sb(f"at_in{q}", [P, 1], I32) for q in range(2)]
        at_out = [sb(f"at_out{q}", [P, 1], I32) for q in range(2)]
        slots = nc.dram_tensor("slots", (N_SLOTS, 1), I32).ap()
        rows = nc.dram_tensor("rows", (2 * T, D), F32).ap()
        back = nc.dram_tensor("back", (2 * T, D), F32).ap()

        def col(name, a=0, w=1):
            o = COL[name][0] + a
            return colt[:, o:o + w]

        def cs(name):
            return cst[:, CST[name][0]:CST[name][1]]

        def ar(off, n):
            return arena[:, off:off + n]

        def ar3(off, a, b):
            return arena[:, off:off + a * b].rearrange("p (a b) -> p a b", a=a)

        ident = cs("ident")
        ss = st[:, 0:4]
        ms = st[:, 4:8]
        rt = st[:, 8:12]
        rstd = st[:, 12:16]
        sums = st[:, 16:112].rearrange("p (w h) -> p w h", w=12)
        nm = st[:, 112:116].rearrange("p (u h) -> p u h", u=2)
        fac = st[:, 116:148]
        csum = st[:, 148:180]
        cmaxn = st[:, 180:212]
        mss = st[:, 212:220]
        mrt = st[:, 220:228]
        mrs = st[:, 228:236]
        hns = st[:, 236:300]
        hnr = st[:, 300:364]
        hni = st[:, 364:428]

        xn = ar3(0, NT, D)
        qT = ar3(0, 4, T)
        kvT = ar3(2048, 4, T)
        Vsw = ar3(4096, NT, 256)
        cqkv = ar3(5120, NT, 416)
        gates = ar3(6784, NT, 24)
        qTm = ar3(6880, HEADS, T)
        kTm = ar3(10976, HEADS, T)
        Vm = ar3(15072, NT, 512)
        O_nsa = ar3(17120, NT, 512)
        O_mla = ar3(19168, NT, 512)
        cqT = ar3(17120, 3, T)
        chat = ar3(18656, NT, 384)
        Pr = ar(21216, 2048).rearrange("p (u h k) -> p u h k", u=2, h=2)
        PTs = ar(23264, 2048).rearrange("p (u h k) -> p u h k", u=2, h=2)
        qkt = ar(21216, 3072).rearrange("p (u w c) -> p u w c", u=2, w=2)
        ropet = ar(24300, 1000)
        cmpt = ar(25312, 992)
        kb = ar(21216, 1984).rearrange("p (w l j) -> p w l j", w=2, l=32)
        Pc = ar(21216, 1024).rearrange("p (i h j) -> p i h j", i=NT, h=HEADS)
        PcT = ar(22240, 1024).rearrange("p (i c) -> p i c", i=NT)
        Vbd = ar(26304, 512).rearrange("p (g c) -> p g c", g=2)
        kcT = ar(26816, 32)
        gk = ar(26848, 32)
        gv4 = ar(26880, 128)
        oTn = ar3(6880, 4, T)
        oTm = ar3(8928, 4, T)
        mT = ar3(10976, ND, T)
        mgt = ar(0, 4096).rearrange("p (u k c) -> p u k c", u=2, k=4)
        ptmp = ar3(21216, 2, 1024)
        gT = ar3(4096, NF, T)
        cva = ar(15360, 2048).rearrange("p (u k c) -> p u k c", u=2, k=2)
        ga = ar3(17408, 2, T)
        pTs = ar3(24000, 2, T)
        E = ar3(0, NT, D)
        Gs = ar3(4096, NT, D)

        def tile(n):
            return ring[:, n % RING, :]

        def arrived(pe, n):
            pe.wait_ge(landed[n % RING], 16 * (n // RING + 1))


        uc = ar3(0, 12, T)
        uF = ar3(6144, 4, T)
        zt = ar3(8192, NT, CH)
        x0t = ar3(10240, NT, CH)
        Pk = ar3(12288, NT, CH)
        Mk = ar3(14336, NT, CH)
        HF = ar3(16384, NT, CH)
        HB = ar3(18432, NT, CH)
        prod = ar3(16384, 4, CH)
        Y = ar3(16384, NT, D)
        decs = ar3(20480, NT, CH)
        absb = ar(22528, 2048).rearrange("p (u c) -> p u c", u=2)
        vCS = ar(20480, 4096).rearrange("p (i w c) -> p i w c", i=NT, w=2)
        Kt = ar(24576, 2048).rearrange("p (u w c) -> p u w c", u=2, w=2)
        Kn = ar(26624, 512)
        YA = ar3(0, 4, CH)
        YB = ar3(2048, 4, CH)
        ysq = ar3(0, NT, D)
        yt = ar(4096, 2048).rearrange("p (u w c) -> p u w c", u=2, w=2)
        fws = ar(6144, 1024)
        fzs = ar(26624, 512)
        farg, fturn, fred, fh = [ar(24576 + 512 * q, 512)[0:64, :] for q in range(4)]
        sil = ar(4096, 512)
        hb = ar(4608, 512)
        hbT = ar(7168, 512)
        ysb = ar3(7680, 2, D)
        G = ar3(9728, 2 * NT, D)
        xo = ar3(18000, NT, D)
        Xg = ar3(22100, 2, D)
        XT = ar3(24148, 2, D)
        fbias, rsum_b = grow[:, 0:512], grow[:, 512:1024]
        RT = ar(5120, 2000)
        sel = RT[:, 144:272].rearrange("p (i e) -> p i e", i=NT)
        lg = RT[:, 0:144].rearrange("p (i c) -> p i c", i=NT)

        def opening(b):
            return isinstance(b, int) and b < 2

        def second_pool(pool):
            pool.wait_ge(S["p3_prod"], NT)
            pool.dma_start(fws[0:64, :], fwout).then_inc(S["f_in"], 16)
            pool.dma_start(fzs, fconst).then_inc(S["f_in"], 16)
            pool.wait_ge(S["post_x"], 3 * NT)
            pool.dma_start(ar(20480, 2048), decay).then_inc(S["decay_in"], 16)
            pool.dma_start(fbias, frow).then_inc(S["fb_in"], 16)
            pool.wait_ge(S["yo_ev"], NT)
            pool.dma_start(grow[:, :], grows[3, :, :]).then_inc(S["g_in"], 16)
            pool.wait_ge(S["norm_xn"], 4 * NT)
            for j in range(2 * NT):
                pool.dma_start(rows[j * P:(j + 1) * P, :], xn[:, j % NT, :]).then_inc(S["rows_st"], 16)
            pool.dma_start(grow[:, :], grows[4, :, :]).then_inc(S["g_in"], 16)
            pool.memset(ar(22100, 2048), 0.0).then_inc(S["xg_zero"], 1)
            pool.wait_ge(S["slots_set"], 16)
            pool.wait_ge(S["dest_ready"], 1)
            for j in range(2 * NT):
                pool.indirect_dma_start(out=slots, out_offset=bass.IndirectOffsetOnAxis(ap=dest[:, j:j + 1], axis=0),
                                        in_=choice[:, j:j + 1], in_offset=None).then_inc(S["slots_st"], 16)
            pool.wait_ge(S["slots_st"], 16 * 2 * NT)
            pool.dma_start(idx[:, :], slots.rearrange("(p n) c -> p (n c)", p=P)).then_inc(S["idx_in"], 16)
            pool.wait_ge(S["rows_st"], 16 * 2 * NT)
            pool.wait_ge(S["xg_zero"], 1)
            pool.wait_ge(S["idx_in"], 16)

            def gather(b, q, column):
                pool.wait_ge(S["x_tr"], b * 2 + 2)
                pool.sem_inc(S["gathers"], 1)
                nc.gpsimd.tensor_copy(at_in[q][:, :], idx[:, column]).then_inc(S["at_in"], 1)
                pool.wait_ge(S["at_in"], b + 1)
                pool.sem_inc(S["gathers"], 1)
                pool.indirect_dma_start(out=Xg[:, q, :], out_offset=None, in_=rows,
                                        in_offset=bass.IndirectOffsetOnAxis(ap=at_in[q][:, 0:1], axis=0),
                                        bounds_check=2 * T - 1, oob_is_err=False).then_inc(S[f"xg_in{q}"], 16)

            def scatter(b, half, q, column):
                if not opening(b):
                    pool.wait_ge(S[f"y_st{q}"], half * 16)
                    pool.sem_inc(S["scatters"], 1)
                nc.gpsimd.tensor_copy(at_out[q][:, :], idx[:, column]).then_inc(S["at_out"], 1)
                pool.wait_ge(S["at_out"], b + 1)
                pool.wait_ge(S["y_ev_act"], b + 2)
                pool.wait_ge(S["y_ev_dve"], b + 2)
                pool.sem_inc(S["scatters"], 1)
                pool.indirect_dma_start(out=back, out_offset=bass.IndirectOffsetOnAxis(ap=at_out[q][:, 0:1], axis=0),
                                        in_=ysb[:, q, :], in_offset=None,
                                        bounds_check=2 * T - 1, oob_is_err=False).then_inc(S[f"y_st{q}"], 16)

            def first_of(e):
                return slice(NT * e, NT * e + 1)

            gather(0, 0, first_of(0))
            gather(1, 1, first_of(1))
            for q in range(2):
                gather(2 + q, q, first_of(2 + q))
                scatter(q, 0, q, first_of(q))
            with pool.Fori(1, N_EXP // 2 - 1) as turn:
                for q in range(2):
                    gather(turn * 2 + (q + 2), q, bass.ds(turn * (2 * NT) + NT * (q + 2), 1))
                    scatter(turn * 2 + q, turn, q, bass.ds(turn * (2 * NT) + NT * q, 1))
            for q in range(2):
                scatter(N_EXP - 2 + q, N_EXP // 2 - 1, q, first_of(N_EXP - 2 + q))
            pool.wait_ge(S["over_ready"], 1)
            with pool.Fori(0, N_OVER // 2) as turn:
                for q in range(2):
                    valid = pool.value_load(over[0:1, bass.ds(turn * 2 + q, 1)], min_val=0, max_val=1)
                    with pool.If(valid > 0):
                        column = pool.value_load(over[0:1, bass.ds(turn * 2 + (q + N_OVER), 1)], min_val=0, max_val=NT * N_EXP - 1)
                        gather(turn * 2 + (N_EXP + q), q, bass.ds(column, 1))
                        scatter(turn * 2 + (N_EXP + q), turn + N_EXP // 2, q, bass.ds(column, 1))
                        pool.wait_ge(S[f"y_st{q}"], turn * 16 + 16 * (N_EXP // 2 + 1))
            for q in range(2):
                pool.wait_ge(S[f"y_st{q}"], 16 * (N_EXP // 2))
            for i in range(NT):
                for c in range(2):
                    pool.dma_start(G[:, 2 * i + c, :], back[(NT * c + i) * P:(NT * c + i + 1) * P, :]).then_inc(S[f"back{i}"], 16)
            for i in range(NT):
                pool.wait_ge(S["fin_y"], i + 1)
                pool.dma_start(out[i * P:(i + 1) * P, :], xo[:, i, :]).then_inc(S["out_st"], 16)
            pool.wait_ge(S["out_st"], 16 * NT)

        def expert_stream(sp):
            def part(g, places, first):
                for s in places:
                    sp.wait_ge(S["w_used"], g * RING + (W_EXP + s + 1 - RING))
                    sp.dma_start(ring[:, s, :], W[first + s, :, :]).then_inc(landed[s], 16)

            part(0, range(0, 4), W_EXP)
            part(0, range(8, 12), W_EXP - 4)
            with sp.Fori(1, N_EXP) as g:
                part(g, range(0, 4), g * RING + W_EXP)
                part(g, range(4, 8), g * RING + (W_EXP - RING + 4))
                part(g, range(8, 12), g * RING + (W_EXP - 4))
            part(N_EXP, range(4, 8), N_EXP * RING + (W_EXP - RING + 4))
            sp.wait_ge(S["over_ready"], 1)
            with sp.Fori(0, N_OVER // 2) as turn:
                for q in range(2):
                    valid = sp.value_load(over[0:1, bass.ds(turn * 2 + q, 1)], min_val=0, max_val=1)
                    with sp.If(valid > 0):
                        first = sp.value_load(over[0:1, bass.ds(turn * 2 + (q + 2 * N_OVER), 1)], min_val=0,
                                              max_val=N_TILES - RING)
                        for s in range(RING):
                            sp.wait_ge(S["w_used"], turn * (2 * RING) + (W_EXP + (N_EXP + q) * RING + s + 1))
                            sp.dma_start(ring[:, s, :], W[bass.ds(first + s, 1), :, :]).then_inc(landed[s], 16)

        def second_pe(pe):
            used = S["w_used"]
            pe.wait_ge(S["pg_sig"], NT)
            pe.wait_ge(S["f_in"], 32)
            nc.tensor.matmul(pb[0:64, 0, :], col("f_w_in", 0, 64)[0:33, :], fzs[0:33, :], start=True, stop=True)\
                .then_inc(S["fm_mm"], 1)
            for q in range(2):
                pe.wait_ge(S["fm_sin"], q + 1)
                nc.tensor.matmul(pb[0:64, q + 1, :], col("f_w_mid", 64 * q, 64)[0:64, :], fh, start=True, stop=True)\
                    .then_inc(S["fm_mm"], 1)
            pe.wait_ge(S["fm_sin"], 3)
            for i in range(NT):
                for h in range(2):
                    last = nc.tensor.matmul(pb[:, 2 * i + h, :], fh[:, i * P:(i + 1) * P], fws[0:64, h * 512:(h + 1) * 512],
                                            start=True, stop=True)
                last.then_inc(S["fo_mm"], 1)
            pe.wait_ge(S["fo_ev"], NT)
            for i in range(NT):
                pe.wait_ge(S["habs"], i + 1)
                for h in range(2):
                    last = nc.tensor.matmul(pb[:, 0, :], cs("ones"), absb[:, i % 2, h * 512:(h + 1) * 512],
                                            start=(i == 0 and h == 0), stop=(i == NT - 1 and h == 1))
                last.then_inc(S["hs_mm"], 1)
            pe.wait_ge(S["norm_xn"], 3 * NT)
            pe.wait_ge(S["hs_ready"], 1)
            tr_pe(pe, "n3", xn, NT, ND)
            tr_wait(pe, "n3")
            for m in range(16):
                n = W_IN2 + m
                arrived(pe, n)
                if m >= 8:
                    pe.wait_ge(S["in2_conv"], m - 7)
                for k in range(ND):
                    last = nc.tensor.matmul(pb[:, m % 8, :], tile(n)[:, k * P:(k + 1) * P], hT[:, k, :],
                                            start=(k == 0), stop=(k == ND - 1))
                last.then_inc(used, 1)
            pe.wait_ge(S["in2_conv"], 12)
            pe.wait_ge(S["in2_f"], 4)
            for i in range(NT):
                for w in range(2):
                    for m in range(4):
                        last = nc.tensor.matmul(pb[:, 2 * i + w, m * P:(m + 1) * P], uF[:, m, i * P:(i + 1) * P],
                                                cs("dft64")[:, w * P:(w + 1) * P], start=True, stop=True)
                last.then_inc(S["fd_mm"], 1)
            pe.wait_ge(S["fd_ev"], NT)
            pe.wait_ge(S["z_ready"], 4)
            tr_pe(pe, "z", uc[:, 4:8, :], 4, NT)
            tr_pe(pe, "x0", uc[:, 0:4, :], 4, NT, bank0=4)
            tr_wait(pe, "z")
            tr_wait(pe, "x0")
            pe.wait_ge(S["pm_ready"], 1)
            arrived(pe, W_DFT)
            for m in range(4):
                b = 4 * (m % 2)
                n = W_DFT + 1 + m
                arrived(pe, n)
                if m == 1:
                    pe.wait_ge(S["kf_ev"], 3)
                if m >= 2:
                    pe.wait_ge(S["y_ready"], m - 1)
                for w, src in ((0, Pk), (1, Mk)):
                    for k in range(NT):
                        last = nc.tensor.matmul(pb[:, b + w, :], tile(n)[:, (4 * w + k) * P:(4 * w + k + 1) * P], src[:, k, :],
                                                start=(k == 0), stop=(k == NT - 1))
                    last.then_inc(S["kf_mm"], 1)
                if m == 0:
                    for k in range(NT):
                        last = nc.tensor.matmul(pb[:, 4, :], tile(W_DFT)[:, k * P:(k + 1) * P], Pk[:, k, :],
                                                start=(k == 0), stop=(k == NT - 1))
                    last.then_inc(S["kf_mm"], 1)
                for w in range(2):
                    basis = tile(W_DFT) if m == 0 and w == 1 else tile(n)
                    for k in range(NT):
                        last = nc.tensor.matmul(pb[:, b + 2 + w, :], basis[:, (4 * w + k) * P:(4 * w + k + 1) * P], zt[:, k, :],
                                                start=(k == 0), stop=(k == NT - 1))
                last.then_inc(used, 2 if m == 0 else 1)
            pe.wait_ge(S["y_ready"], 4)
            for i in range(NT):
                n = W_IDFT + i
                arrived(pe, n)
                for w, src in ((0, YA), (1, YB)):
                    for k in range(NT):
                        last = nc.tensor.matmul(pb[:, i, :], tile(n)[:, (4 * w + k) * P:(4 * w + k + 1) * P], src[:, k, :],
                                                start=(w == 0 and k == 0), stop=(w == 1 and k == NT - 1))
                last.then_inc(used, 1)
            for i in range(NT):
                n = W_FFT + i
                arrived(pe, n)
                for w in range(2):
                    for k in range(NT):
                        last = nc.tensor.matmul(pb[:, 4 + i, :], tile(n)[:, (4 * w + k) * P:(4 * w + k + 1) * P], vCS[:, k, w, :],
                                                start=(w == 0 and k == 0), stop=(w == 1 and k == NT - 1))
                last.then_inc(used, 1)
            pe.wait_ge(S["hn_y"], NT)
            tr_pe(pe, "y2", Y, NT, ND)
            tr_wait(pe, "y2")
            tokens_pe(pe, W_OUT2, ND, hT, S["wo2_mm"])
            pe.wait_ge(S["norm_xn"], 4 * NT)
            tr_pe(pe, "n4", xn, NT, ND)
            tr_wait(pe, "n4")
            arrived(pe, W_ROUTE)
            for i in range(NT):
                for k in range(ND):
                    last = nc.tensor.matmul(pb[:, i, 0:36], hT[:, k, i * P:(i + 1) * P], tile(W_ROUTE)[:, 36 * k:36 * k + 36],
                                            start=(k == 0), stop=(k == ND - 1))
            last.then_inc(used, 1)
            pe.wait_ge(S["rt_lg"], 1)
            pe.wait_ge(S["sel_ready"], 1)
            for i in range(NT):
                for j in range(i + 1):
                    nc.tensor.matmul(pb[:, 4 + i, 0:32], cs("tri") if j == i else cs("ones"), sel[:, j, :],
                                     start=(j == 0), stop=(j == i))
            for j in range(NT):
                last = nc.tensor.matmul(pb[:, 0, 0:32], cs("ones"), sel[:, j, :], start=(j == 0), stop=(j == NT - 1))
            last.then_inc(S["rank_mm"], 1)
            pe.wait_ge(S["over_ready"], 1)
            pe.sem_inc(S["x_tr"], 4)

            def turn_rows(b, half, q):
                pe.wait_ge(S[f"xg_in{q}"], half * 16 + 16)
                pe.wait_ge(S["x_ev_dve"], b + 1)
                pe.wait_ge(S["x_ev_act"], b + 1)
                for h in range(2):
                    for k in range(4):
                        last = nc.tensor.transpose(pb[:, 2 + h, k * P:(k + 1) * P], Xg[:, q, (4 * h + k) * P:(4 * h + k + 1) * P], ident)
                    last.then_inc(S["x_tr"], 1)

            def product(b, q, bank, place, skipped=0):
                for k in range(ND):
                    s = place + k // 2
                    if k % 2 == 0:
                        pe.wait_ge(landed[s], b * 16 + 16 * (W_EXP // RING + 1))
                    last = nc.tensor.matmul(pb[:, bank, :], XT[:, q, k * P:(k + 1) * P],
                                            ring[:, s, (k % 2) * 512:(k % 2 + 1) * 512], start=(k == 0), stop=(k == ND - 1))
                    if k % 2:
                        last.then_inc(used, 1 + (skipped if k == ND - 1 else 0))

            def gate(b, q, skipped=0):
                pe.wait_ge(S["x_ev_dve"], b + 2)
                pe.wait_ge(S["x_ev_act"], b + 2)
                pe.wait_ge(S["ex_sig"], b + 1)
                product(b, q, 0, 0, skipped)

            def turn_hidden(b):
                pe.wait_ge(S["ex_hid"], b + 1)
                for k in range(4):
                    last = nc.tensor.transpose(pb[:, 4, k * P:(k + 1) * P], hb[:, k * P:(k + 1) * P], ident)
                last.then_inc(S["h_tr"], 1)

            def down(b, place, skipped=0):
                pe.wait_ge(S["h_ev"], b + 1)
                pe.wait_ge(S["y_ev_act"], b + 1)
                pe.wait_ge(S["y_ev_dve"], b + 1)
                for k in range(4):
                    pe.wait_ge(landed[place + k], b * 16 + 16 * (W_EXP // RING + 1))
                    for h in range(2):
                        last = nc.tensor.matmul(pb[:, 6 + h, :], hbT[:, k * P:(k + 1) * P],
                                                ring[:, place + k, h * 512:(h + 1) * 512], start=(k == 0), stop=(k == 3))
                    last.then_inc(used, 1 + (skipped if k == 3 else 0))

            def between(b, half, q, follow):
                gate(b + 1, 1 - q)
                turn_hidden(b)
                if follow:
                    turn_rows(b + 2, half + 1, q)
                down(b, 4)
                product(b + 1, 1 - q, 1, 8, 0 if follow else 4)

            turn_rows(0, 0, 0)
            turn_rows(1, 0, 1)
            gate(0, 0, 4)
            product(0, 0, 1, 8)
            with pe.Fori(0, N_EXP // 2 - 1) as turn:
                for q in range(2):
                    between(turn * 2 + q, turn, q, True)
            between(N_EXP - 2, N_EXP // 2 - 1, 0, False)
            turn_hidden(N_EXP - 1)
            down(N_EXP - 1, 4, 4)
            with pe.Fori(0, N_OVER // 2) as turn:
                for q in range(2):
                    valid = pe.value_load(over[0:1, bass.ds(turn * 2 + q, 1)], min_val=0, max_val=1)
                    with pe.If(valid > 0):
                        b = turn * 2 + (N_EXP + q)
                        turn_rows(b, turn + N_EXP // 2, q)
                        gate(b, q)
                        product(b, q, 1, 4)
                        turn_hidden(b)
                        down(b, 8)

        def second_act(act):
            for q in range(3):
                act.wait_ge(S["fm_arg"], q + 1)
                nc.scalar.activation(fh, fred, ACT.Sin).then_inc(S["fm_sin"], 1)
            for i in range(NT):
                act.wait_ge(S["fo_ev"], i + 1)
                if i >= 2:
                    act.wait_ge(S["hs_mm"], i - 1)
                nc.scalar.activation(absb[:, i % 2, 0:512], HF[:, i, :], ACT.Abs)
                nc.scalar.activation(absb[:, i % 2, 512:1024], HB[:, i, :], ACT.Abs).then_inc(S["habs"], 1)
            norm_act(act, "n3", S["post_x"], 3 * NT)
            tr_act(act, "n3", hT, ND, "norm1")
            for m in range(16):
                act.wait_ge(S["w_used"], W_IN2 + m + 1)
                if m < 12:
                    nc.scalar.activation(uc[:, m, :], pb[:, m % 8, :], ACT.Identity, scale=col("conv_w", 12 + m),
                                         bias=col("conv_b", m)).then_inc(S["in2_lin"], 1)
                else:
                    nc.scalar.activation(uF[:, m - 12, :], pb[:, m % 8, :], ACT.Copy).then_inc(S["in2_f"], 1)
            for i in range(NT):
                act.wait_ge(S["fd_mm"], i + 1)
                nc.scalar.activation(vCS[:, i, :, :], pb[:, 2 * i:2 * i + 2, :], ACT.Copy).then_inc(S["fd_ev"], 1)
            tr_act(act, "z", zt, NT)
            tr_act(act, "x0", x0t, NT, bank0=4)
            count = 0
            for m in range(4):
                if m >= 2:
                    act.wait_ge(S["y_ready"], m - 1)
                for w in range(3 if m == 0 else 2):
                    count += 1
                    act.wait_ge(S["kf_mm"], count)
                    src = pb[:, 4, :] if w == 2 else pb[:, 4 * (m % 2) + w, :]
                    nc.scalar.activation(Kn if w == 2 else Kt[:, m % 2, w, :], src, ACT.Copy).then_inc(S["kf_ev"], 1)
            for i in range(NT):
                act.wait_ge(S["w_used"], W_FFT + i + 1)
                act.wait_ge(S["y_ready"], 4)
                nc.scalar.activation(Y[:, i, 512:1024], pb[:, 4 + i, :], ACT.Copy).then_inc(S["fo2_ev"], 1)
            for i in range(NT):
                act.wait_ge(S["yo_ev"], i + 1)
                act.wait_ge(S["fo2_ev"], i + 1)
                nc.scalar.activation(ysq[:, i, :], Y[:, i, :], ACT.Square).then_inc(S["hn_sq"], 1)
            act.wait_ge(S["hn_ms"], 1)
            nc.scalar.activation(hnr, hns, ACT.Sqrt).then_inc(S["hn_rt"], 1)
            tr_act(act, "y2", hT, ND, "mix_g")
            norm_act(act, "n4", S["wo2_x"], NT)
            tr_act(act, "n4", hT, ND)
            act.wait_ge(S["rt_g"], 1)
            nc.scalar.activation(RT[:, 288:304], RT[:, 272:288], ACT.Exp).then_inc(S["rt_exp"], 1)
            act.wait_ge(S["rt_d"], 1)
            nc.scalar.activation(RT[:, 308:312], RT[:, 304:308], ACT.Exp).then_inc(S["rt_exp"], 1)
            act.wait_ge(S["over_ready"], 1)
            act.sem_inc(S["y_ev_act"], 1)
            act.sem_inc(S["x_ev_act"], 1)
            act.sem_inc(S["ex_sig"], 1)

            def rows_act(b, q):
                act.wait_ge(S["x_tr"], b * 2 + 6)
                nc.scalar.activation(XT[:, q, 512:1024], pb[:, 3, :], ACT.Copy).then_inc(S["x_ev_act"], 1)

            def hidden_act(b):
                act.wait_ge(S["h_tr"], b + 1)
                nc.scalar.activation(hbT, pb[:, 4, :], ACT.Copy).then_inc(S["h_ev"], 1)

            def silu_act(b, past):
                act.wait_ge(S["w_used"], b * RING + past)
                act.wait_ge(S["ex_mul"], b + 1)
                nc.scalar.activation(sil, pb[:, 0, :], ACT.Silu).then_inc(S["ex_sig"], 1)

            def out_act(b, half, q, past):
                act.wait_ge(S["w_used"], b * RING + past)
                if not opening(b):
                    act.wait_ge(S[f"y_st{q}"], half * 16)
                nc.scalar.activation(ysb[:, q, 0:512], pb[:, 6, :], ACT.Copy).then_inc(S["y_ev_act"], 1)

            def between_act(b, half, q, follow):
                hidden_act(b)
                silu_act(b + 1, W_EXP + 4)
                if follow:
                    rows_act(b + 2, q)
                out_act(b, half, q, W_EXP + RING + 8)

            rows_act(0, 0)
            rows_act(1, 1)
            silu_act(0, W_EXP + 4)
            for q in range(2):
                between_act(q, 0, q, True)
            with act.Fori(1, N_EXP // 2 - 1) as turn:
                for q in range(2):
                    between_act(turn * 2 + q, turn, q, True)
            between_act(N_EXP - 2, N_EXP // 2 - 1, 0, False)
            hidden_act(N_EXP - 1)
            out_act(N_EXP - 1, N_EXP // 2 - 1, 1, W_EXP + RING + 8)
            with act.Fori(0, N_OVER // 2) as turn:
                for q in range(2):
                    valid = act.value_load(over[0:1, bass.ds(turn * 2 + q, 1)], min_val=0, max_val=1)
                    with act.If(valid > 0):
                        b = turn * 2 + (N_EXP + q)
                        rows_act(b, q)
                        silu_act(b, W_EXP + RING + 4)
                        hidden_act(b)
                        out_act(b, turn + N_EXP // 2, q, W_EXP + 2 * RING)
            norm_act(act, "n5", S["moe_x"], NT)

        def second_dve(dve, chain):
            def L(ins):
                link(dve, chain, ins)

            TT, TS, STT = nc.vector.tensor_tensor, nc.vector.tensor_scalar, nc.vector.scalar_tensor_tensor
            for q in range(3):
                dve.wait_ge(S["fm_mm"], q + 1)
                b = col("f_b_in") if q == 0 else col("f_b_mid", q - 1)
                L(TS(farg, pb[0:64, q, :], b[0:64, :], col("f_freq", q)[0:64, :], ALU.add, ALU.mult))
                reduce_angle(L, nc, farg, fturn, fred)
                TS(fred, fred, PI_LOW, -PI_LOW, ALU.min, ALU.max).then_inc(S["fm_arg"], 1)
            dve.wait_ge(S["decay_in"], 16)
            for i in range(NT):
                dve.wait_ge(S["fo_mm"], i + 1)
                TT(HF[:, i, :], pb[:, 2 * i, :], decs[:, i, :], ALU.mult)
                ins = TT(HB[:, i, :], pb[:, 2 * i + 1, :], decs[:, i, :], ALU.mult)
                if i == 0:
                    L(ins)
                    ins = nc.vector.memset(HB[0:1, 0, :], 0.0)
                ins.then_inc(S["fo_ev"], 1)
                dve.wait_ge(S["fo_ev"], i + 1)
            for i in range(NT):
                TT(Pk[:, i, :], HF[:, i, :], HB[:, i, :], ALU.add)
                last = TT(Mk[:, i, :], HF[:, i, :], HB[:, i, :], ALU.subtract)
            last.then_inc(S["pm_ready"], 1)
            dve.wait_ge(S["hs_mm"], NT)
            dve.wait_ge(S["fb_in"], 16)
            L(nc.vector.reciprocal(rsum_b, pb[:, 0, :]))
            TS(rsum_b, rsum_b, 2.0 / (2 * T), None, ALU.mult).then_inc(S["hs_ready"], 1)
            norm_dve(dve, chain, "n3")
            tr_dve(dve, "n3", hT, ND, "norm1")
            for m in range(12):
                dve.wait_ge(S["in2_lin"], m + 1)
                u = pb[:, m % 8, :]
                L(STT(out=uc[:, m, 1:T], in0=u[:, 0:T - 1], scalar=col("conv_w", m), in1=uc[:, m, 1:T],
                      op0=ALU.mult, op1=ALU.add))
                STT(out=uc[:, m, 0:T - 1], in0=u[:, 1:T], scalar=col("conv_w", 24 + m), in1=uc[:, m, 0:T - 1],
                    op0=ALU.mult, op1=ALU.add).then_inc(S["in2_conv"], 1)
                if m >= 8:
                    dve.wait_ge(S["in2_conv"], m + 1)
                    TT(uc[:, m - 4, :], uc[:, m - 4, :], uc[:, m, :], ALU.mult).then_inc(S["z_ready"], 1)
            tr_dve(dve, "z", zt, NT)
            tr_dve(dve, "x0", x0t, NT, bank0=4)
            for m in range(4):
                b = 4 * (m % 2)
                dve.wait_ge(S["kf_ev"], 3 + 2 * m)
                dve.wait_ge(S["w_used"], W_DFT + 2 + m)
                if m:
                    dve.wait_ge(S["y_ready"], m)
                KA, KB = Kt[:, m % 2, 0, :], Kt[:, m % 2, 1, :]
                ZA, ZB = pb[:, b + 2, :], pb[:, b + 3, :]
                TT(prod[:, 0, :], ZA, KA, ALU.mult)
                TT(prod[:, 1, :], ZB, KB, ALU.mult)
                TT(prod[:, 2, :], ZA, KB, ALU.mult)
                L(TT(prod[:, 3, :], ZB, Kn if m == 0 else KA, ALU.mult))
                TT(YA[:, m, :], prod[:, 0, :], prod[:, 1, :], ALU.subtract)
                TT(YB[:, m, :], prod[:, 2, :], prod[:, 3, :], ALU.add).then_inc(S["y_ready"], 1)
            dve.wait_ge(S["y_ready"], 4)
            for i in range(NT):
                dve.wait_ge(S["w_used"], W_IDFT + i + 1)
                TT(yt[:, i % 2, 0, :], pb[:, i, :], rsum_b, ALU.mult)
                L(TT(yt[:, i % 2, 1, :], zt[:, i, :], fbias, ALU.mult))
                L(TT(yt[:, i % 2, 0, :], yt[:, i % 2, 0, :], yt[:, i % 2, 1, :], ALU.add))
                TT(Y[:, i, 0:512], yt[:, i % 2, 0, :], x0t[:, i, :], ALU.mult).then_inc(S["yo_ev"], 1)
                dve.wait_ge(S["yo_ev"], i + 1)
            for i in range(NT):
                dve.wait_ge(S["hn_sq"], i + 1)
                ins = nc.vector.tensor_reduce(hni[:, 16 * i:16 * i + 16], ysq[:, i, :].rearrange("p (h c) -> p h c", c=64),
                                              AX.X, ALU.add)
            L(ins)
            TS(hns, hni, 1.0 / 64, EPS, ALU.mult, ALU.add).then_inc(S["hn_ms"], 1)
            dve.wait_ge(S["hn_rt"], 1)
            L(nc.vector.reciprocal(hni, hnr))
            for i in range(NT):
                y = Y[:, i, :].rearrange("p (h c) -> p h c", c=64)
                TT(y, y, hni[:, 16 * i:16 * i + 16].unsqueeze(2).broadcast_to([P, 16, 64]), ALU.mult).then_inc(S["hn_y"], 1)
            tr_dve(dve, "y2", hT, ND, "mix_g")
            for i in range(NT):
                product(dve, S["wo2_mm"], 0, i, W_ROUTE - 1)
                TT(X[:, i, :], X[:, i, :], pair(i), ALU.add).then_inc(S["wo2_x"], 1)
            dve.wait_ge(S["wo2_x"], NT)
            dve.wait_ge(S["g_in"], 64)
            norm_dve(dve, chain, "n4", grow)
            tr_dve(dve, "n4", hT, ND)
            dve.wait_ge(S["w_used"], W_EXP)
            b4 = [P, NT, 4]
            TT(lg, pb[:, 0:4, 0:36], col("r_bias", 0, 36).unsqueeze(1).broadcast_to([P, NT, 36]), ALU.add)\
                .then_inc(S["rt_lg"], 1)
            dve.wait_ge(S["rt_lg"], 1)
            glog = lg[:, :, 0:4]
            elog = lg[:, :, 4:36]

            def by_t(a, n):
                return RT[:, a:a + NT * n].rearrange("p (i c) -> p i c", i=NT)

            def first_of(src, n, iota, best, mark, low, hot):
                L(nc.vector.tensor_reduce(best, src, AX.X, ALU.max))
                L(TT(mark, src, best.unsqueeze(2).broadcast_to([P, NT, n]), ALU.is_equal))
                L(STT(out=mark, in0=mark, scalar=-64.0, in1=iota.unsqueeze(1).broadcast_to([P, NT, n]), op0=ALU.mult, op1=ALU.add))
                L(nc.vector.tensor_reduce(low, mark, AX.X, ALU.min))
                L(TT(hot, mark, low.unsqueeze(2).broadcast_to([P, NT, n]), ALU.is_equal))

            gbest, low, ghot, gmark = RT[:, 312:316], RT[:, 316:320], by_t(320, 4), by_t(336, 4)
            first_of(glog, 4, cs("giota"), gbest, gmark, low, ghot)
            TT(by_t(272, 4), glog, gbest.unsqueeze(2).broadcast_to(b4), ALU.subtract).then_inc(S["rt_g"], 1)
            L(TS(gmark, ghot, -NEG, NEG, ALU.mult, ALU.add))
            masked, mark, hot1, hot2 = by_t(352, 32), by_t(480, 32), by_t(608, 32), by_t(736, 32)
            for i in range(NT):
                ins = TT(masked[:, i, :].rearrange("p (g c) -> p g c", g=4), elog[:, i, :].rearrange("p (g c) -> p g c", g=4),
                         gmark[:, i, :].unsqueeze(2).broadcast_to([P, 4, 8]), ALU.add)
            L(ins)
            best1, best2 = RT[:, 864:868], RT[:, 868:872]
            first_of(masked, 32, cs("eiota"), best1, mark, low, hot1)
            L(STT(out=masked, in0=hot1, scalar=2 * NEG, in1=masked, op0=ALU.mult, op1=ALU.add))
            first_of(masked, 32, cs("eiota"), best2, mark, low, hot2)
            TT(sel, hot1, hot2, ALU.add).then_inc(S["sel_ready"], 1)
            TT(RT[:, 304:308], best2, best1, ALU.subtract).then_inc(S["rt_d"], 1)
            dve.wait_ge(S["rt_exp"], 2)
            L(nc.vector.tensor_reduce(RT[:, 872:876], by_t(288, 4), AX.X, ALU.add))
            L(TS(RT[:, 876:880], RT[:, 308:312], 1.0, None, ALU.add))
            L(TT(RT[:, 872:876], RT[:, 872:876], RT[:, 876:880], ALU.mult))
            L(nc.vector.reciprocal(RT[:, 880:884], RT[:, 872:876]))
            L(TT(RT[:, 884:888], RT[:, 880:884], RT[:, 308:312], ALU.mult))
            dve.wait_ge(S["rank_mm"], 1)
            for c, hot in ((0, hot1), (1, hot2)):
                L(TT(masked, hot, pb[:, 4:8, 0:32], ALU.mult))
                L(nc.vector.tensor_reduce(RT[:, 888 + 4 * c:892 + 4 * c], masked, AX.X, ALU.add))
                L(TT(masked, hot, cs("eiota").unsqueeze(1).broadcast_to([P, NT, 32]), ALU.mult))
                L(nc.vector.tensor_reduce(RT[:, 896 + 4 * c:900 + 4 * c], masked, AX.X, ALU.add))
            rank, which, slot = RT[:, 888:896], RT[:, 896:904], RT[:, 904:912]
            L(TS(slot, rank, float(P), None, ALU.is_ge))
            for n in (2, 3):
                L(TS(RT[:, 912:920], rank, float(n * P), None, ALU.is_ge))
                L(TT(slot, slot, RT[:, 912:920], ALU.add))
            L(TS(slot, slot, 1.0 - P * N_SLOTS // P, None, ALU.mult))
            L(STT(out=slot, in0=rank, scalar=float(N_SLOTS // P), in1=slot, op0=ALU.mult, op1=ALU.add))
            L(STT(out=slot, in0=which, scalar=float(NT), in1=slot, op0=ALU.mult, op1=ALU.add))
            nc.vector.tensor_copy(choice[:, :], cs("choice"))
            nc.vector.tensor_copy(dest[:, :], RT[:, 904:912]).then_inc(S["dest_ready"], 1)
            o1 = RT[0:1, :]
            extra, incl, alt, both = o1[:, 920:952], o1[:, 952:984], o1[:, 984:1016], o1[:, 1016:1272]
            L(TS(extra, pb[0:1, 0, 0:32], float(P), None, ALU.is_gt))
            for n in (2, 3):
                L(TS(alt, pb[0:1, 0, 0:32], float(n * P), None, ALU.is_gt))
                L(TT(extra, extra, alt, ALU.add))
            L(nc.vector.tensor_copy(incl, extra))
            for step in (1, 2, 4, 8, 16):
                L(nc.vector.tensor_copy(alt, incl))
                L(TT(incl[:, step:32], alt[:, step:32], alt[:, 0:32 - step], ALU.add))
            v = cs("eiota")[0:1, 0:N_OVER]
            both3 = both.rearrange("p (v e) -> p v e", e=32)
            L(TT(both3, incl.unsqueeze(1).broadcast_to([1, N_OVER, 32]), v.unsqueeze(2).broadcast_to([1, N_OVER, 32]), ALU.is_le))
            res = o1[:, 1272:1272 + 4 * N_OVER].rearrange("p (k v) -> p k v", k=4)
            L(nc.vector.tensor_reduce(res[:, 3, :], both3, AX.X, ALU.add))
            L(TT(both3, both3, extra.unsqueeze(1).broadcast_to([1, N_OVER, 32]), ALU.mult))
            L(nc.vector.tensor_reduce(res[:, 1, :], both3, AX.X, ALU.add))
            L(TT(res[:, 1, :], v, res[:, 1, :], ALU.subtract))
            L(TS(res[:, 3, :], res[:, 3, :], float(N_EXP - 1), None, ALU.min))
            L(TS(res[:, 1, :], res[:, 1, :], 1.0, float(NT - 1), ALU.add, ALU.min))
            L(STT(out=res[:, 1, :], in0=res[:, 3, :], scalar=float(NT), in1=res[:, 1, :], op0=ALU.mult, op1=ALU.add))
            L(TS(res[:, 2, :], res[:, 3, :], float(RING), float(W_EXP), ALU.mult, ALU.add))
            L(TS(res[:, 0, :], v, incl[:, 31:32], None, ALU.is_lt))
            L(nc.vector.tensor_copy(over[:, :], o1[:, 1272:1272 + 3 * N_OVER]))
            dve.sem_inc(S["y_ev_dve"], 1)
            dve.sem_inc(S["x_ev_dve"], 1)
            dve.sem_inc(S["ex_mul"], 1)
            nc.vector.tensor_copy(o1[:, 1272:1273], o1[:, 1273:1274]).then_inc(S["over_ready"], 1)

            def rows_dve(b, q):
                dve.wait_ge(S["x_tr"], b * 2 + 5)
                nc.vector.tensor_copy(XT[:, q, 0:512], pb[:, 2, :]).then_inc(S["x_ev_dve"], 1)

            def hidden_dve(b, past):
                dve.wait_ge(S["w_used"], b * RING + past)
                dve.wait_ge(S["ex_sig"], b + 2)
                TT(hb, sil, pb[:, 1, :], ALU.mult).then_inc(S["ex_hid"], 1)
                dve.wait_ge(S["ex_hid"], b + 1)
                dve.sem_inc(S["ex_mul"], 1)

            def out_dve(b, half, q, past):
                dve.wait_ge(S["w_used"], b * RING + past)
                if not opening(b):
                    dve.wait_ge(S[f"y_st{q}"], half * 16)
                nc.vector.tensor_copy(ysb[:, q, 512:1024], pb[:, 7, :]).then_inc(S["y_ev_dve"], 1)

            def between_dve(b, half, q, follow):
                if follow:
                    rows_dve(b + 2, q)
                out_dve(b, half, q, W_EXP + RING + 8)
                hidden_dve(b + 1, W_EXP + RING)

            rows_dve(0, 0)
            rows_dve(1, 1)
            hidden_dve(0, W_EXP + RING)
            for q in range(2):
                between_dve(q, 0, q, True)
            with dve.Fori(1, N_EXP // 2 - 1) as turn:
                for q in range(2):
                    between_dve(turn * 2 + q, turn, q, True)
            between_dve(N_EXP - 2, N_EXP // 2 - 1, 0, False)
            out_dve(N_EXP - 1, N_EXP // 2 - 1, 1, W_EXP + RING + 8)
            with dve.Fori(0, N_OVER // 2) as turn:
                for q in range(2):
                    valid = dve.value_load(over[0:1, bass.ds(turn * 2 + q, 1)], min_val=0, max_val=1)
                    with dve.If(valid > 0):
                        b = turn * 2 + (N_EXP + q)
                        rows_dve(b, q)
                        hidden_dve(b, W_EXP + RING + 8)
                        out_dve(b, turn + N_EXP // 2, q, W_EXP + 2 * RING)
            for i in range(NT):
                dve.wait_ge(S[f"back{i}"], 32)
                L(STT(out=X[:, i, :], in0=G[:, 2 * i, :], scalar=RT[:, 880 + i:881 + i], in1=X[:, i, :], op0=ALU.mult, op1=ALU.add))
                STT(out=X[:, i, :], in0=G[:, 2 * i + 1, :], scalar=RT[:, 884 + i:885 + i], in1=X[:, i, :],
                    op0=ALU.mult, op1=ALU.add).then_inc(S["moe_x"], 1)
            dve.wait_ge(S["norm_ss"], 5 * NT)
            TS(ms, ss, 1.0 / D, EPS, ALU.mult, ALU.add).then_inc(S["norm_ms"], 1)
            dve.wait_ge(S["norm_rt"], 5)
            dve.wait_ge(S["g_in"], 80)
            L(nc.vector.reciprocal(rstd, rt))
            for i in range(NT):
                STT(out=xo[:, i, :], in0=X[:, i, :], scalar=rstd[:, i:i + 1], in1=grow[:, :], op0=ALU.mult, op1=ALU.mult)\
                    .then_inc(S["fin_y"], 1)

        block = ctx.enter_context(nc.Block())

        @block.sync
        def _(sp):
            for s in range(RING):
                sp.dma_start(ring[:, s, :], W[s, :, :]).then_inc(landed[s], 16)
            with sp.Fori(1, W_EXP // RING) as turn:
                for s in range(RING):
                    sp.wait_ge(S["w_used"], turn * RING + (s + 1 - RING))
                    sp.dma_start(ring[:, s, :], W[turn * RING + s, :, :]).then_inc(landed[s], 16)
            expert_stream(sp)

        @block.gpsimd
        def _(pool):
            pool.dma_start(colt[:, :], cols).then_inc(S["small_in"], 16)
            pool.dma_start(cst[:, :], csts).then_inc(S["small_in"], 16)
            pool.dma_start(posi[:, :], pos).then_inc(S["pos_in"], 16)
            pool.dma_start(cmpt, cmp_tab).then_inc(S["tab_in"], 16)
            pool.dma_start(grow[:, :], grows[0, :, :]).then_inc(S["g_in"], 16)
            pool.dma_start(idx[:, :], free).then_inc(S["past_set"], 16)
            pool.wait_ge(S["past_set"], 16)
            pool.dma_start(slots.rearrange("(p n) c -> p (n c)", p=P), idx[:, :]).then_inc(S["slots_set"], 16)
            pool.wait_ge(S["post_x"], NT)
            pool.dma_start(ar(24000, 1024), pT).then_inc(S["p_in"], 16)
            pool.dma_start(grow[:, :], grows[1, :, :]).then_inc(S["g_in"], 16)
            pool.wait_ge(S["post_x"], 2 * NT)
            pool.dma_start(grow[:, :], grows[2, :, :]).then_inc(S["g_in"], 16)
            second_pool(pool)

        def norm_act(act, n, ready, count):
            act.wait_ge(ready, count)
            for i in range(NT):
                if NT * NORMS.index(n) + i:
                    act.wait_ge(S["norm_ss"], NT * NORMS.index(n) + i)
                nc.scalar.activation(junk[:, :], X[:, i, :], ACT.Square, accum_out=ss[:, i:i + 1])\
                    .then_inc(S["norm_ss"], 1)
            act.wait_ge(S["norm_ms"], NORMS.index(n) + 1)
            nc.scalar.activation(rt, ms, ACT.Sqrt).then_inc(S["norm_rt"], 1)

        def link(dve, chain, ins):
            chain[0] += 1
            ins.then_inc(S["dve_chain"], 1)
            dve.wait_ge(S["dve_chain"], chain[0])

        def norm_dve(dve, chain, n, gain=None):
            at = NORMS.index(n)
            dve.wait_ge(S["norm_ss"], NT * (at + 1))
            nc.vector.tensor_scalar(ms, ss, 1.0 / D, EPS, ALU.mult, ALU.add).then_inc(S["norm_ms"], 1)
            dve.wait_ge(S["norm_rt"], at + 1)
            link(dve, chain, nc.vector.reciprocal(rstd, rt))
            for i in range(NT):
                if gain is None:
                    ins = nc.vector.tensor_scalar(xn[:, i, :], X[:, i, :], rstd[:, i:i + 1], None, ALU.mult)
                else:
                    ins = nc.vector.scalar_tensor_tensor(out=xn[:, i, :], in0=X[:, i, :], scalar=rstd[:, i:i + 1],
                                                         in1=gain[:, :], op0=ALU.mult, op1=ALU.mult)
                ins.then_inc(S["norm_xn"], 1)

        def tr_pe(pe, n, src, A, B, bank0=0):
            for b in range(B):
                for a in range(A):
                    last = nc.tensor.transpose(pb[:, bank0 + b, a * P:(a + 1) * P], src[:, a, b * P:(b + 1) * P], ident)
                last.then_inc(S["turned"], 1)

        def tr_dve(dve, n, dst, B, gain=None, bank0=0):
            for b in range(0, B, 2):
                dve.wait_ge(S["turned"], TURNS[n][0] + b + 1)
                if gain:
                    ins = nc.vector.tensor_scalar(dst[:, b, :], pb[:, bank0 + b, :], col(gain, b), None, ALU.mult)
                else:
                    ins = nc.vector.tensor_copy(dst[:, b, :], pb[:, bank0 + b, :])
                ins.then_inc(S["copied_dve"], 1)

        def tr_act(act, n, dst, B, gain=None, bank0=0):
            for b in range(1, B, 2):
                act.wait_ge(S["turned"], TURNS[n][0] + b + 1)
                nc.scalar.activation(dst[:, b, :], pb[:, bank0 + b, :], ACT.Copy, scale=col(gain, b) if gain else 1.0)\
                    .then_inc(S["copied_act"], 1)

        def tr_wait(eng, n):
            eng.wait_ge(S["copied_dve"], sum(TURNS[n]) // 2)
            eng.wait_ge(S["copied_act"], sum(TURNS[n]) // 2)

        def tokens_pe(pe, base, K, src, done):
            for k in range(K):
                arrived(pe, base + k)
                for i in range(NT):
                    for h in range(2):
                        last = nc.tensor.matmul(pb[:, 2 * i + h, :], src[:, k, i * P:(i + 1) * P],
                                                tile(base + k)[:, h * 512:(h + 1) * 512],
                                                start=(k == 0), stop=(k == K - 1))
                    if k == K - 1 and i < NT - 1:
                        last.then_inc(done, 1)
                last.then_inc(S["w_used"], 1)

        def product(eng, sem, before, i, last_tile):
            if i < NT - 1:
                eng.wait_ge(sem, (NT - 1) * before + i + 1)
            else:
                eng.wait_ge(S["w_used"], last_tile + 1)

        def pair(i):
            return pb[:, 2 * i:2 * i + 2, :].rearrange("p b c -> p (b c)")

        def post_act(act, n, src, last_tile=None):
            at = POSTS.index(n)
            for i in range(NT):
                if last_tile is None:
                    act.wait_ge(S["p3_prod"], i + 1)
                else:
                    product(act, S["post_mm"], at, i, last_tile)
                if i:
                    act.wait_ge(S["post_ss"], NT * at + i)
                nc.scalar.activation(junk[:, :], src(i), ACT.Square, accum_out=ss[:, i:i + 1])\
                    .then_inc(S["post_ss"], 1)
            act.wait_ge(S["post_ms"], at + 1)
            nc.scalar.activation(rt, ms, ACT.Sqrt).then_inc(S["post_rt"], 1)

        def post_dve(dve, chain, n, src, load):
            at = POSTS.index(n)
            dve.wait_ge(S["post_ss"], NT * (at + 1))
            nc.vector.tensor_scalar(ms, ss, 1.0 / D, EPS, ALU.mult, ALU.add).then_inc(S["post_ms"], 1)
            dve.wait_ge(S["g_in"], 16 * load)
            dve.wait_ge(S["post_rt"], at + 1)
            link(dve, chain, nc.vector.reciprocal(rstd, rt))
            for i in range(NT):
                link(dve, chain, nc.vector.scalar_tensor_tensor(out=ptmp[:, i % 2, :], in0=src(i), scalar=rstd[:, i:i + 1],
                                                                in1=grow[:, :], op0=ALU.mult, op1=ALU.mult))
                nc.vector.tensor_tensor(X[:, i, :], X[:, i, :], ptmp[:, i % 2, :], ALU.add).then_inc(S["post_x"], 1)

        UNITS = [(i, kind, pr) for i in range(NT) for kind in range(3) for pr in range(4)]

        @block.tensor
        def _(pe):
            used = S["w_used"]
            pe.wait_ge(S["small_in"], 32)
            pe.wait_ge(S["norm_xn"], 1 * NT)
            tr_pe(pe, "n1", xn, NT, ND)
            tr_wait(pe, "n1")
            for m in range(8):
                arrived(pe, W_PROJ_FM + m)
                for k in range(ND):
                    last = nc.tensor.matmul(pb[:, m, :], tile(W_PROJ_FM + m)[:, k * P:(k + 1) * P], hT[:, k, :],
                                            start=(k == 0), stop=(k == ND - 1))
                last.then_inc(used, 1)
            pe.wait_ge(S["proj_fm_ev"], 4)
            for k in range(ND):
                n = W_PROJ_MLA + k // 2
                arrived(pe, n)
                for i in range(NT):
                    last = nc.tensor.matmul(pb[:, i, 0:416], hT[:, k, i * P:(i + 1) * P],
                                            tile(n)[:, (k % 2) * 416:(k % 2 + 1) * 416], start=(k == 0), stop=(k == ND - 1))
                if k % 2:
                    last.then_inc(used, 1)
            pe.wait_ge(S["proj_fm_ev"], 8)
            for k in range(ND):
                n = W_PROJ_V + k // 3
                arrived(pe, n)
                for i in range(NT):
                    last = nc.tensor.matmul(pb[:, 4 + i, 0:280], hT[:, k, i * P:(i + 1) * P],
                                            tile(n)[:, (k % 3) * 280:(k % 3 + 1) * 280], start=(k == 0), stop=(k == ND - 1))
                if k % 3 == 2 or k == ND - 1:
                    last.then_inc(used, 1)
            pe.wait_ge(S["cmp_blocks"], 4)
            pe.wait_ge(S["proj_mla_ev"], NT)
            for w in range(2):
                for half in range(2):
                    n = W_CMP + 2 * w + half
                    arrived(pe, n)
                    for l in range(16 * half, 16 * half + 16):
                        for g in range(2):
                            last = nc.tensor.matmul(pb[g * 64:g * 64 + 64, w, 0:31],
                                                    tile(n)[g * 64:g * 64 + 64, (l % 16) * 64:(l % 16 + 1) * 64],
                                                    kb[g * 64:g * 64 + 64, w, l, :], start=(l == 0), stop=(l == 31))
                    last.then_inc(used, 1)
            pe.wait_ge(S["cmp_gelu"], 5)
            for g in range(2):
                r = slice(g * 64, g * 64 + 64)
                nc.tensor.matmul(pb[r, 2, 0:31], col("w2k", 0, 64)[r, :], gk[r, 0:31], start=True, stop=True)
                last = nc.tensor.matmul(pb[:, 3 * (1 - g), 0:64], gv4[r, :], col("w2v", 0, 64)[r, :], start=True, stop=True)
            last.then_inc(S["cmp_kv"], 1)
            pe.wait_ge(S["proj_v_ev"], 2)
            pe.wait_ge(S["mla_norm"], 1)
            for b in range(3):
                for i in range(NT):
                    last = nc.tensor.transpose(pb[:, 4 + b, i * P:(i + 1) * P], chat[:, i, b * P:(b + 1) * P], ident)
                last.then_inc(S["mla_tr"], 1)
            pe.wait_ge(S["mla_tr_ev"], 3)
            pe.wait_ge(S["cmp_ready"], 1)
            for n in (W_UQ, W_UQ + 1, W_UKV):
                arrived(pe, n)
            for i in range(NT):
                if i:
                    pe.wait_ge(S["q_ev"], i)
                    pe.wait_ge(S["kv_ev"], i)
                for h in range(2):
                    for k in range(2):
                        nc.tensor.matmul(pb[:, h, 0:384], cqT[:, k, i * P:(i + 1) * P],
                                         tile(W_UQ + k)[:, h * 384:(h + 1) * 384], start=(k == 0), stop=(k == 1))
                for h in range(2):
                    last = nc.tensor.matmul(pb[:, 2 + h, :], cqT[:, 2, i * P:(i + 1) * P],
                                            tile(W_UKV)[:, h * 512:(h + 1) * 512], start=True, stop=True)
                last.then_inc(S["mla_up"], 1)
                pe.wait_ge(S["q_ev"], i + 1)
                pe.wait_ge(S["kv_ev"], i + 1)
                if i:
                    pe.wait_ge(S["qk_ev_act"], 2 * i)
                    pe.wait_ge(S["qk_ev_dve"], 2 * i)
                for w in range(2):
                    for b in range(2):
                        for h in range(4):
                            last = nc.tensor.transpose(pb[0:QK, 4 + 2 * w + b, h * P:(h + 1) * P],
                                                       qkt[:, i % 2, w, (4 * b + h) * QK:(4 * b + h + 1) * QK], ident)
                        last.then_inc(S["qk_tr"], 1)
            pe.wait_ge(S["qk_ev_act"], 2 * NT)
            pe.wait_ge(S["qk_ev_dve"], 2 * NT)
            pe.wait_ge(S["cmp_ready"], 1)
            for i in range(NT):
                for h in range(HEADS):
                    r = slice((h // 4) * 64, (h // 4) * 64 + 64)
                    last = nc.tensor.matmul(pb[:, 4 * (h // 4) + i, (h % 4) * 32:(h % 4) * 32 + 31], qT[r, h % 4, i * P:(i + 1) * P], kcT[r, 0:31],
                                            start=True, stop=True)
                if i == 0:
                    last.then_inc(used, 3)
            last.then_inc(S["cs_mm"], 1)
            pe.wait_ge(S["cs_exp"], 1)
            for i in range(NT):
                for g in range(2):
                    last = nc.tensor.transpose(pb[:, 4 + i, g * P:(g + 1) * P],
                                               Pc[:, i, 4 * g:4 * g + 4, :].rearrange("p h j -> p (h j)"), ident)
            last.then_inc(S["cs_tr"], 1)
            pe.wait_ge(S["cs_tr_ev"], 1)
            for i in range(NT):
                for g in range(2):
                    last = nc.tensor.matmul(pb[:, i, g * 256:(g + 1) * 256], PcT[:, i, g * P:(g + 1) * P], Vbd[:, g, :],
                                            start=True, stop=True)
            last.then_inc(S["cs_pv"], 1)

            pe.wait_ge(S["cs_o"], 1)

            def scores(u):
                i, kind, pr = UNITS[u]
                nk = (i + 1) * P
                if u >= 2:
                    pe.wait_ge(S["at_exp"], 2 * (u - 1))
                for hh in range(2):
                    h = 2 * pr + hh
                    dst = pb[:, 2 * (u % 2) + hh, 0:nk]
                    if kind == 2:
                        last = nc.tensor.matmul(dst, qTm[0:QK, h, i * P:(i + 1) * P], kTm[0:QK, h, 0:nk], start=True, stop=True)
                    else:
                        r = slice((h // 4) * 64, (h // 4) * 64 + 64)
                        last = nc.tensor.matmul(dst, qT[r, h % 4, i * P:(i + 1) * P], kvT[r, 2 + kind, 0:nk], start=True, stop=True)
                last.then_inc(S["at_s"], 1)

            def turn_probs(u):
                i, kind, pr = UNITS[u]
                for hh in range(2):
                    pe.wait_ge(S["at_exp"], 2 * u + hh + 1)
                    if u:
                        pe.wait_ge(S["at_ev_dve"] if hh == 0 else S["at_ev_act"], u)
                    for kt in range(i + 1):
                        last = nc.tensor.transpose(pb[:, 4 + hh, kt * P:(kt + 1) * P], Pr[:, u % 2, hh, kt * P:(kt + 1) * P], ident)
                    last.then_inc(S["at_tr"], 1)

            def values(u):
                i, kind, pr = UNITS[u]
                w = u // 4
                if pr == 0 and w >= 2:
                    pe.wait_ge(S["at_o"], w - 1)
                for hh in range(2):
                    h = 2 * pr + hh
                    pe.wait_ge(S["at_ev_dve"] if hh == 0 else S["at_ev_act"], u + 1)
                    for kt in range(i + 1):
                        v = Vm[:, kt, h * DH:(h + 1) * DH] if kind == 2 else \
                            Vsw[:, kt, kind * P + (h // 4) * DH:kind * P + (h // 4) * DH + DH]
                        last = nc.tensor.matmul(pb[:, 6 + w % 2, h * DH:(h + 1) * DH], PTs[:, u % 2, hh, kt * P:(kt + 1) * P], v,
                                                start=(kt == 0), stop=(kt == i))
                    last.then_inc(S["at_pv"], 1)

            scores(0)
            for u in range(len(UNITS)):
                if u + 1 < len(UNITS):
                    scores(u + 1)
                turn_probs(u)
                if u:
                    values(u - 1)
            values(len(UNITS) - 1)
            pe.wait_ge(S["at_o"], 12)
            tr_pe(pe, "o_nsa", O_nsa, NT, 4)
            tr_pe(pe, "o_mla", O_mla, NT, 4, bank0=4)
            tr_wait(pe, "o_nsa")
            tr_wait(pe, "o_mla")
            for m in range(ND):
                n = W_MERGE + 3 * m
                b = 4 * (m % 2)
                if m >= 2:
                    pe.wait_ge(S["mg_ev"], m - 1)
                for w in range(2):
                    arrived(pe, n + w)
                    for k in range(ND):
                        last = nc.tensor.matmul(pb[:, b + w, :], tile(n + w)[:, k * P:(k + 1) * P], hT[:, k, :],
                                                start=(k == 0), stop=(k == ND - 1))
                    last.then_inc(used, 1)
                arrived(pe, n + 2)
                for w, src in ((0, oTn), (1, oTm)):
                    for k in range(4):
                        last = nc.tensor.matmul(pb[:, b + 2 + w, :], tile(n + 2)[:, (4 * w + k) * P:(4 * w + k + 1) * P],
                                                src[:, k, :], start=(k == 0), stop=(k == 3))
                last.then_inc(used, 1)
            pe.wait_ge(S["mg_ev"], ND)
            tokens_pe(pe, W_O, ND, mT, S["post_mm"])
            pe.wait_ge(S["norm_xn"], 2 * NT)
            tr_pe(pe, "n2", xn, NT, ND)
            tr_wait(pe, "n2")
            for j in range(NF):
                if j >= 4:
                    pe.wait_ge(S["up_dve"], 2 * (j - 3))
                for w in range(2):
                    n = W_UP + 2 * j + w
                    arrived(pe, n)
                    for k in range(ND):
                        last = nc.tensor.matmul(pb[:, 2 * (j % 4) + w, :], tile(n)[:, k * P:(k + 1) * P], hT[:, k, :],
                                                start=(k == 0), stop=(k == ND - 1))
                    last.then_inc(used, 1)
            pe.wait_ge(S["up_g"], NF)
            tokens_pe(pe, W_DOWN, NF, gT, S["post_mm"])
            pe.wait_ge(S["post_x"], 2 * NT)
            pe.wait_ge(S["p_in"], 16)
            tokens_pe(pe, W_PLE, 2, pTs, S["ple_mm"])
            pe.wait_ge(S["ple_ev"], NT)
            tr_pe(pe, "x2", X, NT, ND)
            tr_wait(pe, "x2")
            tokens_pe(pe, W_PGATE, ND, hT, S["pg_mm"])
            second_pe(pe)

        @block.scalar
        def _(act):
            for i in range(NT):
                act.dma_start(X[:, i, :], x[i * P:(i + 1) * P, :]).then_inc(S["x_in"], 16)
            norm_act(act, "n1", S["x_in"], 16 * NT)
            act.wait_ge(S["small_in"], 32)
            tr_act(act, "n1", hT, ND, "g_pre_mix")
            for m in range(8):
                act.wait_ge(S["w_used"], W_PROJ_FM + m + 1)
                dst = qT[:, m, :] if m < 4 else kvT[:, m - 4, :]
                nc.scalar.activation(dst, pb[:, m, :], ACT.Copy, scale=DH ** -0.5 if m < 4 else 1.0)\
                    .then_inc(S["proj_fm_ev"], 1)
            for i in range(NT):
                act.wait_ge(S["w_used"], W_PROJ_V)
                nc.scalar.activation(cqkv[:, i, :], pb[:, i, 0:416], ACT.Copy).then_inc(S["proj_mla_ev"], 1)
            act.wait_ge(S["w_used"], W_CMP)
            nc.scalar.activation(Vsw[:, :, :], pb[:, 4:8, 0:256], ACT.Copy).then_inc(S["proj_v_ev"], 1)
            nc.scalar.activation(gates[:, :, :], pb[:, 4:8, 256:280], ACT.Sigmoid).then_inc(S["proj_v_ev"], 1)
            act.wait_ge(S["ang_ready"], 1)
            nc.scalar.activation(ropet[:, 0:128], ropet[:, 128:256], ACT.Sin).then_inc(S["sin_ready"], 1)
            act.wait_ge(S["mla_ms"], 1)
            nc.scalar.activation(mrt, mss, ACT.Sqrt).then_inc(S["mla_rt"], 1)
            act.wait_ge(S["w_used"], W_CMP + 2)
            nc.scalar.activation(gk[:, 0:31], pb[:, 0, 0:31], ACT.Gelu_apprx_tanh, bias=col("b1k")).then_inc(S["cmp_gelu"], 1)
            act.wait_ge(S["w_used"], W_CMP + 4)
            act.wait_ge(S["cmp_blocks"], 5)
            for q in range(4):
                nc.scalar.activation(gv4[:, 32 * q:32 * q + 31], pb[:, 1, 0:31], ACT.Gelu_apprx_tanh, bias=col("b1v"))\
                    .then_inc(S["cmp_gelu"], 1)
            for b in range(3):
                act.wait_ge(S["mla_tr"], b + 1)
                nc.scalar.activation(cqT[:, b, :], pb[:, 4 + b, :], ACT.Copy,
                                     scale=col("g_q", b) if b < 2 else col("g_kv")).then_inc(S["mla_tr_ev"], 1)
            for i in range(NT):
                act.wait_ge(S["mla_up"], i + 1)
                if i >= 2:
                    act.wait_ge(S["qk_tr"], 4 * (i - 1))
                nc.scalar.activation(qkt[:, i % 2, 0, :].rearrange("p (b c) -> p b c", b=2), pb[:, 0:2, 0:384], ACT.Copy,
                                     scale=QK_SCALE).then_inc(S["q_raw"], 1)
                for w, dst in ((0, qTm), (1, kTm)):
                    act.wait_ge(S["qk_tr"], 4 * i + 2 * w + 2)
                    nc.scalar.activation(dst[0:QK, 4:8, i * P:(i + 1) * P],
                                         pb[0:QK, 5 + 2 * w, :].rearrange("p (h c) -> p h c", h=4), ACT.Copy)\
                        .then_inc(S["qk_ev_act"], 1)
            act.wait_ge(S["cs_max"], 1)
            nc.scalar.activation(Pc[:, :, :, 0:31], Pc[:, :, :, 0:31], ACT.Exp).then_inc(S["cs_exp"], 1)

            def exps(u):
                i, kind, pr = UNITS[u]
                nk = (i + 1) * P
                act.wait_ge(S["at_max"], u + 1)
                for hh in range(2):
                    if u >= 2:
                        act.wait_ge(S["at_tr"], 2 * (u - 2) + hh + 1)
                    nc.scalar.activation(Pr[:, u % 2, hh, 0:nk], pb[:, 2 * (u % 2) + hh, 0:nk], ACT.Exp,
                                         bias=nm[:, u % 2, hh:hh + 1],
                                         accum_out=sums[:, u // 4, 2 * pr + hh:2 * pr + hh + 1]).then_inc(S["at_exp"], 1)

            def copy_turned(u):
                nk = (UNITS[u][0] + 1) * P
                act.wait_ge(S["at_tr"], 2 * u + 2)
                if u >= 2:
                    act.wait_ge(S["at_pv"], 2 * (u - 2) + 2)
                nc.scalar.activation(PTs[:, u % 2, 1, 0:nk], pb[:, 5, 0:nk], ACT.Copy).then_inc(S["at_ev_act"], 1)

            for u in range(len(UNITS)):
                exps(u)
                if u:
                    copy_turned(u - 1)
            copy_turned(len(UNITS) - 1)
            tr_act(act, "o_nsa", oTn, 4)
            tr_act(act, "o_mla", oTm, 4, bank0=4)
            for m in range(ND):
                b = 4 * (m % 2)
                for w in range(2):
                    act.wait_ge(S["w_used"], W_MERGE + 3 * m + w + 1)
                    if m >= 2:
                        act.wait_ge(S["mg_ev"], m - 1)
                    nc.scalar.activation(mgt[:, m % 2, w, :], pb[:, b + w, :], ACT.Sigmoid).then_inc(S["mg_sig"], 1)
            post_act(act, "p1", pair, W_UP - 1)
            norm_act(act, "n2", S["post_x"], 1 * NT)
            tr_act(act, "n2", hT, ND, "g_pre_ffn")

            def conv_last(j, w):
                m = w * NF + j
                act.wait_ge(S["w_used"], W_UP + 2 * j + w + 1)
                if j >= 2:
                    act.wait_ge(S["up_g"], j - 1)
                nc.scalar.activation(cva[:, j % 2, w, :], pb[:, 2 * (j % 4) + w, :], ACT.Identity,
                                     scale=col("w_conv", 2 * 2 * NF + m), bias=col("b_conv", m)).then_inc(S["up_conv"], 1)

            for j in range(NF):
                for w in range(2):
                    conv_last(j, w)
                act.wait_ge(S["up_dve"], 2 * j + 1)
                nc.scalar.activation(ga[:, j % 2, :], cva[:, j % 2, 0, :], ACT.Gelu_apprx_tanh).then_inc(S["up_gelu"], 1)
            post_act(act, "p2", pair, W_PLE - 1)
            for i in range(NT):
                product(act, S["ple_mm"], 0, i, W_PGATE - 1)
                nc.scalar.activation(E[:, i, :], pair(i), ACT.Copy).then_inc(S["ple_ev"], 1)
            tr_act(act, "x2", hT, ND)
            for i in range(NT):
                product(act, S["pg_mm"], 0, i, W_IN2 - 1)
                nc.scalar.activation(Gs[:, i, :], pair(i), ACT.Sigmoid).then_inc(S["pg_sig"], 1)
            post_act(act, "p3", lambda i: E[:, i, :])
            second_act(act)

        @block.vector
        def _(dve):
            chain = [0]

            def L(ins):
                link(dve, chain, ins)

            norm_dve(dve, chain, "n1")
            dve.wait_ge(S["small_in"], 32)
            tr_dve(dve, "n1", hT, ND, "g_pre_mix")
            dve.wait_ge(S["pos_in"], 16)
            posf = ropet[:, 256:260]
            ang = ropet[:, 264:328]
            turns = ropet[:, 328:392]
            red = ropet[:, 128:192]
            redc = ropet[:, 192:256]
            L(nc.vector.tensor_copy(posf, posi[:, :]))
            L(nc.vector.tensor_tensor(ang.rearrange("p (i f) -> p i f", i=NT), posf.unsqueeze(2).broadcast_to([P, NT, 16]),
                                      cs("inv_freq").unsqueeze(1).broadcast_to([P, NT, 16]), ALU.mult))
            reduce_angle(L, nc, ang, turns, red)
            L(nc.vector.tensor_scalar(red, red, PI_LOW, -PI_LOW, ALU.min, ALU.max))
            L(nc.vector.scalar_tensor_tensor(out=redc, in0=red, scalar=-1.0, in1=red, op0=ALU.mult, op1=ALU.max))
            nc.vector.tensor_scalar(redc, redc, -1.0, PI_HALF, ALU.mult, ALU.add).then_inc(S["ang_ready"], 1)
            dve.wait_ge(S["proj_fm_ev"], 6)
            for w in range(2):
                src = kvT[:, w, :].rearrange("p (b l) -> p l b", l=16)
                for half in range(2):
                    nc.vector.tensor_tensor(
                        kb[:, w, 16 * half:16 * half + 16, :], src[:, :, half:half + 31],
                        col("pos_k" if w == 0 else "pos_v", 16 * half, 16).unsqueeze(2).broadcast_to([P, 16, 31]), ALU.add)\
                        .then_inc(S["cmp_blocks"], 1)
            nc.vector.memset(gv4, 0.0).then_inc(S["cmp_blocks"], 1)
            nc.vector.memset(ar(26304, 512), 0.0)
            dve.wait_ge(S["proj_mla_ev"], NT)
            L(nc.vector.tensor_tensor(chat[:, :, :], cqkv[:, :, 0:384], cqkv[:, :, 0:384], ALU.mult))
            L(nc.vector.tensor_reduce(mrs[:, 0:4], chat[:, :, 0:256], AX.X, ALU.add))
            L(nc.vector.tensor_reduce(mrs[:, 4:8], chat[:, :, 256:384], AX.X, ALU.add))
            nc.vector.tensor_scalar(mss[:, 0:4], mrs[:, 0:4], 1.0 / 256, EPS, ALU.mult, ALU.add)
            nc.vector.tensor_scalar(mss[:, 4:8], mrs[:, 4:8], 1.0 / 128, EPS, ALU.mult, ALU.add).then_inc(S["mla_ms"], 1)
            dve.wait_ge(S["mla_rt"], 1)
            L(nc.vector.reciprocal(mrs, mrt))
            nc.vector.tensor_tensor(chat[:, :, 0:256], cqkv[:, :, 0:256], mrs[:, 0:4].unsqueeze(2).broadcast_to([P, NT, 256]), ALU.mult)
            nc.vector.tensor_tensor(chat[:, :, 256:384], cqkv[:, :, 256:384], mrs[:, 4:8].unsqueeze(2).broadcast_to([P, NT, 128]), ALU.mult)\
                .then_inc(S["mla_norm"], 1)
            dve.wait_ge(S["sin_ready"], 1)
            sin, cos = ropet[:, 0:64], ropet[:, 64:128]

            def by_tile(t):
                return t.rearrange("p (i f) -> p i f", i=NT)

            krr = ropet[:, 520:648].rearrange("p (i c) -> p i c", i=NT)
            r1, r2 = ropet[:, 648:712], ropet[:, 712:776]
            x1, x2 = cqkv[:, :, 384:400], cqkv[:, :, 400:416]
            L(nc.vector.tensor_tensor(by_tile(r1), x1, by_tile(cos), ALU.mult))
            L(nc.vector.tensor_tensor(by_tile(r2), x2, by_tile(sin), ALU.mult))
            L(nc.vector.tensor_tensor(krr[:, :, 0:16], by_tile(r1), by_tile(r2), ALU.subtract))
            L(nc.vector.tensor_tensor(by_tile(r1), x2, by_tile(cos), ALU.mult))
            L(nc.vector.tensor_tensor(by_tile(r2), x1, by_tile(sin), ALU.mult))
            L(nc.vector.tensor_tensor(krr[:, :, 16:32], by_tile(r1), by_tile(r2), ALU.add))
            dve.wait_ge(S["cmp_kv"], 1)
            nc.vector.tensor_copy(kcT[:, 0:31], pb[:, 2, 0:31])
            for g in range(2):
                for q in range(4):
                    last = nc.vector.tensor_copy(Vbd[32 * q:32 * q + 32, g, q * DH:(q + 1) * DH],
                                                 pb[32 * q:32 * q + 32, 3 * (1 - g), 0:64])
            last.then_inc(S["cmp_ready"], 1)
            q1, q2, q3, q4 = [t.rearrange("p (h c) -> p h c", h=HEADS)
                              for t in (ropet[:, 776:904], ropet[:, 264:392], ropet[:, 392:520], ropet[:, 128:256])]
            for i in range(NT):
                dve.wait_ge(S["mla_up"], i + 1)
                if i >= 2:
                    dve.wait_ge(S["qk_tr"], 4 * (i - 1))
                kvv = pb[:, 2:4, :].rearrange("p b (h c) -> p (b h) c", c=P)
                qd = qkt[:, i % 2, 0, :].rearrange("p (h c) -> p h c", c=QK)
                kd = qkt[:, i % 2, 1, :].rearrange("p (h c) -> p h c", c=QK)
                nc.vector.tensor_copy(kd[:, :, 64:96], krr[:, i, :].unsqueeze(1).broadcast_to([P, HEADS, 32]))
                nc.vector.tensor_copy(Vm[:, i, :].rearrange("p (h c) -> p h c", c=DH), kvv[:, :, 64:128])
                nc.vector.tensor_copy(kd[:, :, 0:64], kvv[:, :, 0:64]).then_inc(S["kv_ev"], 1)
                dve.wait_ge(S["q_raw"], i + 1)
                y1, y2 = qd[:, :, 64:80], qd[:, :, 80:96]
                ci = cos[:, 16 * i:16 * i + 16].unsqueeze(1).broadcast_to([P, HEADS, 16])
                si = sin[:, 16 * i:16 * i + 16].unsqueeze(1).broadcast_to([P, HEADS, 16])
                if i:
                    dve.wait_ge(S["q_ev"], i)
                nc.vector.tensor_tensor(q1, y1, ci, ALU.mult)
                nc.vector.tensor_tensor(q2, y2, si, ALU.mult)
                nc.vector.tensor_tensor(q3, y2, ci, ALU.mult)
                L(nc.vector.tensor_tensor(q4, y1, si, ALU.mult))
                nc.vector.tensor_tensor(y1, q1, q2, ALU.subtract)
                nc.vector.tensor_tensor(y2, q3, q4, ALU.add).then_inc(S["q_ev"], 1)
                for w, dst in ((0, qTm), (1, kTm)):
                    dve.wait_ge(S["qk_tr"], 4 * i + 2 * w + 1)
                    nc.vector.tensor_copy(dst[0:QK, 0:4, i * P:(i + 1) * P],
                                          pb[0:QK, 4 + 2 * w, :].rearrange("p (h c) -> p h c", h=4))\
                        .then_inc(S["qk_ev_dve"], 1)
            dve.wait_ge(S["tab_in"], 16)
            dve.wait_ge(S["cs_mm"], 1)
            L(nc.vector.memset(ar(21216, 1024), 0.0))
            for g in range(2):
                sc = pb[:, 4 * g:4 * g + 4, 0:128].rearrange("p i (h j) -> p i h j", j=32)
                ins = nc.vector.tensor_tensor(Pc[:, :, 4 * g:4 * g + 4, 0:31], sc[:, :, :, 0:31],
                                              cmpt.rearrange("p (i h j) -> p i h j", i=NT, j=31)[:, :, 4 * g:4 * g + 4, :],
                                              ALU.add)
            L(ins)
            L(nc.vector.tensor_reduce(cmaxn.rearrange("p (i h) -> p i h", i=NT), Pc[:, :, :, 0:31], AX.X, ALU.max))
            nc.vector.tensor_tensor(Pc[:, :, :, 0:31], Pc[:, :, :, 0:31],
                                    cmaxn.rearrange("p (i h) -> p i h", i=NT).unsqueeze(3).broadcast_to([P, NT, HEADS, 31]),
                                    ALU.subtract).then_inc(S["cs_max"], 1)
            dve.wait_ge(S["cs_exp"], 1)
            L(nc.vector.tensor_reduce(csum.rearrange("p (i h) -> p i h", i=NT), Pc[:, :, :, 0:31], AX.X, ALU.add))
            L(nc.vector.reciprocal(csum, csum))
            f3 = fac.rearrange("p (i h) -> p i h", i=NT)
            dve.wait_ge(S["proj_v_ev"], 2)
            L(nc.vector.tensor_tensor(f3, csum.rearrange("p (i h) -> p i h", i=NT), gates[:, :, 0:8], ALU.mult))
            L(nc.vector.tensor_scalar(fac[:, 0:8], fac[:, 0:8], cs("row_ok"), None, ALU.mult))
            dve.wait_ge(S["cs_tr"], 1)
            nc.vector.tensor_copy(PcT[:, :, :], pb[:, 4:8, 0:256]).then_inc(S["cs_tr_ev"], 1)
            dve.wait_ge(S["cs_pv"], 1)
            nc.vector.tensor_tensor(ar(17120, 2048).rearrange("p (a c) -> p a c", c=DH),
                                    pb[:, 0:4, :].rearrange("p i (h c) -> p (i h) c", c=DH),
                                    fac.unsqueeze(2).broadcast_to([P, 32, DH]), ALU.mult).then_inc(S["cs_o"], 1)
            dve.wait_ge(S["cs_o"], 1)

            alibi = cs("alibi")
            rinv = st[:, 428:436]
            otmp = junk[:, 0:512]

            def mask_max(u):
                i, kind, pr = UNITS[u]
                nk = (i + 1) * P
                b = 2 * (u % 2)
                dve.wait_ge(S["at_s"], u + 1)
                if kind == 2:
                    L(nc.vector.tensor_tensor(pb[:, b:b + 2, nk - P:nk], pb[:, b:b + 2, nk - P:nk],
                                              cs("diag").unsqueeze(1).broadcast_to([P, 2, P]), ALU.add))
                else:
                    for hh in range(2):
                        ins = nc.vector.scalar_tensor_tensor(out=pb[:, b + hh, 0:nk], in0=alibi[:, 512 - nk:512],
                                                             scalar=SLOPES[2 * pr + hh], in1=pb[:, b + hh, 0:nk],
                                                             op0=ALU.mult, op1=ALU.add)
                    L(ins)
                nc.vector.tensor_reduce(nm[:, u % 2, :], pb[:, b:b + 2, 0:nk], AX.X, ALU.max, negate=True)\
                    .then_inc(S["at_max"], 1)

            def copy_turned(u):
                nk = (UNITS[u][0] + 1) * P
                dve.wait_ge(S["at_tr"], 2 * u + 1)
                if u >= 2:
                    dve.wait_ge(S["at_pv"], 2 * (u - 2) + 1)
                nc.vector.tensor_copy(PTs[:, u % 2, 0, 0:nk], pb[:, 4, 0:nk]).then_inc(S["at_ev_dve"], 1)

            def combine(w):
                i, kind = w // 3, w % 3
                dve.wait_ge(S["at_pv"], 8 * (w + 1))
                L(nc.vector.reciprocal(rinv, sums[:, w, :]))
                if kind < 2:
                    L(nc.vector.tensor_tensor(rinv, rinv, gates[:, i, 8 * (kind + 1):8 * (kind + 2)], ALU.mult))
                dst = O_mla[:, i, :] if kind == 2 else otmp
                ins = nc.vector.tensor_tensor(dst.rearrange("p (h c) -> p h c", c=DH),
                                              pb[:, 6 + w % 2, :].rearrange("p (h c) -> p h c", c=DH),
                                              rinv.unsqueeze(2).broadcast_to([P, HEADS, DH]), ALU.mult)
                if kind < 2:
                    L(ins)
                    ins = nc.vector.tensor_tensor(O_nsa[:, i, :], O_nsa[:, i, :], otmp, ALU.add)
                ins.then_inc(S["at_o"], 1)
                dve.wait_ge(S["at_o"], w + 1)

            for u in range(len(UNITS)):
                mask_max(u)
                if u:
                    copy_turned(u - 1)
                if u % 4 == 1 and u >= 5:
                    combine((u - 5) // 4)
            copy_turned(len(UNITS) - 1)
            combine(11)
            tr_dve(dve, "o_nsa", oTn, 4)
            tr_dve(dve, "o_mla", oTm, 4, bank0=4)
            for m in range(ND):
                b = 4 * (m % 2)
                dve.wait_ge(S["mg_sig"], 2 * m + 2)
                dve.wait_ge(S["w_used"], W_MERGE + 3 * m + 3)
                for w in range(2):
                    ins = nc.vector.tensor_tensor(mgt[:, m % 2, 2 + w, :], mgt[:, m % 2, w, :], pb[:, b + 2 + w, :], ALU.mult)
                L(ins)
                nc.vector.tensor_tensor(mT[:, m, :], mgt[:, m % 2, 2, :], mgt[:, m % 2, 3, :], ALU.add).then_inc(S["mg_ev"], 1)
            post_dve(dve, chain, "p1", pair, 1)
            dve.wait_ge(S["post_x"], 1 * NT)
            norm_dve(dve, chain, "n2")
            tr_dve(dve, "n2", hT, ND, "g_pre_ffn")
            for j in range(NF):
                for w in range(2):
                    m = w * NF + j
                    dve.wait_ge(S["up_conv"], 2 * j + w + 1)
                    c = cva[:, j % 2, w, :]
                    u = pb[:, 2 * (j % 4) + w, :]
                    L(nc.vector.scalar_tensor_tensor(out=c[:, 1:T], in0=u[:, 0:T - 1], scalar=col("w_conv", 2 * NF + m),
                                                     in1=c[:, 1:T], op0=ALU.mult, op1=ALU.add))
                    nc.vector.scalar_tensor_tensor(out=c[:, 2:T], in0=u[:, 0:T - 2], scalar=col("w_conv", m),
                                                   in1=c[:, 2:T], op0=ALU.mult, op1=ALU.add).then_inc(S["up_dve"], 1)
                dve.wait_ge(S["up_dve"], 2 * j + 2)
                dve.wait_ge(S["up_gelu"], j + 1)
                nc.vector.tensor_tensor(gT[:, j, :], ga[:, j % 2, :], cva[:, j % 2, 1, :], ALU.mult).then_inc(S["up_g"], 1)
            post_dve(dve, chain, "p2", pair, 2)
            dve.wait_ge(S["post_x"], 2 * NT)
            tr_dve(dve, "x2", hT, ND)
            for i in range(NT):
                dve.wait_ge(S["pg_sig"], i + 1)
                nc.vector.tensor_tensor(E[:, i, :], E[:, i, :], Gs[:, i, :], ALU.mult).then_inc(S["p3_prod"], 1)
            dve.wait_ge(S["p3_prod"], NT)
            post_dve(dve, chain, "p3", lambda i: E[:, i, :], 3)
            dve.wait_ge(S["post_x"], 3 * NT)
            second_dve(dve, chain)



TWO_PI = 6.283185307179586
PI_HALF = 1.5707963267948966
TWO_PI_A = 6.28125
TWO_PI_B = float(np.float32(np.round((TWO_PI - 6.28125) * 2.0 ** 21) / 2.0 ** 21))
TWO_PI_C = TWO_PI - TWO_PI_A - TWO_PI_B
ROUND = 12582912.0


def reduce_angle(L, nc, ang, turns, red):
    L(nc.vector.tensor_scalar(turns, ang, 1.0 / TWO_PI, ROUND, ALU.mult, ALU.add))
    L(nc.vector.tensor_scalar(turns, turns, ROUND, None, ALU.subtract))
    L(nc.vector.scalar_tensor_tensor(out=red, in0=turns, scalar=-TWO_PI_A, in1=ang, op0=ALU.mult, op1=ALU.add))
    L(nc.vector.scalar_tensor_tensor(out=red, in0=turns, scalar=-TWO_PI_B, in1=red, op0=ALU.mult, op1=ALU.add))
    L(nc.vector.scalar_tensor_tensor(out=red, in0=turns, scalar=-TWO_PI_C, in1=red, op0=ALU.mult, op1=ALU.add))


PI_LOW = 3.1415925025939941


def constants():
    f32 = np.float32
    p = np.arange(P)
    c = {"ident": np.eye(P), "ones": np.ones((P, P)), "diag": np.where(p[None, :] <= p[:, None], 0.0, NEG)}
    dist = p[:, None] - (np.arange(512)[None, :] - 384)
    c["alibi"] = np.where(dist >= 0, -dist, NEG)
    inv = (np.float32(10000.0) ** (-np.arange(0, 32, 2, dtype=f32) / f32(32))).astype(f32)
    c["inv_freq"] = np.broadcast_to(inv, (P, 16))
    c["row_ok"] = (p >= 31)[:, None]
    a = 2 * np.pi * np.outer(np.arange(64), np.arange(64)) / 64
    z = np.zeros((64, 64))
    c["dft64"] = np.block([[np.cos(a), z, -np.sin(a), z], [z, np.cos(a), z, -np.sin(a)]])
    c["giota"] = np.broadcast_to(np.arange(4), (P, 4))
    c["eiota"] = np.broadcast_to(np.arange(32), (P, 32))
    c["tri"] = p[:, None] < p[None, :]
    c["choice"] = p[:, None] + P * np.arange(2 * NT)[None, :]
    csts = np.concatenate([c[n].astype(f32) for n, _ in CSTS], axis=1)
    t = np.arange(T).reshape(NT, P).T
    dist = t[:, :, None] - (np.arange(N_CMP) * 16 + 31)[None, None, :]
    slopes = np.array(SLOPES)
    tab = np.where(dist[:, :, None, :] >= 0, -slopes[None, None, :, None] * dist[:, :, None, :], NEG)
    return csts, tab.astype(f32).reshape(P, -1)


def transforms():
    n = np.arange(T)
    a = 2 * np.pi * (np.outer(n, n) % (2 * T)) / (2 * T)
    C, Sn, alt = np.cos(a), np.sin(a), (-1.0) ** n

    def blocks(c, s, m):
        cols = slice(m * P, (m + 1) * P)
        return np.concatenate([by_rows(c[:, cols]), by_rows(s[:, cols])], axis=1).astype(np.float32)

    Cn, Sa = C.copy(), Sn.copy()
    Cn[:, 0] = alt
    Sa[:, 0] = alt
    forward = [blocks(Cn, Sa, 0)] + [blocks(C, Sn, m) for m in range(4)]
    Ci, Si = C.copy(), Sn.copy()
    Ci[0, :] = 0.5
    Si[0, :] = 0.5 * alt
    inverse = [blocks(Ci, Si, i) for i in range(NT)]
    b = 2 * np.pi * (np.outer(n, n) % T) / T
    scale = 1.0 / np.sqrt(64.0 * T)
    time = [blocks(np.cos(b) * scale, np.sin(b) * scale, i) for i in range(NT)]
    return (W_DFT, forward), (W_IDFT, inverse), (W_FFT, time)


def filter_tables():
    f32 = np.float32
    t = np.linspace(0.0, 1.0, T, dtype=f32)[:, None]
    w = (f32(2.0 * np.pi / T) * np.arange(T, dtype=f32))[:, None]
    f = np.linspace(1e-4, 15, 16, dtype=f32)[None, :]
    z = np.concatenate([t, np.cos(f * w), -np.sin(f * w)], axis=-1)
    deltas = np.abs(np.linspace(np.log(1e-2) / 1.5, np.log(1e-2) / 0.3, CH, dtype=f32))
    zp = np.zeros((P, T), f32)
    zp[:33] = z.T
    return zp, by_rows(np.exp(-t * deltas).astype(f32)).reshape(P, -1)


def by_rows(w):
    return w.reshape(-1, P, w.shape[-1]).transpose(1, 0, 2)


def pack(tiles, dest, at, m):
    flat = tiles.reshape(P, -1)
    dest[at + m, :, :flat.shape[1]] = flat


def kernel(**a):
    import concourse.bacc as bacc
    from concourse.bass_utils import run_bass_kernel_spmd

    a = {k: np.asarray(v) for k, v in a.items()}
    f32 = np.float32
    W = np.zeros((N_TILES, P, 1024), f32)
    w_in = a["w_in"][0]
    put = lambda tiles, at, m: pack(tiles, W, at, m)
    for m in range(4):
        cols = [*range(m * 64, m * 64 + 64), *range((m + 4) * 64, (m + 4) * 64 + 64)]
        put(by_rows(w_in[:, cols]), W_PROJ_FM, m)
    for m, part in enumerate((0, 1, 2, 4)):
        put(by_rows(w_in[:, 512 + part * 128:512 + part * 128 + 128]), W_PROJ_FM, 4 + m)
    mla = by_rows(w_in[:, 1304:1720])
    for m in range(4):
        put(mla[:, 2 * m:2 * m + 2], W_PROJ_MLA, m)
    vv = by_rows(np.concatenate([w_in[:, 896:1024], w_in[:, 1152:1304]], axis=1))
    for m in range(3):
        put(vv[:, 3 * m:3 * m + 3], W_PROJ_V, m)
    for w, name in enumerate(("nsa_ck_w1", "nsa_cv_w1")):
        w1 = a[name][0].reshape(32, 64, 64).transpose(1, 0, 2)
        w1 = np.concatenate([w1, w1], axis=0)
        for half in range(2):
            put(w1[:, 16 * half:16 * half + 16], W_CMP, 2 * w + half)
    uq = by_rows(a["mla_w_uq"][0])
    put(uq[:, 0], W_UQ, 0)
    put(uq[:, 1], W_UQ, 1)
    put(a["mla_w_ukv"][0], W_UKV, 0)
    for m in range(ND):
        s = slice(m * P, m * P + P)
        put(by_rows(w_in[:, 1720:2744][:, s]), W_MERGE, 3 * m)
        put(by_rows(w_in[:, 2744:3768][:, s]), W_MERGE, 3 * m + 1)
        put(np.concatenate([by_rows(a["w_br_nsa"][0][:, s]), by_rows(a["w_br_mla"][0][:, s])], axis=1), W_MERGE, 3 * m + 2)
    for name, at in (("w_o", W_O), ("w_down", W_DOWN), ("w_ple", W_PLE), ("w_ple_gate", W_PGATE), ("w_out_2", W_OUT2)):
        w = by_rows(a[name][0])
        for k in range(w.shape[1]):
            put(w[:, k], at, k)
    w_up = a["w_up"][0]
    for j in range(NF):
        for w in range(2):
            o = w * D_FF + j * P
            put(by_rows(w_up[:, o:o + P]), W_UP, 2 * j + w)
    w_in2 = a["w_in_2"][0]
    for m in range(16):
        put(by_rows(w_in2[:, m * P:(m + 1) * P]), W_IN2, m)
    for at, tiles in transforms():
        for m, t in enumerate(tiles):
            put(t, at, m)
    put(by_rows(np.concatenate([a["w_group_2"][0], a["w_router_2"][0].transpose(1, 0, 2).reshape(D, 32)], axis=1)), W_ROUTE, 0)
    experts = W[W_EXP:].reshape(N_EXP, 3, 4, P, 1024)
    for w, name in enumerate(("w_gate_2", "w_up_2")):
        experts[:, w] = a[name][0].reshape(N_EXP, 4, 2, P, 512).transpose(0, 1, 3, 2, 4).reshape(N_EXP, 4, P, 1024)
    experts[:, 2] = a["w_down_2"][0].reshape(N_EXP, 4, P, 1024)
    vec = lambda v: v.reshape(-1, P).T
    twice = lambda v: np.concatenate([v, v], axis=0)
    low = lambda v: np.concatenate([v, np.zeros((P - v.shape[0], v.shape[1]), f32)], axis=0)
    c = {"g_pre_mix": vec(a["g_pre_mix"][0]), "g_pre_ffn": vec(a["g_pre_ffn"][0]), "norm1": vec(a["norm1_g_2"][0]),
         "norm2": vec(a["norm2_g_2"][0]), "mix_g": vec(a["mix_g_2"][0]), "g_q": vec(a["mla_g_q"][0]),
         "g_kv": vec(a["mla_g_kv"][0]), "w_conv": vec(a["w_conv"][0].reshape(-1)), "b_conv": vec(a["b_conv"][0]),
         "conv_w": vec(a["conv_w_2"][0].reshape(-1)), "conv_b": vec(a["conv_b_2"][0]),
         "b1k": twice(a["nsa_ck_b1"][0][:, None]), "b1v": twice(a["nsa_cv_b1"][0][:, None]),
         "w2k": twice(a["nsa_ck_w2"][0]), "w2v": twice(a["nsa_cv_w2"][0]),
         "pos_k": twice(a["nsa_pos_k"][0].T), "pos_v": twice(a["nsa_pos_v"][0].T),
         "f_b_in": low(a["f_b_in_2"][0][:, None]), "f_freq": low(a["f_freq_2"][0].T), "f_b_mid": low(a["f_b_mid_2"][0].T),
         "f_w_in": low(a["f_w_in_2"][0]), "r_bias": np.broadcast_to(np.concatenate([a["b_group_2"][0], a["b_router_2"][0].reshape(-1)]), (P, 36)),
         "f_w_mid": low(a["f_w_mid_2"][0].transpose(1, 0, 2).reshape(64, 128))}
    cols = np.concatenate([c[n] for n, _ in COLS], axis=1)
    csts, cmp_tab = constants()
    ins = {"stream": W, "x": a["x"][0], "cols": cols, "csts": csts, "cmp_tab": cmp_tab,
           "pos": np.ascontiguousarray(a["positions"][0].reshape(NT, P).T),
           "grows": np.stack([np.broadcast_to(v, (P, D)) for v in (a["g_post_mix"][0], a["g_post_ffn"][0], a["g_ple"][0],
                                                             a["norm2_g_2"][0], a["final_g_2"])]),
           "pT": np.ascontiguousarray(by_rows(np.ascontiguousarray(a["p"][0, 0].T))).reshape(P, -1)}
    ins["fconst"], ins["decay"] = filter_tables()
    ins["fwout"] = a["f_w_out_2"][0]
    ins["frow"] = np.broadcast_to(a["f_bias_2"][0], (P, CH))
    ins["free"] = np.broadcast_to(np.arange(2 * T, 2 * T + P, dtype=np.int32)[:, None], (P, N_SLOTS // P))
    nc = bacc.Bacc("TRN2", target_bir_lowering=False, num_devices=1)
    ap = {}
    for n, v in ins.items():
        v = ins[n] = np.ascontiguousarray(v)
        ap[n] = nc.dram_tensor(n, v.shape, mybir.dt.from_np(v.dtype), kind="ExternalInput").ap()
    out = nc.dram_tensor("out", (T, D), F32, kind="ExternalOutput").ap()
    build(nc, ap["stream"], ap["x"], ap["cols"], ap["csts"], ap["cmp_tab"], ap["pos"], ap["grows"],
          ap["pT"], ap["fconst"], ap["fwout"], ap["decay"], ap["frow"], ap["free"], out)
    r = run_bass_kernel_spmd(nc, [ins], core_ids=[0])
    return r.results[0]["out"].reshape(1, T, D)
```

```python
from contextlib import ExitStack

import numpy as np
import concourse.bass as bass
from concourse import mybir

F32 = mybir.dt.float32
F32R = mybir.dt.float32r
BF16 = mybir.dt.bfloat16
I32 = mybir.dt.int32
ALU = mybir.AluOpType
ACT = mybir.ActivationFunctionType
AX = mybir.AxisListType

P = 128
T = 512
NT = T // P
D = 1024
ND = D // P
EPS = 1e-6
NEG = -1e30
HEADS = 8
DH = 64
N_CMP = (T - 32) // 16 + 1
QK = 96
QK_SCALE = float(QK) ** -0.5
D_FF = 2816
NF = D_FF // P
N_EXP = 32
CH = 512
RING = 12
N_SLOTS = N_EXP * T
EXTRA = 2 * T // P - 1
N_OVER = EXTRA + 1

W_PROJ_FM = 0
W_PROJ_MLA = W_PROJ_FM + 8
W_PROJ_V = W_PROJ_MLA + 4
W_CMP = W_PROJ_V + 3
W_UQ = W_CMP + 4
W_UKV = W_UQ + 2
W_MERGE = W_UKV + 1
W_O = W_MERGE + 24
W_UP = W_O + 8
W_DOWN = W_UP + 2 * NF
W_PLE = W_DOWN + NF
W_PGATE = W_PLE + 2
W_IN2 = W_PGATE + 8
W_DFT = W_IN2 + 16
W_IDFT = W_DFT + 5
W_FFT = W_IDFT + 4
W_OUT2 = W_FFT + 4
W_ROUTE = W_OUT2 + 8
W_EXP = W_ROUTE + 1
N_TILES = W_EXP + 12 * N_EXP
assert W_EXP % RING == 0 and N_TILES % RING == 0

SPLIT = {"proj": (W_PROJ_FM, W_CMP, 8192), "merge": (W_MERGE, 24, 17120), "w_o": (W_O, 8, 17120),
         "up": (W_UP, 2 * NF, 0), "down": (W_DOWN, NF, 0), "pgate": (W_PGATE, 8, 8192),
         "in2": (W_IN2, 16, 8192), "out2": (W_OUT2, 8, 8192)}
SPLIT_TILES = [first + m for first, count, _ in SPLIT.values() for m in range(count)]
SPLIT_ROWS = [(name, k) for name in ("w_o", "down", "pgate", "out2") for k in range(SPLIT[name][1])]

COLS = [("g_pre_mix", 8), ("g_pre_ffn", 8), ("norm1", 8), ("norm2", 8), ("mix_g", 8), ("g_q", 2), ("g_kv", 1),
        ("w_conv", 3 * 2 * NF), ("b_conv", 2 * NF), ("conv_w", 3 * 12), ("conv_b", 12), ("b1k", 1), ("b1v", 1),
        ("w2k", 64), ("w2v", 64), ("pos_k", 32), ("pos_v", 32), ("f_b_in", 1), ("f_freq", 3), ("f_b_mid", 2),
        ("f_w_in", 64), ("f_w_mid", 128), ("r_bias", 36)]
COL = {}
_at = 0
for _n, _w in COLS:
    COL[_n] = (_at, _at + _w)
    _at += _w
N_COLS = _at

CSTS = [("ident", 128), ("ones", 128), ("diag", 128), ("alibi", 512), ("inv_freq", 16), ("row_ok", 1),
        ("dft64", 256), ("giota", 4), ("eiota", 32), ("tri", 128), ("iota", 128), ("choice", 8), ("empty", 1)]
CST = {}
_at = 0
for _n, _w in CSTS:
    CST[_n] = (_at, _at + _w)
    _at += _w
N_CST = _at

SLOPES = [2.0 ** (-(h + 1)) for h in range(HEADS)]

SEMS = """p3_prod norm_ss norm_ms norm_rt norm_xn post_mm post_ss post_ms post_rt post_x turned copied_dve copied_act
w_used w_high w_low rows_low hT_low oT_low h_back small_in x_in tab_in pos_in g_in p_in decay_in out_st
dve_chain proj_fm_ev proj_mla_ev proj_v_ev cmp_blocks cmp_gelu cmp_kv cmp_ready ang_ready sin_ready mla_ms
mla_rt mla_norm mla_tr mla_tr_ev mla_up q_ev kv_ev q_raw qk_tr qk_ev_act qk_ev_dve cs_mm cs_max cs_exp cs_tr
cs_tr_ev cs_pv cs_o at_s at_max at_exp at_tr at_ev_dve at_ev_act at_pv at_o mg_sig mg_ev up_conv up_dve
up_gelu up_g ple_mm ple_ev pg_mm pg_sig in2_lin in2_conv in2_f z_ready f_in fb_in fm_mm fm_arg fm_sin fo_mm
fo_ev habs hs_mm hs_ready pm_ready kf_mm kf_ev y_ready yo_ev fd_mm fd_ev fo2_ev hn_sq hn_ms hn_rt hn_y
wo2_mm wo2_x rt_lg rt_g rt_d rt_exp rows_st xg_zero slot_ready slot_mm sel_ready rank_mm counts_out
over_ready x_tr x_ev_dve x_ev_act ex_sig ex_hid ex_mul h_tr h_ev y_ev_dve y_ev_act xg_in0 xg_in1 idx_in
at_in at_out gathers scatters y_st0 y_st1 back0 back1 back2 back3 moe_x fin_y""".split()
NORMS = ["n1", "n2", "n3", "n4", "n5"]
POSTS = ["p1", "p2", "p3"]
TURNS = {}
_at = 0
for _n, _w in (("n1", 8), ("o_nsa", 4), ("o_mla", 4), ("n2", 8), ("x2", 8), ("n3", 8), ("z", 4), ("x0", 4), ("y2", 8), ("n4", 8)):
    TURNS[_n] = (_at, _w)
    _at += _w


def build(nc, W, x, cols, csts, cmp_tab, pos, grows, pT, fconst, fwout, decay, frow, out):
    ctx = ExitStack()
    with ctx:
        def sem(name):
            return ctx.enter_context(nc.semaphore(name))

        def sb(name, shape, dt=F32):
            return ctx.enter_context(nc.sbuf_tensor(name, shape, dt))

        def two_views(name, shape):
            with nc.sbuf_tensor(name + "_r", shape, F32R) as as_rounded:
                pass
            return as_rounded, sb(name, shape)

        S = {n: sem(n) for n in SEMS}
        landed = [sem(f"w_landed{s}") for s in range(RING)]

        pb = ctx.enter_context(nc.psum_tensor("banks", [P, 8, 512], F32))
        ring = sb("ring", [P, RING, 1024])
        X = sb("resid", [P, NT, D])
        hT_r, hT = two_views("hT", [P, ND, T])
        colt = sb("colt", [P, N_COLS])
        cst = sb("cst", [P, N_CST])
        grow = sb("grow", [P, D])
        junk = sb("junk", [P, 1024])
        st = sb("st", [P, 640])
        posi = sb("posi", [P, NT], I32)
        arena_r, arena = two_views("arena", [P, 27300])
        idx = sb("idx", [P, N_SLOTS // P], I32)
        sel = sb("sel", [P, NT, N_EXP], BF16)
        tri16 = sb("tri16", [P, P], BF16)
        ones16 = sb("ones16", [P, P], BF16)
        over = sb("over", [1, 3 * N_OVER], I32)
        at_in = [sb(f"at_in{q}", [P, 1], I32) for q in range(2)]
        at_out = [sb(f"at_out{q}", [P, 1], I32) for q in range(2)]
        rows = nc.dram_tensor("rows", (2 * T, D), F32).ap()
        back = nc.dram_tensor("back", (2 * T, D), F32).ap()

        def col(name, a=0, w=1):
            o = COL[name][0] + a
            return colt[:, o:o + w]

        def cs(name):
            return cst[:, CST[name][0]:CST[name][1]]

        def ar(off, n):
            return arena[:, off:off + n]

        def ar3(off, a, b):
            return arena[:, off:off + a * b].rearrange("p (a b) -> p a b", a=a)

        ident = cs("ident")
        ss = st[:, 0:4]
        ms = st[:, 4:8]
        rt = st[:, 8:12]
        rstd = st[:, 12:16]
        sums = st[:, 16:112].rearrange("p (w h) -> p w h", w=12)
        nm = st[:, 112:116].rearrange("p (u h) -> p u h", u=2)
        fac = st[:, 116:148]
        csum = st[:, 148:180]
        cmaxn = st[:, 180:212]
        mss = st[:, 212:220]
        mrt = st[:, 220:228]
        mrs = st[:, 228:236]
        hns = st[:, 236:300]
        hnr = st[:, 300:364]
        hni = st[:, 364:428]

        xn = ar3(0, NT, D)
        qT = ar3(0, 4, T)
        kvT = ar3(2048, 4, T)
        Vsw = ar3(4096, NT, 256)
        cqkv = ar3(5120, NT, 416)
        gates = ar3(6784, NT, 24)
        qTm = ar3(6880, HEADS, T)
        kTm = ar3(10976, HEADS, T)
        Vm = ar3(15072, NT, 512)
        O_nsa = ar3(17120, NT, 512)
        O_mla = ar3(19168, NT, 512)
        cqT = ar3(17120, 3, T)
        chat = ar3(18656, NT, 384)
        Pr = ar(21216, 2048).rearrange("p (u h k) -> p u h k", u=2, h=2)
        PTs = ar(23264, 2048).rearrange("p (u h k) -> p u h k", u=2, h=2)
        qkt = ar(21216, 3072).rearrange("p (u w c) -> p u w c", u=2, w=2)
        ropet = ar(24300, 1000)
        cmpt = ar(25312, 992)
        kb = ar(21216, 1984).rearrange("p (w l j) -> p w l j", w=2, l=32)
        Pc = ar(21216, 1024).rearrange("p (i h j) -> p i h j", i=NT, h=HEADS)
        PcT = ar(22240, 1024).rearrange("p (i c) -> p i c", i=NT)
        Vbd = ar(26304, 512).rearrange("p (g c) -> p g c", g=2)
        kcT = ar(26816, 32)
        gk = ar(26848, 32)
        gv4 = ar(26880, 128)
        mT = ar3(10976, ND, T)
        mgt = ar(0, 4096).rearrange("p (u k c) -> p u k c", u=2, k=4)
        ptmp = ar3(21216, 2, 1024)
        gT = ar3(4096, NF, T)
        cva = ar(15360, 2048).rearrange("p (u k c) -> p u k c", u=2, k=2)
        ga = ar3(17408, 2, T)
        pTs = ar3(24000, 2, T)
        E = ar3(0, NT, D)
        Gs = ar3(4096, NT, D)

        def plain(ap):
            return ap.bitcast(F32)

        def ar_r(off, n):
            return arena_r[:, off:off + n]

        rows_split = ar_r(25024, 2048).rearrange("p (u w c) -> p u w c", u=2, w=2)
        up_low = ar_r(18432, ND * T).rearrange("p (k t) -> p k t", k=ND)
        h_high = ar_r(21216, ND * T).rearrange("p (k t) -> p k t", k=ND)
        nsa_high, mla_high, nsa_low, mla_low = [ar_r(off, 4 * T).rearrange("p (k t) -> p k t", k=4)
                                                for off in (6880, 8928, 4096, 15072)]
        proj_low = ar_r(12288, ND * T).rearrange("p (k t) -> p k t", k=ND)
        in2_low = ar_r(20480, ND * T).rearrange("p (k t) -> p k t", k=ND)

        def parts(name, m):
            n = SPLIT_TILES.index(SPLIT[name][0] + m)
            return ar_r(SPLIT[name][2] + 2048 * (n % 2), 2048).rearrange("p (w c) -> p w c", w=2)

        def high_act(act, name, m):
            tile_n = SPLIT[name][0] + m
            n = SPLIT_TILES.index(tile_n)
            arrived(act, tile_n)
            if n >= 2:
                act.wait_ge(S["w_used"], SPLIT_TILES[n - 2] + 1)
            nc.scalar.activation(parts(name, m)[:, 0, :], tile(tile_n), ACT.Copy).then_inc(S["w_high"], 1)

        def high_at(act, n):
            for name, (first, count, _) in SPLIT.items():
                if first <= SPLIT_TILES[n] < first + count:
                    high_act(act, name, SPLIT_TILES[n] - first)

        def low_pool(pool, name):
            for m in range(SPLIT[name][1]):
                tile_n = SPLIT[name][0] + m
                w = parts(name, m)
                pool.wait_ge(S["w_high"], SPLIT_TILES.index(tile_n) + 1)
                nc.gpsimd.tensor_tensor(w[:, 1, :], tile(tile_n), plain(w[:, 0, :]), ALU.subtract).then_inc(S["w_low"], 1)

        def split_dve(dve, chain, name, src):
            for k in range(SPLIT[name][1]):
                n = SPLIT_ROWS.index((name, k))
                if n >= 2:
                    before, at = SPLIT_ROWS[n - 2]
                    dve.wait_ge(S["w_used"], SPLIT[before][0] + at + 1)
                high, low = rows_split[:, n % 2, 0, :], rows_split[:, n % 2, 1, :]
                link(dve, chain, nc.vector.tensor_copy(high, src[:, k, :]))
                nc.vector.tensor_tensor(low, src[:, k, :], plain(high), ALU.subtract).then_inc(S["rows_low"], 1)

        def split_features(pe, name, m, bank, high, low, turn):
            w = parts(name, m)
            pe.wait_ge(S["w_low"], SPLIT_TILES.index(SPLIT[name][0] + m) + 1)
            for k in range(ND):
                if m == 0:
                    pe.wait_ge(S["hT_low"], ND * turn + k + 1)
                for part, (a, b) in enumerate(((0, high), (0, low), (1, high))):
                    last = nc.tensor.matmul(pb[:, bank, :], w[:, a, k * P:(k + 1) * P], b[:, k, :],
                                            start=(k == 0 and part == 0), stop=(k == ND - 1 and part == 2))
            last.then_inc(S["w_used"], 1)

        def split_columns(pe, k, n, q, width, bank0):
            w = parts("proj", n)
            pe.wait_ge(S["w_low"], n + 1)
            for i in range(NT):
                for part, (a, v) in enumerate(((hT_r, 0), (hT_r, 1), (proj_low, 0))):
                    last = nc.tensor.matmul(pb[:, bank0 + i, 0:width], a[:, k, i * P:(i + 1) * P],
                                            w[:, v, q * width:(q + 1) * width], start=(k == 0 and part == 0),
                                            stop=(k == ND - 1 and part == 2))
            return last

        def split_tokens(pe, name, done):
            base, K, _ = SPLIT[name]
            for k in range(K):
                w = parts(name, k)
                n = SPLIT_ROWS.index((name, k))
                a = rows_split[:, n % 2, :, :]
                pe.wait_ge(S["w_low"], SPLIT_TILES.index(base + k) + 1)
                pe.wait_ge(S["rows_low"], n + 1)
                for i in range(NT):
                    for part, (u, v) in enumerate(((0, 0), (0, 1), (1, 0))):
                        for h in range(2):
                            last = nc.tensor.matmul(pb[:, 2 * i + h, :], a[:, u, i * P:(i + 1) * P],
                                                    w[:, v, h * 512:(h + 1) * 512],
                                                    start=(k == 0 and part == 0), stop=(k == K - 1 and part == 2))
                    if k == K - 1 and i < NT - 1:
                        last.then_inc(done, 1)
                last.then_inc(S["w_used"], 1)

        def tile(n):
            return ring[:, n % RING, :]

        def arrived(pe, n):
            pe.wait_ge(landed[n % RING], 16 * (n // RING + 1))


        uc = ar3(0, 12, T)
        uF = ar3(6144, 4, T)
        zt = ar3(8192, NT, CH)
        x0t = ar3(10240, NT, CH)
        Pk = ar3(12288, NT, CH)
        Mk = ar3(14336, NT, CH)
        HF = ar3(16384, NT, CH)
        HB = ar3(18432, NT, CH)
        prod = ar3(16384, 4, CH)
        Y = ar3(16384, NT, D)
        decs = ar3(20480, NT, CH)
        absb = ar(22528, 2048).rearrange("p (u c) -> p u c", u=2)
        vCS = ar(20480, 4096).rearrange("p (i w c) -> p i w c", i=NT, w=2)
        Kt = ar(24576, 2048).rearrange("p (u w c) -> p u w c", u=2, w=2)
        Kn = ar(26624, 512)
        YA = ar3(0, 4, CH)
        YB = ar3(2048, 4, CH)
        ysq = ar3(0, NT, D)
        yt = ar(4096, 2048).rearrange("p (u w c) -> p u w c", u=2, w=2)
        fws = ar(6144, 1024)
        fzs = ar(26624, 512)
        farg, fturn, fred, fh = [ar(24576 + 512 * q, 512)[0:64, :] for q in range(4)]
        sil = ar(4096, 512)
        hb = ar(4608, 512)
        hbT = ar(7168, 512)
        ysb = ar3(7680, 2, D)
        G = ar3(9728, 2 * NT, D)
        xo = ar3(18000, NT, D)
        Xg = ar3(22100, 2, D)
        XT = ar3(24148, 2, D)
        fbias, rsum_b = grow[:, 0:512], grow[:, 512:1024]
        RT = ar(5120, 2000)
        slot_row, slot_value = hT[:, :, 0:P], hT[:, :, P:2 * P]
        lg = RT[:, 0:144].rearrange("p (i c) -> p i c", i=NT)

        def opening(b):
            return isinstance(b, int) and b < 2

        def second_pool(pool):
            pool.wait_ge(S["p3_prod"], NT)
            pool.dma_start(fws[0:64, :], fwout).then_inc(S["f_in"], 16)
            pool.dma_start(fzs, fconst).then_inc(S["f_in"], 16)
            pool.wait_ge(S["post_x"], 3 * NT)
            pool.dma_start(ar(20480, 2048), decay).then_inc(S["decay_in"], 16)
            pool.dma_start(fbias, frow).then_inc(S["fb_in"], 16)
            low_pool(pool, "in2")
            pool.wait_ge(S["yo_ev"], NT)
            low_pool(pool, "out2")
            pool.dma_start(grow[:, :], grows[3, :, :]).then_inc(S["g_in"], 16)
            pool.wait_ge(S["norm_xn"], 4 * NT)
            for j in range(2 * NT):
                pool.dma_start(rows[j * P:(j + 1) * P, :], xn[:, j % NT, :]).then_inc(S["rows_st"], 16)
            pool.dma_start(grow[:, :], grows[4, :, :]).then_inc(S["g_in"], 16)
            pool.memset(ar(22100, 2048), 0.0).then_inc(S["xg_zero"], 1)
            pool.wait_ge(S["rows_st"], 16 * 2 * NT)
            pool.wait_ge(S["xg_zero"], 1)
            pool.wait_ge(S["idx_in"], 1)

            def gather(b, q, column):
                pool.wait_ge(S["x_tr"], b * 2 + 2)
                pool.sem_inc(S["gathers"], 1)
                nc.gpsimd.tensor_copy(at_in[q][:, :], idx[:, column]).then_inc(S["at_in"], 1)
                pool.wait_ge(S["at_in"], b + 1)
                pool.sem_inc(S["gathers"], 1)
                pool.indirect_dma_start(out=Xg[:, q, :], out_offset=None, in_=rows,
                                        in_offset=bass.IndirectOffsetOnAxis(ap=at_in[q][:, 0:1], axis=0),
                                        bounds_check=2 * T - 1, oob_is_err=False).then_inc(S[f"xg_in{q}"], 16)

            def scatter(b, half, q, column):
                if not opening(b):
                    pool.wait_ge(S[f"y_st{q}"], half * 16)
                    pool.sem_inc(S["scatters"], 1)
                nc.gpsimd.tensor_copy(at_out[q][:, :], idx[:, column]).then_inc(S["at_out"], 1)
                pool.wait_ge(S["at_out"], b + 1)
                pool.wait_ge(S["y_ev_act"], b + 2)
                pool.wait_ge(S["y_ev_dve"], b + 2)
                pool.sem_inc(S["scatters"], 1)
                pool.indirect_dma_start(out=back, out_offset=bass.IndirectOffsetOnAxis(ap=at_out[q][:, 0:1], axis=0),
                                        in_=ysb[:, q, :], in_offset=None,
                                        bounds_check=2 * T - 1, oob_is_err=False).then_inc(S[f"y_st{q}"], 16)

            def first_of(e):
                return slice(NT * e, NT * e + 1)

            gather(0, 0, first_of(0))
            gather(1, 1, first_of(1))
            for q in range(2):
                gather(2 + q, q, first_of(2 + q))
                scatter(q, 0, q, first_of(q))
            with pool.Fori(1, N_EXP // 2 - 1) as turn:
                for q in range(2):
                    gather(turn * 2 + (q + 2), q, bass.ds(turn * (2 * NT) + NT * (q + 2), 1))
                    scatter(turn * 2 + q, turn, q, bass.ds(turn * (2 * NT) + NT * q, 1))
            for q in range(2):
                scatter(N_EXP - 2 + q, N_EXP // 2 - 1, q, first_of(N_EXP - 2 + q))
            pool.wait_ge(S["over_ready"], 1)
            some = pool.value_load(over[0:1, 0:1], min_val=0, max_val=1)
            with pool.If(some > 0):
                with pool.Fori(0, N_OVER // 2) as turn:
                    for q in range(2):
                        valid = pool.value_load(over[0:1, bass.ds(turn * 2 + q, 1)], min_val=0, max_val=1)
                        with pool.If(valid > 0):
                            column = pool.value_load(over[0:1, bass.ds(turn * 2 + (q + N_OVER), 1)], min_val=0, max_val=NT * N_EXP - 1)
                            gather(turn * 2 + (N_EXP + q), q, bass.ds(column, 1))
                            scatter(turn * 2 + (N_EXP + q), turn + N_EXP // 2, q, bass.ds(column, 1))
                            pool.wait_ge(S[f"y_st{q}"], turn * 16 + 16 * (N_EXP // 2 + 1))
            for q in range(2):
                pool.wait_ge(S[f"y_st{q}"], 16 * (N_EXP // 2))
            for i in range(NT):
                for c in range(2):
                    pool.dma_start(G[:, 2 * i + c, :], back[(NT * c + i) * P:(NT * c + i + 1) * P, :]).then_inc(S[f"back{i}"], 16)
            for i in range(NT):
                pool.wait_ge(S["fin_y"], i + 1)
                pool.dma_start(out[i * P:(i + 1) * P, :], xo[:, i, :]).then_inc(S["out_st"], 16)
            pool.wait_ge(S["out_st"], 16 * NT)

        def expert_stream(sp):
            def part(g, places, first):
                for s in places:
                    sp.wait_ge(S["w_used"], g * RING + (W_EXP + s + 1 - RING))
                    sp.dma_start(ring[:, s, :], W[first + s, :, :]).then_inc(landed[s], 16)

            part(0, range(0, 4), W_EXP)
            part(0, range(8, 12), W_EXP - 4)
            with sp.Fori(1, N_EXP) as g:
                part(g, range(0, 4), g * RING + W_EXP)
                part(g, range(4, 8), g * RING + (W_EXP - RING + 4))
                part(g, range(8, 12), g * RING + (W_EXP - 4))
            part(N_EXP, range(4, 8), N_EXP * RING + (W_EXP - RING + 4))
            sp.wait_ge(S["over_ready"], 1)
            some = sp.value_load(over[0:1, 0:1], min_val=0, max_val=1)
            with sp.If(some > 0):
                with sp.Fori(0, N_OVER // 2) as turn:
                    for q in range(2):
                        valid = sp.value_load(over[0:1, bass.ds(turn * 2 + q, 1)], min_val=0, max_val=1)
                        with sp.If(valid > 0):
                            first = sp.value_load(over[0:1, bass.ds(turn * 2 + (q + 2 * N_OVER), 1)], min_val=0,
                                                  max_val=N_TILES - RING)
                            for s in range(RING):
                                sp.wait_ge(S["w_used"], turn * (2 * RING) + (W_EXP + (N_EXP + q) * RING + s + 1))
                                sp.dma_start(ring[:, s, :], W[bass.ds(first + s, 1), :, :]).then_inc(landed[s], 16)

        def second_pe(pe):
            used = S["w_used"]
            pe.wait_ge(S["pg_sig"], NT)
            pe.wait_ge(S["f_in"], 32)
            nc.tensor.matmul(pb[0:64, 0, :], col("f_w_in", 0, 64)[0:33, :], fzs[0:33, :], start=True, stop=True)\
                .then_inc(S["fm_mm"], 1)
            for q in range(2):
                pe.wait_ge(S["fm_sin"], q + 1)
                nc.tensor.matmul(pb[0:64, q + 1, :], col("f_w_mid", 64 * q, 64)[0:64, :], fh, start=True, stop=True)\
                    .then_inc(S["fm_mm"], 1)
            pe.wait_ge(S["fm_sin"], 3)
            for i in range(NT):
                for h in range(2):
                    last = nc.tensor.matmul(pb[:, 2 * i + h, :], fh[:, i * P:(i + 1) * P], fws[0:64, h * 512:(h + 1) * 512],
                                            start=True, stop=True)
                last.then_inc(S["fo_mm"], 1)
            pe.wait_ge(S["fo_ev"], NT)
            for i in range(NT):
                pe.wait_ge(S["habs"], i + 1)
                for h in range(2):
                    last = nc.tensor.matmul(pb[:, 0, :], cs("ones"), absb[:, i % 2, h * 512:(h + 1) * 512],
                                            start=(i == 0 and h == 0), stop=(i == NT - 1 and h == 1))
                last.then_inc(S["hs_mm"], 1)
            pe.wait_ge(S["hs_ready"], 1)
            tr_pe(pe, "n3", xn, NT, ND, ready=S["norm_xn"], before=2 * NT)
            for m in range(16):
                if m >= 8:
                    pe.wait_ge(S["in2_conv"], m - 7)
                split_features(pe, "in2", m, m % 8, hT_r, in2_low, 3)
            pe.wait_ge(S["in2_conv"], 12)
            pe.wait_ge(S["in2_f"], 4)
            for i in range(NT):
                for w in range(2):
                    for m in range(4):
                        last = nc.tensor.matmul(pb[:, 2 * i + w, m * P:(m + 1) * P], uF[:, m, i * P:(i + 1) * P],
                                                cs("dft64")[:, w * P:(w + 1) * P], start=True, stop=True)
                last.then_inc(S["fd_mm"], 1)
            pe.wait_ge(S["fd_ev"], NT)
            pe.wait_ge(S["z_ready"], 4)
            tr_pe(pe, "z", uc[:, 4:8, :], 4, NT)
            tr_pe(pe, "x0", uc[:, 0:4, :], 4, NT, bank0=4)
            tr_wait(pe, "z")
            tr_wait(pe, "x0")
            pe.wait_ge(S["pm_ready"], 1)
            arrived(pe, W_DFT)
            for m in range(4):
                b = 4 * (m % 2)
                n = W_DFT + 1 + m
                arrived(pe, n)
                if m == 1:
                    pe.wait_ge(S["kf_ev"], 3)
                if m >= 2:
                    pe.wait_ge(S["y_ready"], m - 1)
                for w, src in ((0, Pk), (1, Mk)):
                    for k in range(NT):
                        last = nc.tensor.matmul(pb[:, b + w, :], tile(n)[:, (4 * w + k) * P:(4 * w + k + 1) * P], src[:, k, :],
                                                start=(k == 0), stop=(k == NT - 1))
                    last.then_inc(S["kf_mm"], 1)
                if m == 0:
                    for k in range(NT):
                        last = nc.tensor.matmul(pb[:, 4, :], tile(W_DFT)[:, k * P:(k + 1) * P], Pk[:, k, :],
                                                start=(k == 0), stop=(k == NT - 1))
                    last.then_inc(S["kf_mm"], 1)
                for w in range(2):
                    basis = tile(W_DFT) if m == 0 and w == 1 else tile(n)
                    for k in range(NT):
                        last = nc.tensor.matmul(pb[:, b + 2 + w, :], basis[:, (4 * w + k) * P:(4 * w + k + 1) * P], zt[:, k, :],
                                                start=(k == 0), stop=(k == NT - 1))
                last.then_inc(used, 2 if m == 0 else 1)
            pe.wait_ge(S["y_ready"], 4)
            for i in range(NT):
                n = W_IDFT + i
                arrived(pe, n)
                for w, src in ((0, YA), (1, YB)):
                    for k in range(NT):
                        last = nc.tensor.matmul(pb[:, i, :], tile(n)[:, (4 * w + k) * P:(4 * w + k + 1) * P], src[:, k, :],
                                                start=(w == 0 and k == 0), stop=(w == 1 and k == NT - 1))
                last.then_inc(used, 1)
            for i in range(NT):
                n = W_FFT + i
                arrived(pe, n)
                for w in range(2):
                    for k in range(NT):
                        last = nc.tensor.matmul(pb[:, 4 + i, :], tile(n)[:, (4 * w + k) * P:(4 * w + k + 1) * P], vCS[:, k, w, :],
                                                start=(w == 0 and k == 0), stop=(w == 1 and k == NT - 1))
                last.then_inc(used, 1)
            tr_pe(pe, "y2", Y, NT, ND, ready=S["hn_y"])
            tr_wait(pe, "y2")
            split_tokens(pe, "out2", S["wo2_mm"])
            pe.wait_ge(S["wo2_x"], NT)
            tr_pe(pe, "n4", xn, NT, ND, ready=S["norm_xn"], before=3 * NT)
            tr_wait(pe, "n4")
            arrived(pe, W_ROUTE)
            for i in range(NT):
                for k in range(ND):
                    last = nc.tensor.matmul(pb[:, i, 0:36], hT[:, k, i * P:(i + 1) * P], tile(W_ROUTE)[:, 36 * k:36 * k + 36],
                                            start=(k == 0), stop=(k == ND - 1))
            last.then_inc(used, 1)
            pe.wait_ge(S["rt_lg"], 1)
            pe.wait_ge(S["sel_ready"], 1)
            for i in range(NT):
                for j in range(i + 1):
                    nc.tensor.matmul(pb[:, 4 + i, 0:32], tri16[:, :] if j == i else ones16[:, :], sel[:, j, :],
                                     start=(j == 0), stop=(j == i))
            for j in range(NT):
                last = nc.tensor.matmul(pb[:, 0, 0:32], ones16[:, :], sel[:, j, :], start=(j == 0), stop=(j == NT - 1))
            last.then_inc(S["rank_mm"], 1)
            for j in range(2 * NT):
                pe.wait_ge(S["slot_ready"], j + 1)
                last = nc.tensor.matmul(pb[:, 1, 0:P], slot_row[:, j, :], slot_value[:, j, :], start=(j == 0), stop=(j == 2 * NT - 1))
            last.then_inc(S["slot_mm"], 1)
            pe.sem_inc(S["x_tr"], 4)

            def turn_rows(b, half, q):
                pe.wait_ge(S[f"xg_in{q}"], half * 16 + 16)
                pe.wait_ge(S["x_ev_dve"], b + 1)
                pe.wait_ge(S["x_ev_act"], b + 1)
                for h in range(2):
                    for k in range(4):
                        last = nc.tensor.transpose(pb[:, 2 + h, k * P:(k + 1) * P], Xg[:, q, (4 * h + k) * P:(4 * h + k + 1) * P], ident)
                    last.then_inc(S["x_tr"], 1)

            def product(b, q, bank, place, skipped=0):
                for k in range(ND):
                    s = place + k // 2
                    if k % 2 == 0:
                        pe.wait_ge(landed[s], b * 16 + 16 * (W_EXP // RING + 1))
                    last = nc.tensor.matmul(pb[:, bank, :], XT[:, q, k * P:(k + 1) * P],
                                            ring[:, s, (k % 2) * 512:(k % 2 + 1) * 512], start=(k == 0), stop=(k == ND - 1))
                    if k % 2:
                        last.then_inc(used, 1 + (skipped if k == ND - 1 else 0))

            def gate(b, q, skipped=0):
                pe.wait_ge(S["x_ev_dve"], b + 2)
                pe.wait_ge(S["x_ev_act"], b + 2)
                pe.wait_ge(S["ex_sig"], b + 1)
                product(b, q, 0, 0, skipped)

            def turn_hidden(b):
                pe.wait_ge(S["ex_hid"], b + 1)
                for k in range(4):
                    last = nc.tensor.transpose(pb[:, 4, k * P:(k + 1) * P], hb[:, k * P:(k + 1) * P], ident)
                last.then_inc(S["h_tr"], 1)

            def down(b, place, skipped=0):
                pe.wait_ge(S["h_ev"], b + 1)
                pe.wait_ge(S["y_ev_act"], b + 1)
                pe.wait_ge(S["y_ev_dve"], b + 1)
                for k in range(4):
                    pe.wait_ge(landed[place + k], b * 16 + 16 * (W_EXP // RING + 1))
                    for h in range(2):
                        last = nc.tensor.matmul(pb[:, 6 + h, :], hbT[:, k * P:(k + 1) * P],
                                                ring[:, place + k, h * 512:(h + 1) * 512], start=(k == 0), stop=(k == 3))
                    last.then_inc(used, 1 + (skipped if k == 3 else 0))

            def between(b, half, q, follow):
                gate(b + 1, 1 - q)
                turn_hidden(b)
                if follow:
                    turn_rows(b + 2, half + 1, q)
                down(b, 4)
                product(b + 1, 1 - q, 1, 8, 0 if follow else 4)

            turn_rows(0, 0, 0)
            turn_rows(1, 0, 1)
            pe.wait_ge(S["counts_out"], 1)
            gate(0, 0, 4)
            product(0, 0, 1, 8)
            with pe.Fori(0, N_EXP // 2 - 1) as turn:
                for q in range(2):
                    between(turn * 2 + q, turn, q, True)
            between(N_EXP - 2, N_EXP // 2 - 1, 0, False)
            turn_hidden(N_EXP - 1)
            down(N_EXP - 1, 4, 4)
            pe.wait_ge(S["over_ready"], 1)
            some = pe.value_load(over[0:1, 0:1], min_val=0, max_val=1)
            with pe.If(some > 0):
                with pe.Fori(0, N_OVER // 2) as turn:
                    for q in range(2):
                        valid = pe.value_load(over[0:1, bass.ds(turn * 2 + q, 1)], min_val=0, max_val=1)
                        with pe.If(valid > 0):
                            b = turn * 2 + (N_EXP + q)
                            turn_rows(b, turn + N_EXP // 2, q)
                            gate(b, q)
                            product(b, q, 1, 4)
                            turn_hidden(b)
                            down(b, 8)

        def second_act(act):
            for q in range(3):
                act.wait_ge(S["fm_arg"], q + 1)
                nc.scalar.activation(fh, fred, ACT.Sin).then_inc(S["fm_sin"], 1)
            for i in range(NT):
                act.wait_ge(S["fo_ev"], i + 1)
                if i >= 2:
                    act.wait_ge(S["hs_mm"], i - 1)
                nc.scalar.activation(absb[:, i % 2, 0:512], HF[:, i, :], ACT.Abs)
                nc.scalar.activation(absb[:, i % 2, 512:1024], HB[:, i, :], ACT.Abs).then_inc(S["habs"], 1)
            for m in range(2):
                high_act(act, "in2", m)
            norm_act(act, "n3", S["post_x"], 3 * NT)
            tr_act(act, "n3", hT_r, ND, "norm1")
            for m in range(16):
                if m < 14:
                    high_act(act, "in2", m + 2)
                act.wait_ge(S["w_used"], W_IN2 + m + 1)
                if m < 12:
                    nc.scalar.activation(uc[:, m, :], pb[:, m % 8, :], ACT.Identity, scale=col("conv_w", 12 + m),
                                         bias=col("conv_b", m)).then_inc(S["in2_lin"], 1)
                else:
                    nc.scalar.activation(uF[:, m - 12, :], pb[:, m % 8, :], ACT.Copy).then_inc(S["in2_f"], 1)
            for i in range(NT):
                act.wait_ge(S["fd_mm"], i + 1)
                nc.scalar.activation(vCS[:, i, :, :], pb[:, 2 * i:2 * i + 2, :], ACT.Copy).then_inc(S["fd_ev"], 1)
            tr_act(act, "z", zt, NT)
            tr_act(act, "x0", x0t, NT, bank0=4)
            count = 0
            for m in range(4):
                if m >= 2:
                    act.wait_ge(S["y_ready"], m - 1)
                for w in range(3 if m == 0 else 2):
                    count += 1
                    act.wait_ge(S["kf_mm"], count)
                    src = pb[:, 4, :] if w == 2 else pb[:, 4 * (m % 2) + w, :]
                    nc.scalar.activation(Kn if w == 2 else Kt[:, m % 2, w, :], src, ACT.Copy).then_inc(S["kf_ev"], 1)
            for i in range(NT):
                act.wait_ge(S["w_used"], W_FFT + i + 1)
                act.wait_ge(S["y_ready"], 4)
                nc.scalar.activation(Y[:, i, 512:1024], pb[:, 4 + i, :], ACT.Copy).then_inc(S["fo2_ev"], 1)
            for i in range(NT):
                act.wait_ge(S["yo_ev"], i + 1)
                act.wait_ge(S["fo2_ev"], i + 1)
                nc.scalar.activation(ysq[:, i, :], Y[:, i, :], ACT.Square).then_inc(S["hn_sq"], 1)
            for m in range(2):
                high_act(act, "out2", m)
            act.wait_ge(S["hn_ms"], 1)
            nc.scalar.activation(hnr, hns, ACT.Sqrt).then_inc(S["hn_rt"], 1)
            tr_act(act, "y2", hT, ND, "mix_g")
            for m in range(2, ND):
                high_act(act, "out2", m)
            norm_act(act, "n4", S["wo2_x"], NT)
            tr_act(act, "n4", hT, ND)
            act.wait_ge(S["rt_g"], 1)
            nc.scalar.activation(RT[:, 288:304], RT[:, 272:288], ACT.Exp).then_inc(S["rt_exp"], 1)
            act.wait_ge(S["rt_d"], 1)
            nc.scalar.activation(RT[:, 308:312], RT[:, 304:308], ACT.Exp).then_inc(S["rt_exp"], 1)
            act.sem_inc(S["y_ev_act"], 1)
            act.sem_inc(S["x_ev_act"], 1)
            act.sem_inc(S["ex_sig"], 1)

            def rows_act(b, q):
                act.wait_ge(S["x_tr"], b * 2 + 6)
                nc.scalar.activation(XT[:, q, 512:1024], pb[:, 3, :], ACT.Copy).then_inc(S["x_ev_act"], 1)

            def hidden_act(b):
                act.wait_ge(S["h_tr"], b + 1)
                nc.scalar.activation(hbT, pb[:, 4, :], ACT.Copy).then_inc(S["h_ev"], 1)

            def silu_act(b, past):
                act.wait_ge(S["w_used"], b * RING + past)
                act.wait_ge(S["ex_mul"], b + 1)
                nc.scalar.activation(sil, pb[:, 0, :], ACT.Silu).then_inc(S["ex_sig"], 1)

            def out_act(b, half, q, past):
                act.wait_ge(S["w_used"], b * RING + past)
                if not opening(b):
                    act.wait_ge(S[f"y_st{q}"], half * 16)
                nc.scalar.activation(ysb[:, q, 0:512], pb[:, 6, :], ACT.Copy).then_inc(S["y_ev_act"], 1)

            def between_act(b, half, q, follow):
                hidden_act(b)
                silu_act(b + 1, W_EXP + 4)
                if follow:
                    rows_act(b + 2, q)
                out_act(b, half, q, W_EXP + RING + 8)

            rows_act(0, 0)
            rows_act(1, 1)
            silu_act(0, W_EXP + 4)
            for q in range(2):
                between_act(q, 0, q, True)
            with act.Fori(1, N_EXP // 2 - 1) as turn:
                for q in range(2):
                    between_act(turn * 2 + q, turn, q, True)
            between_act(N_EXP - 2, N_EXP // 2 - 1, 0, False)
            hidden_act(N_EXP - 1)
            out_act(N_EXP - 1, N_EXP // 2 - 1, 1, W_EXP + RING + 8)
            act.wait_ge(S["over_ready"], 1)
            some = act.value_load(over[0:1, 0:1], min_val=0, max_val=1)
            with act.If(some > 0):
                with act.Fori(0, N_OVER // 2) as turn:
                    for q in range(2):
                        valid = act.value_load(over[0:1, bass.ds(turn * 2 + q, 1)], min_val=0, max_val=1)
                        with act.If(valid > 0):
                            b = turn * 2 + (N_EXP + q)
                            rows_act(b, q)
                            silu_act(b, W_EXP + RING + 4)
                            hidden_act(b)
                            out_act(b, turn + N_EXP // 2, q, W_EXP + 2 * RING)
            norm_act(act, "n5", S["moe_x"], NT)

        def second_dve(dve, chain):
            def L(ins):
                link(dve, chain, ins)

            TT, TS, STT = nc.vector.tensor_tensor, nc.vector.tensor_scalar, nc.vector.scalar_tensor_tensor
            for q in range(3):
                dve.wait_ge(S["fm_mm"], q + 1)
                b = col("f_b_in") if q == 0 else col("f_b_mid", q - 1)
                L(TS(farg, pb[0:64, q, :], b[0:64, :], col("f_freq", q)[0:64, :], ALU.add, ALU.mult))
                reduce_angle(L, nc, farg, fturn, fred)
                TS(fred, fred, PI_LOW, -PI_LOW, ALU.min, ALU.max).then_inc(S["fm_arg"], 1)
            dve.wait_ge(S["decay_in"], 16)
            for i in range(NT):
                dve.wait_ge(S["fo_mm"], i + 1)
                TT(HF[:, i, :], pb[:, 2 * i, :], decs[:, i, :], ALU.mult)
                ins = TT(HB[:, i, :], pb[:, 2 * i + 1, :], decs[:, i, :], ALU.mult)
                if i == 0:
                    L(ins)
                    ins = nc.vector.memset(HB[0:1, 0, :], 0.0)
                ins.then_inc(S["fo_ev"], 1)
                dve.wait_ge(S["fo_ev"], i + 1)
            for i in range(NT):
                TT(Pk[:, i, :], HF[:, i, :], HB[:, i, :], ALU.add)
                last = TT(Mk[:, i, :], HF[:, i, :], HB[:, i, :], ALU.subtract)
            last.then_inc(S["pm_ready"], 1)
            dve.wait_ge(S["hs_mm"], NT)
            dve.wait_ge(S["fb_in"], 16)
            L(nc.vector.reciprocal(rsum_b, pb[:, 0, :]))
            TS(rsum_b, rsum_b, 2.0 / (2 * T), None, ALU.mult).then_inc(S["hs_ready"], 1)
            norm_dve(dve, chain, "n3")
            tr_split_dve(dve, "n3", hT_r, in2_low, S["hT_low"], gain="norm1")
            for m in range(12):
                dve.wait_ge(S["in2_lin"], m + 1)
                u = pb[:, m % 8, :]
                L(STT(out=uc[:, m, 1:T], in0=u[:, 0:T - 1], scalar=col("conv_w", m), in1=uc[:, m, 1:T],
                      op0=ALU.mult, op1=ALU.add))
                STT(out=uc[:, m, 0:T - 1], in0=u[:, 1:T], scalar=col("conv_w", 24 + m), in1=uc[:, m, 0:T - 1],
                    op0=ALU.mult, op1=ALU.add).then_inc(S["in2_conv"], 1)
                if m >= 8:
                    dve.wait_ge(S["in2_conv"], m + 1)
                    TT(uc[:, m - 4, :], uc[:, m - 4, :], uc[:, m, :], ALU.mult).then_inc(S["z_ready"], 1)
            tr_dve(dve, "z", zt, NT)
            tr_dve(dve, "x0", x0t, NT, bank0=4)
            for m in range(4):
                b = 4 * (m % 2)
                dve.wait_ge(S["kf_ev"], 3 + 2 * m)
                dve.wait_ge(S["w_used"], W_DFT + 2 + m)
                if m:
                    dve.wait_ge(S["y_ready"], m)
                KA, KB = Kt[:, m % 2, 0, :], Kt[:, m % 2, 1, :]
                ZA, ZB = pb[:, b + 2, :], pb[:, b + 3, :]
                TT(prod[:, 0, :], ZA, KA, ALU.mult)
                TT(prod[:, 1, :], ZB, KB, ALU.mult)
                TT(prod[:, 2, :], ZA, KB, ALU.mult)
                L(TT(prod[:, 3, :], ZB, Kn if m == 0 else KA, ALU.mult))
                TT(YA[:, m, :], prod[:, 0, :], prod[:, 1, :], ALU.subtract)
                TT(YB[:, m, :], prod[:, 2, :], prod[:, 3, :], ALU.add).then_inc(S["y_ready"], 1)
            dve.wait_ge(S["y_ready"], 4)
            for i in range(NT):
                dve.wait_ge(S["w_used"], W_IDFT + i + 1)
                TT(yt[:, i % 2, 0, :], pb[:, i, :], rsum_b, ALU.mult)
                L(TT(yt[:, i % 2, 1, :], zt[:, i, :], fbias, ALU.mult))
                L(TT(yt[:, i % 2, 0, :], yt[:, i % 2, 0, :], yt[:, i % 2, 1, :], ALU.add))
                TT(Y[:, i, 0:512], yt[:, i % 2, 0, :], x0t[:, i, :], ALU.mult).then_inc(S["yo_ev"], 1)
                dve.wait_ge(S["yo_ev"], i + 1)
            for i in range(NT):
                dve.wait_ge(S["hn_sq"], i + 1)
                ins = nc.vector.tensor_reduce(hni[:, 16 * i:16 * i + 16], ysq[:, i, :].rearrange("p (h c) -> p h c", c=64),
                                              AX.X, ALU.add)
            L(ins)
            TS(hns, hni, 1.0 / 64, EPS, ALU.mult, ALU.add).then_inc(S["hn_ms"], 1)
            dve.wait_ge(S["hn_rt"], 1)
            L(nc.vector.reciprocal(hni, hnr))
            for i in range(NT):
                y = Y[:, i, :].rearrange("p (h c) -> p h c", c=64)
                TT(y, y, hni[:, 16 * i:16 * i + 16].unsqueeze(2).broadcast_to([P, 16, 64]), ALU.mult).then_inc(S["hn_y"], 1)
            tr_dve(dve, "y2", hT, ND, "mix_g")
            tr_wait(dve, "y2")
            split_dve(dve, chain, "out2", hT)
            for i in range(NT):
                product(dve, S["wo2_mm"], 0, i, W_ROUTE - 1)
                TT(X[:, i, :], X[:, i, :], pair(i), ALU.add).then_inc(S["wo2_x"], 1)
            dve.wait_ge(S["wo2_x"], NT)
            dve.wait_ge(S["g_in"], 64)
            norm_dve(dve, chain, "n4", grow)
            tr_dve(dve, "n4", hT, ND)
            dve.wait_ge(S["w_used"], W_EXP)
            b4 = [P, NT, 4]
            TT(lg, pb[:, 0:4, 0:36], col("r_bias", 0, 36).unsqueeze(1).broadcast_to([P, NT, 36]), ALU.add)\
                .then_inc(S["rt_lg"], 1)
            dve.wait_ge(S["rt_lg"], 1)
            glog = lg[:, :, 0:4]
            elog = lg[:, :, 4:36]

            def by_t(a, n):
                return RT[:, a:a + NT * n].rearrange("p (i c) -> p i c", i=NT)

            def first_of(src, n, iota, best, mark, low, hot):
                L(nc.vector.tensor_reduce(best, src, AX.X, ALU.max))
                L(TT(mark, src, best.unsqueeze(2).broadcast_to([P, NT, n]), ALU.is_equal))
                L(STT(out=mark, in0=mark, scalar=-64.0, in1=iota.unsqueeze(1).broadcast_to([P, NT, n]), op0=ALU.mult, op1=ALU.add))
                L(nc.vector.tensor_reduce(low, mark, AX.X, ALU.min))
                L(TT(hot, mark, low.unsqueeze(2).broadcast_to([P, NT, n]), ALU.is_equal))

            gbest, low, ghot, gmark = RT[:, 312:316], RT[:, 316:320], by_t(320, 4), by_t(336, 4)
            first_of(glog, 4, cs("giota"), gbest, gmark, low, ghot)
            TT(by_t(272, 4), glog, gbest.unsqueeze(2).broadcast_to(b4), ALU.subtract).then_inc(S["rt_g"], 1)
            L(TS(gmark, ghot, -NEG, NEG, ALU.mult, ALU.add))
            masked, mark, hot1, hot2 = by_t(352, 32), by_t(480, 32), by_t(608, 32), by_t(736, 32)
            for i in range(NT):
                ins = TT(masked[:, i, :].rearrange("p (g c) -> p g c", g=4), elog[:, i, :].rearrange("p (g c) -> p g c", g=4),
                         gmark[:, i, :].unsqueeze(2).broadcast_to([P, 4, 8]), ALU.add)
            L(ins)
            best1, best2 = RT[:, 864:868], RT[:, 868:872]
            first_of(masked, 32, cs("eiota"), best1, mark, low, hot1)
            L(STT(out=masked, in0=hot1, scalar=2 * NEG, in1=masked, op0=ALU.mult, op1=ALU.add))
            first_of(masked, 32, cs("eiota"), best2, mark, low, hot2)
            TT(sel[:, :, :], hot1, hot2, ALU.add).then_inc(S["sel_ready"], 1)
            TT(RT[:, 304:308], best2, best1, ALU.subtract).then_inc(S["rt_d"], 1)
            dve.wait_ge(S["rt_exp"], 2)
            L(nc.vector.tensor_reduce(RT[:, 872:876], by_t(288, 4), AX.X, ALU.add))
            L(TS(RT[:, 876:880], RT[:, 308:312], 1.0, None, ALU.add))
            L(TT(RT[:, 872:876], RT[:, 872:876], RT[:, 876:880], ALU.mult))
            L(nc.vector.reciprocal(RT[:, 880:884], RT[:, 872:876]))
            L(TT(RT[:, 884:888], RT[:, 880:884], RT[:, 308:312], ALU.mult))
            dve.wait_ge(S["rank_mm"], 1)
            for c, hot in ((0, hot1), (1, hot2)):
                L(TT(masked, hot, pb[:, 4:8, 0:32], ALU.mult))
                L(nc.vector.tensor_reduce(RT[:, 888 + 4 * c:892 + 4 * c], masked, AX.X, ALU.add))
                L(TT(masked, hot, cs("eiota").unsqueeze(1).broadcast_to([P, NT, 32]), ALU.mult))
                L(nc.vector.tensor_reduce(RT[:, 896 + 4 * c:900 + 4 * c], masked, AX.X, ALU.add))
            rank, which, block, row, value, column = RT[:, 888:896], RT[:, 896:904], RT[:, 904:912], RT[:, 912:920], \
                RT[:, 920:928], RT[:, 928:936]
            L(TS(block, rank, float(P), None, ALU.is_ge))
            for n in (2, 3):
                L(TS(row, rank, float(n * P), None, ALU.is_ge))
                L(TT(block, block, row, ALU.add))
            L(STT(out=row, in0=block, scalar=-float(P), in1=rank, op0=ALU.mult, op1=ALU.add))
            L(STT(out=column, in0=which, scalar=float(NT), in1=block, op0=ALU.mult, op1=ALU.add))
            L(TT(value, cs("choice"), row, ALU.subtract))
            for j in range(2 * NT):
                TS(slot_row[:, j, :], cs("iota"), row[:, j:j + 1], None, ALU.is_equal)
                TS(slot_value[:, j, :], cs("iota"), column[:, j:j + 1], value[:, j:j + 1], ALU.is_equal, ALU.mult)\
                    .then_inc(S["slot_ready"], 1)
            dve.wait_ge(S["slot_mm"], 1)
            L(TS(slot_row[:, 0, :], pb[:, 1, 0:P], cs("empty"), None, ALU.add))
            nc.vector.tensor_copy(idx[:, :], slot_row[:, 0, :]).then_inc(S["idx_in"], 1)
            dve.sem_inc(S["y_ev_dve"], 1)
            dve.sem_inc(S["x_ev_dve"], 1)
            dve.sem_inc(S["ex_mul"], 1)
            counts = RT[0:1, 1400:1432]
            nc.vector.tensor_copy(counts, pb[0:1, 0, 0:32]).then_inc(S["counts_out"], 1)

            def rows_dve(b, q):
                dve.wait_ge(S["x_tr"], b * 2 + 5)
                nc.vector.tensor_copy(XT[:, q, 0:512], pb[:, 2, :]).then_inc(S["x_ev_dve"], 1)

            def hidden_dve(b, past):
                dve.wait_ge(S["w_used"], b * RING + past)
                dve.wait_ge(S["ex_sig"], b + 2)
                TT(hb, sil, pb[:, 1, :], ALU.mult).then_inc(S["ex_hid"], 1)
                dve.wait_ge(S["ex_hid"], b + 1)
                dve.sem_inc(S["ex_mul"], 1)

            def out_dve(b, half, q, past):
                dve.wait_ge(S["w_used"], b * RING + past)
                if not opening(b):
                    dve.wait_ge(S[f"y_st{q}"], half * 16)
                nc.vector.tensor_copy(ysb[:, q, 512:1024], pb[:, 7, :]).then_inc(S["y_ev_dve"], 1)

            def between_dve(b, half, q, follow):
                if follow:
                    rows_dve(b + 2, q)
                out_dve(b, half, q, W_EXP + RING + 8)
                hidden_dve(b + 1, W_EXP + RING)

            rows_dve(0, 0)
            rows_dve(1, 1)
            dve.wait_ge(S["counts_out"], 1)
            o1 = RT[0:1, :]
            extra, incl, alt, both = o1[:, 920:952], o1[:, 952:984], o1[:, 984:1016], o1[:, 1016:1272]
            L(TS(extra, counts, float(P), None, ALU.is_gt))
            for n in (2, 3):
                L(TS(alt, counts, float(n * P), None, ALU.is_gt))
                L(TT(extra, extra, alt, ALU.add))
            L(nc.vector.tensor_copy(incl, extra))
            for step in (1, 2, 4, 8, 16):
                L(nc.vector.tensor_copy(alt, incl))
                L(TT(incl[:, step:32], alt[:, step:32], alt[:, 0:32 - step], ALU.add))
            v = cs("eiota")[0:1, 0:N_OVER]
            both3 = both.rearrange("p (v e) -> p v e", e=32)
            L(TT(both3, incl.unsqueeze(1).broadcast_to([1, N_OVER, 32]), v.unsqueeze(2).broadcast_to([1, N_OVER, 32]), ALU.is_le))
            res = o1[:, 1272:1272 + 4 * N_OVER].rearrange("p (k v) -> p k v", k=4)
            L(nc.vector.tensor_reduce(res[:, 3, :], both3, AX.X, ALU.add))
            L(TT(both3, both3, extra.unsqueeze(1).broadcast_to([1, N_OVER, 32]), ALU.mult))
            L(nc.vector.tensor_reduce(res[:, 1, :], both3, AX.X, ALU.add))
            L(TT(res[:, 1, :], v, res[:, 1, :], ALU.subtract))
            L(TS(res[:, 3, :], res[:, 3, :], float(N_EXP - 1), None, ALU.min))
            L(TS(res[:, 1, :], res[:, 1, :], 1.0, float(NT - 1), ALU.add, ALU.min))
            L(STT(out=res[:, 1, :], in0=res[:, 3, :], scalar=float(NT), in1=res[:, 1, :], op0=ALU.mult, op1=ALU.add))
            L(TS(res[:, 2, :], res[:, 3, :], float(RING), float(W_EXP), ALU.mult, ALU.add))
            L(TS(res[:, 0, :], v, incl[:, 31:32], None, ALU.is_lt))
            L(nc.vector.tensor_copy(over[:, :], o1[:, 1272:1272 + 3 * N_OVER]))
            nc.vector.tensor_copy(o1[:, 1272:1273], o1[:, 1273:1274]).then_inc(S["over_ready"], 1)

            hidden_dve(0, W_EXP + RING)
            for q in range(2):
                between_dve(q, 0, q, True)
            with dve.Fori(1, N_EXP // 2 - 1) as turn:
                for q in range(2):
                    between_dve(turn * 2 + q, turn, q, True)
            between_dve(N_EXP - 2, N_EXP // 2 - 1, 0, False)
            out_dve(N_EXP - 1, N_EXP // 2 - 1, 1, W_EXP + RING + 8)
            some = dve.value_load(over[0:1, 0:1], min_val=0, max_val=1)
            with dve.If(some > 0):
                with dve.Fori(0, N_OVER // 2) as turn:
                    for q in range(2):
                        valid = dve.value_load(over[0:1, bass.ds(turn * 2 + q, 1)], min_val=0, max_val=1)
                        with dve.If(valid > 0):
                            b = turn * 2 + (N_EXP + q)
                            rows_dve(b, q)
                            hidden_dve(b, W_EXP + RING + 8)
                            out_dve(b, turn + N_EXP // 2, q, W_EXP + 2 * RING)
            for i in range(NT):
                dve.wait_ge(S[f"back{i}"], 32)
                L(STT(out=X[:, i, :], in0=G[:, 2 * i, :], scalar=RT[:, 880 + i:881 + i], in1=X[:, i, :], op0=ALU.mult, op1=ALU.add))
                STT(out=X[:, i, :], in0=G[:, 2 * i + 1, :], scalar=RT[:, 884 + i:885 + i], in1=X[:, i, :],
                    op0=ALU.mult, op1=ALU.add).then_inc(S["moe_x"], 1)
            dve.wait_ge(S["norm_ss"], 5 * NT)
            TS(ms, ss, 1.0 / D, EPS, ALU.mult, ALU.add).then_inc(S["norm_ms"], 1)
            dve.wait_ge(S["norm_rt"], 5)
            dve.wait_ge(S["g_in"], 80)
            L(nc.vector.reciprocal(rstd, rt))
            for i in range(NT):
                STT(out=xo[:, i, :], in0=X[:, i, :], scalar=rstd[:, i:i + 1], in1=grow[:, :], op0=ALU.mult, op1=ALU.mult)\
                    .then_inc(S["fin_y"], 1)

        block = ctx.enter_context(nc.Block())

        @block.sync
        def _(sp):
            for s in range(RING):
                if s == 2:
                    sp.wait_ge(S["x_in"], 16 * NT)
                sp.dma_start(ring[:, s, :], W[s, :, :]).then_inc(landed[s], 16)
            with sp.Fori(1, W_EXP // RING) as turn:
                for s in range(RING):
                    sp.wait_ge(S["w_used"], turn * RING + (s + 1 - RING))
                    sp.dma_start(ring[:, s, :], W[turn * RING + s, :, :]).then_inc(landed[s], 16)
            expert_stream(sp)

        @block.gpsimd
        def _(pool):
            pool.dma_start(colt[:, :], cols).then_inc(S["small_in"], 16)
            pool.dma_start(cst[:, :], csts).then_inc(S["small_in"], 16)
            pool.dma_start(posi[:, :], pos).then_inc(S["pos_in"], 16)
            pool.dma_start(cmpt, cmp_tab).then_inc(S["tab_in"], 16)
            pool.dma_start(grow[:, :], grows[0, :, :]).then_inc(S["g_in"], 16)
            low_pool(pool, "proj")
            pool.wait_ge(S["w_used"], W_CMP)
            for k in range(ND):
                nc.gpsimd.tensor_tensor(hT[:, k, :], plain(hT_r[:, k, :]), plain(proj_low[:, k, :]), ALU.add)\
                    .then_inc(S["h_back"], 1)
            low_pool(pool, "merge")
            low_pool(pool, "w_o")
            pool.wait_ge(S["post_x"], NT)
            pool.dma_start(ar(24000, 1024), pT).then_inc(S["p_in"], 16)
            pool.dma_start(grow[:, :], grows[1, :, :]).then_inc(S["g_in"], 16)
            low_pool(pool, "up")
            low_pool(pool, "down")
            low_pool(pool, "pgate")
            pool.wait_ge(S["post_x"], 2 * NT)
            pool.dma_start(grow[:, :], grows[2, :, :]).then_inc(S["g_in"], 16)
            second_pool(pool)

        def norm_act(act, n, ready, count, step=1):
            if step > 1:
                act.wait_ge(ready, count)
            for i in range(NT):
                if step == 1:
                    act.wait_ge(ready, count - NT + i + 1)
                if NT * NORMS.index(n) + i:
                    act.wait_ge(S["norm_ss"], NT * NORMS.index(n) + i)
                nc.scalar.activation(junk[:, :], X[:, i, :], ACT.Square, accum_out=ss[:, i:i + 1])\
                    .then_inc(S["norm_ss"], 1)
            act.wait_ge(S["norm_ms"], NORMS.index(n) + 1)
            nc.scalar.activation(rt, ms, ACT.Sqrt).then_inc(S["norm_rt"], 1)

        def link(dve, chain, ins):
            chain[0] += 1
            ins.then_inc(S["dve_chain"], 1)
            dve.wait_ge(S["dve_chain"], chain[0])

        def norm_dve(dve, chain, n, gain=None):
            at = NORMS.index(n)
            dve.wait_ge(S["norm_ss"], NT * (at + 1))
            nc.vector.tensor_scalar(ms, ss, 1.0 / D, EPS, ALU.mult, ALU.add).then_inc(S["norm_ms"], 1)
            dve.wait_ge(S["norm_rt"], at + 1)
            link(dve, chain, nc.vector.reciprocal(rstd, rt))
            for i in range(NT):
                if gain is None:
                    ins = nc.vector.tensor_scalar(xn[:, i, :], X[:, i, :], rstd[:, i:i + 1], None, ALU.mult)
                else:
                    ins = nc.vector.scalar_tensor_tensor(out=xn[:, i, :], in0=X[:, i, :], scalar=rstd[:, i:i + 1],
                                                         in1=gain[:, :], op0=ALU.mult, op1=ALU.mult)
                ins.then_inc(S["norm_xn"], 1)

        def tr_pe(pe, n, src, A, B, bank0=0, ready=None, before=0):
            if ready is None:
                order = [(a, b) for b in range(B) for a in range(A)]
            else:
                order = [(a, b) for a in range(A) for b in range(B)]
            for a, b in order:
                if ready is not None and b == 0:
                    pe.wait_ge(ready, before + a + 1)
                ins = nc.tensor.transpose(pb[:, bank0 + b, a * P:(a + 1) * P], src[:, a, b * P:(b + 1) * P], ident)
                if a == A - 1:
                    ins.then_inc(S["turned"], 1)

        def tr_dve(dve, n, dst, B, gain=None, bank0=0):
            for b in range(0, B, 2):
                dve.wait_ge(S["turned"], TURNS[n][0] + b + 1)
                if gain:
                    ins = nc.vector.tensor_scalar(dst[:, b, :], pb[:, bank0 + b, :], col(gain, b), None, ALU.mult)
                else:
                    ins = nc.vector.tensor_copy(dst[:, b, :], pb[:, bank0 + b, :])
                ins.then_inc(S["copied_dve"], 1)

        def tr_split_dve(dve, n, high, low, done, B=ND, gain=None, bank0=0):
            half = TURNS[n][0] // 2
            for b in range(B):
                turned, g = pb[:, bank0 + b, :], col(gain, b) if gain else 1.0
                if b % 2 == 0:
                    dve.wait_ge(S["turned"], TURNS[n][0] + b + 1)
                    nc.vector.tensor_scalar(high[:, b, :], turned, g, None, ALU.mult).then_inc(S["copied_dve"], 1)
                dve.wait_ge(S["copied_act" if b % 2 else "copied_dve"], half + b // 2 + 1)
                nc.vector.scalar_tensor_tensor(out=low[:, b, :], in0=turned, scalar=g, in1=plain(high[:, b, :]),
                                               op0=ALU.mult, op1=ALU.subtract).then_inc(done, 1)

        def tr_act(act, n, dst, B, gain=None, bank0=0):
            for b in range(1, B, 2):
                act.wait_ge(S["turned"], TURNS[n][0] + b + 1)
                nc.scalar.activation(dst[:, b, :], pb[:, bank0 + b, :], ACT.Copy, scale=col(gain, b) if gain else 1.0)\
                    .then_inc(S["copied_act"], 1)

        def tr_wait(eng, n):
            eng.wait_ge(S["copied_dve"], sum(TURNS[n]) // 2)
            eng.wait_ge(S["copied_act"], sum(TURNS[n]) // 2)

        def tokens_pe(pe, base, K, src, done):
            for k in range(K):
                arrived(pe, base + k)
                for i in range(NT):
                    for h in range(2):
                        last = nc.tensor.matmul(pb[:, 2 * i + h, :], src[:, k, i * P:(i + 1) * P],
                                                tile(base + k)[:, h * 512:(h + 1) * 512],
                                                start=(k == 0), stop=(k == K - 1))
                    if k == K - 1 and i < NT - 1:
                        last.then_inc(done, 1)
                last.then_inc(S["w_used"], 1)

        def product(eng, sem, before, i, last_tile):
            if i < NT - 1:
                eng.wait_ge(sem, (NT - 1) * before + i + 1)
            else:
                eng.wait_ge(S["w_used"], last_tile + 1)

        def pair(i):
            return pb[:, 2 * i:2 * i + 2, :].rearrange("p b c -> p (b c)")

        def post_act(act, n, src, last_tile=None):
            at = POSTS.index(n)
            for i in range(NT):
                if last_tile is None:
                    act.wait_ge(S["p3_prod"], i + 1)
                else:
                    product(act, S["post_mm"], at, i, last_tile)
                if i:
                    act.wait_ge(S["post_ss"], NT * at + i)
                nc.scalar.activation(junk[:, :], src(i), ACT.Square, accum_out=ss[:, i:i + 1])\
                    .then_inc(S["post_ss"], 1)
            act.wait_ge(S["post_ms"], at + 1)
            nc.scalar.activation(rt, ms, ACT.Sqrt).then_inc(S["post_rt"], 1)

        def post_dve(dve, chain, n, src, load):
            at = POSTS.index(n)
            dve.wait_ge(S["post_ss"], NT * (at + 1))
            nc.vector.tensor_scalar(ms, ss, 1.0 / D, EPS, ALU.mult, ALU.add).then_inc(S["post_ms"], 1)
            dve.wait_ge(S["g_in"], 16 * load)
            dve.wait_ge(S["post_rt"], at + 1)
            link(dve, chain, nc.vector.reciprocal(rstd, rt))
            for i in range(NT):
                link(dve, chain, nc.vector.scalar_tensor_tensor(out=ptmp[:, i % 2, :], in0=src(i), scalar=rstd[:, i:i + 1],
                                                                in1=grow[:, :], op0=ALU.mult, op1=ALU.mult))
                nc.vector.tensor_tensor(X[:, i, :], X[:, i, :], ptmp[:, i % 2, :], ALU.add).then_inc(S["post_x"], 1)

        UNITS = [(i, kind, pr) for i in range(NT) for kind in range(3) for pr in range(4)]

        @block.tensor
        def _(pe):
            used = S["w_used"]
            pe.wait_ge(S["small_in"], 32)
            tr_pe(pe, "n1", xn, NT, ND, ready=S["norm_xn"])
            for m in range(8):
                split_features(pe, "proj", m, m, hT_r, proj_low, 0)
            pe.wait_ge(S["proj_fm_ev"], 4)
            for k in range(ND):
                last = split_columns(pe, k, W_PROJ_MLA + k // 2, k % 2, 416, 0)
                if k % 2:
                    last.then_inc(used, 1)
            pe.wait_ge(S["proj_fm_ev"], 8)
            for k in range(ND):
                last = split_columns(pe, k, W_PROJ_V + k // 3, k % 3, 280, 4)
                if k % 3 == 2 or k == ND - 1:
                    last.then_inc(used, 1)
            pe.wait_ge(S["cmp_blocks"], 4)
            pe.wait_ge(S["proj_mla_ev"], NT)
            for w in range(2):
                for half in range(2):
                    n = W_CMP + 2 * w + half
                    arrived(pe, n)
                    for l in range(16 * half, 16 * half + 16):
                        for g in range(2):
                            last = nc.tensor.matmul(pb[g * 64:g * 64 + 64, w, 0:31],
                                                    tile(n)[g * 64:g * 64 + 64, (l % 16) * 64:(l % 16 + 1) * 64],
                                                    kb[g * 64:g * 64 + 64, w, l, :], start=(l == 0), stop=(l == 31))
                    last.then_inc(used, 1)
            pe.wait_ge(S["cmp_gelu"], 5)
            for g in range(2):
                r = slice(g * 64, g * 64 + 64)
                nc.tensor.matmul(pb[r, 2, 0:31], col("w2k", 0, 64)[r, :], gk[r, 0:31], start=True, stop=True)
                last = nc.tensor.matmul(pb[:, 3 * (1 - g), 0:64], gv4[r, :], col("w2v", 0, 64)[r, :], start=True, stop=True)
            last.then_inc(S["cmp_kv"], 1)
            pe.wait_ge(S["proj_v_ev"], 2)
            pe.wait_ge(S["mla_norm"], 1)
            for b in range(3):
                for i in range(NT):
                    last = nc.tensor.transpose(pb[:, 4 + b, i * P:(i + 1) * P], chat[:, i, b * P:(b + 1) * P], ident)
                last.then_inc(S["mla_tr"], 1)
            pe.wait_ge(S["mla_tr_ev"], 3)
            pe.wait_ge(S["cmp_ready"], 1)
            for n in (W_UQ, W_UQ + 1, W_UKV):
                arrived(pe, n)
            for i in range(NT):
                if i:
                    pe.wait_ge(S["q_ev"], i)
                    pe.wait_ge(S["kv_ev"], i)
                for h in range(2):
                    for k in range(2):
                        nc.tensor.matmul(pb[:, h, 0:384], cqT[:, k, i * P:(i + 1) * P],
                                         tile(W_UQ + k)[:, h * 384:(h + 1) * 384], start=(k == 0), stop=(k == 1))
                for h in range(2):
                    last = nc.tensor.matmul(pb[:, 2 + h, :], cqT[:, 2, i * P:(i + 1) * P],
                                            tile(W_UKV)[:, h * 512:(h + 1) * 512], start=True, stop=True)
                last.then_inc(S["mla_up"], 1)
                pe.wait_ge(S["q_ev"], i + 1)
                pe.wait_ge(S["kv_ev"], i + 1)
                if i:
                    pe.wait_ge(S["qk_ev_act"], 2 * i)
                    pe.wait_ge(S["qk_ev_dve"], 2 * i)
                for w in range(2):
                    for b in range(2):
                        for h in range(4):
                            last = nc.tensor.transpose(pb[0:QK, 4 + 2 * w + b, h * P:(h + 1) * P],
                                                       qkt[:, i % 2, w, (4 * b + h) * QK:(4 * b + h + 1) * QK], ident)
                        last.then_inc(S["qk_tr"], 1)
            pe.wait_ge(S["qk_ev_act"], 2 * NT)
            pe.wait_ge(S["qk_ev_dve"], 2 * NT)
            pe.wait_ge(S["cmp_ready"], 1)
            for i in range(NT):
                for h in range(HEADS):
                    r = slice((h // 4) * 64, (h // 4) * 64 + 64)
                    last = nc.tensor.matmul(pb[:, 4 * (h // 4) + i, (h % 4) * 32:(h % 4) * 32 + 31], qT[r, h % 4, i * P:(i + 1) * P], kcT[r, 0:31],
                                            start=True, stop=True)
                if i == 0:
                    last.then_inc(used, 3)
            last.then_inc(S["cs_mm"], 1)
            pe.wait_ge(S["cs_exp"], 1)
            for i in range(NT):
                for g in range(2):
                    last = nc.tensor.transpose(pb[:, 4 + i, g * P:(g + 1) * P],
                                               Pc[:, i, 4 * g:4 * g + 4, :].rearrange("p h j -> p (h j)"), ident)
            last.then_inc(S["cs_tr"], 1)
            pe.wait_ge(S["cs_tr_ev"], 1)
            for i in range(NT):
                for g in range(2):
                    last = nc.tensor.matmul(pb[:, i, g * 256:(g + 1) * 256], PcT[:, i, g * P:(g + 1) * P], Vbd[:, g, :],
                                            start=True, stop=True)
            last.then_inc(S["cs_pv"], 1)

            pe.wait_ge(S["cs_o"], 1)

            def scores(u):
                i, kind, pr = UNITS[u]
                nk = (i + 1) * P
                if u >= 2:
                    pe.wait_ge(S["at_exp"], 2 * (u - 1))
                for hh in range(2):
                    h = 2 * pr + hh
                    dst = pb[:, 2 * (u % 2) + hh, 0:nk]
                    if kind == 2:
                        last = nc.tensor.matmul(dst, qTm[0:QK, h, i * P:(i + 1) * P], kTm[0:QK, h, 0:nk], start=True, stop=True)
                    else:
                        r = slice((h // 4) * 64, (h // 4) * 64 + 64)
                        last = nc.tensor.matmul(dst, qT[r, h % 4, i * P:(i + 1) * P], kvT[r, 2 + kind, 0:nk], start=True, stop=True)
                last.then_inc(S["at_s"], 1)

            def turn_probs(u):
                i, kind, pr = UNITS[u]
                for hh in range(2):
                    pe.wait_ge(S["at_exp"], 2 * u + hh + 1)
                    if u:
                        pe.wait_ge(S["at_ev_dve"] if hh == 0 else S["at_ev_act"], u)
                    for kt in range(i + 1):
                        last = nc.tensor.transpose(pb[:, 4 + hh, kt * P:(kt + 1) * P], Pr[:, u % 2, hh, kt * P:(kt + 1) * P], ident)
                    last.then_inc(S["at_tr"], 1)

            def values(u):
                i, kind, pr = UNITS[u]
                w = u // 4
                if pr == 0 and w >= 2:
                    pe.wait_ge(S["at_o"], w - 1)
                for hh in range(2):
                    h = 2 * pr + hh
                    pe.wait_ge(S["at_ev_dve"] if hh == 0 else S["at_ev_act"], u + 1)
                    for kt in range(i + 1):
                        v = Vm[:, kt, h * DH:(h + 1) * DH] if kind == 2 else \
                            Vsw[:, kt, kind * P + (h // 4) * DH:kind * P + (h // 4) * DH + DH]
                        last = nc.tensor.matmul(pb[:, 6 + w % 2, h * DH:(h + 1) * DH], PTs[:, u % 2, hh, kt * P:(kt + 1) * P], v,
                                                start=(kt == 0), stop=(kt == i))
                    last.then_inc(S["at_pv"], 1)

            scores(0)
            for u in range(len(UNITS)):
                if u + 1 < len(UNITS):
                    scores(u + 1)
                turn_probs(u)
                if u:
                    values(u - 1)
            values(len(UNITS) - 1)
            pe.wait_ge(S["at_o"], 12)
            tr_pe(pe, "o_nsa", O_nsa, NT, 4)
            tr_pe(pe, "o_mla", O_mla, NT, 4, bank0=4)
            tr_wait(pe, "o_nsa")
            tr_wait(pe, "o_mla")
            for m in range(ND):
                n = W_MERGE + 3 * m
                b = 4 * (m % 2)
                if m >= 2:
                    pe.wait_ge(S["mg_ev"], m - 1)
                for w in range(2):
                    split_features(pe, "merge", 3 * m + w, b + w, h_high, hT_r, 1)
                tw = parts("merge", 3 * m + 2)
                pe.wait_ge(S["w_low"], SPLIT_TILES.index(n + 2) + 1)
                pe.wait_ge(S["oT_low"], 8)
                for w, (high, low) in enumerate(((nsa_high, nsa_low), (mla_high, mla_low))):
                    for k in range(4):
                        for part, (u, src) in enumerate(((0, high), (0, low), (1, high))):
                            last = nc.tensor.matmul(pb[:, b + 2 + w, :], tw[:, u, (4 * w + k) * P:(4 * w + k + 1) * P],
                                                    src[:, k, :], start=(k == 0 and part == 0), stop=(k == 3 and part == 2))
                last.then_inc(used, 1)
            pe.wait_ge(S["mg_ev"], ND)
            split_tokens(pe, "w_o", S["post_mm"])
            pe.wait_ge(S["post_x"], NT)
            tr_pe(pe, "n2", xn, NT, ND, ready=S["norm_xn"], before=NT)
            for j in range(NF):
                if j >= 4:
                    pe.wait_ge(S["up_dve"], 2 * (j - 3))
                for w in range(2):
                    split_features(pe, "up", 2 * j + w, 2 * (j % 4) + w, hT_r, up_low, 2)
            pe.wait_ge(S["up_g"], NF)
            split_tokens(pe, "down", S["post_mm"])
            pe.wait_ge(S["post_x"], 2 * NT)
            pe.wait_ge(S["p_in"], 16)
            tokens_pe(pe, W_PLE, 2, pTs, S["ple_mm"])
            pe.wait_ge(S["ple_ev"], NT)
            tr_pe(pe, "x2", X, NT, ND)
            tr_wait(pe, "x2")
            split_tokens(pe, "pgate", S["pg_mm"])
            second_pe(pe)

        @block.scalar
        def _(act):
            for i in range(NT):
                act.dma_start(X[:, i, :], x[i * P:(i + 1) * P, :]).then_inc(S["x_in"], 16)
            norm_act(act, "n1", S["x_in"], 16 * NT, step=16)
            act.wait_ge(S["small_in"], 32)
            for m in range(2):
                high_at(act, m)
            tr_act(act, "n1", hT_r, ND, "g_pre_mix")
            for m in range(8):
                high_at(act, m + 2)
                act.wait_ge(S["w_used"], W_PROJ_FM + m + 1)
                dst = qT[:, m, :] if m < 4 else kvT[:, m - 4, :]
                nc.scalar.activation(dst, pb[:, m, :], ACT.Copy, scale=DH ** -0.5 if m < 4 else 1.0)\
                    .then_inc(S["proj_fm_ev"], 1)
            for m in range(W_PROJ_MLA + 2, W_PROJ_V + 2):
                high_at(act, m)
            for i in range(NT):
                act.wait_ge(S["w_used"], W_PROJ_V)
                nc.scalar.activation(cqkv[:, i, :], pb[:, i, 0:416], ACT.Copy).then_inc(S["proj_mla_ev"], 1)
            high_at(act, W_CMP - 1)
            act.wait_ge(S["w_used"], W_CMP)
            nc.scalar.activation(Vsw[:, :, :], pb[:, 4:8, 0:256], ACT.Copy).then_inc(S["proj_v_ev"], 1)
            nc.scalar.activation(gates[:, :, :], pb[:, 4:8, 256:280], ACT.Sigmoid).then_inc(S["proj_v_ev"], 1)
            act.wait_ge(S["ang_ready"], 1)
            nc.scalar.activation(ropet[:, 0:128], ropet[:, 128:256], ACT.Sin).then_inc(S["sin_ready"], 1)
            act.wait_ge(S["mla_ms"], 1)
            nc.scalar.activation(mrt, mss, ACT.Sqrt).then_inc(S["mla_rt"], 1)
            act.wait_ge(S["w_used"], W_CMP + 2)
            nc.scalar.activation(gk[:, 0:31], pb[:, 0, 0:31], ACT.Gelu_apprx_tanh, bias=col("b1k")).then_inc(S["cmp_gelu"], 1)
            act.wait_ge(S["w_used"], W_CMP + 4)
            act.wait_ge(S["cmp_blocks"], 5)
            for q in range(4):
                nc.scalar.activation(gv4[:, 32 * q:32 * q + 31], pb[:, 1, 0:31], ACT.Gelu_apprx_tanh, bias=col("b1v"))\
                    .then_inc(S["cmp_gelu"], 1)
            for b in range(3):
                act.wait_ge(S["mla_tr"], b + 1)
                nc.scalar.activation(cqT[:, b, :], pb[:, 4 + b, :], ACT.Copy,
                                     scale=col("g_q", b) if b < 2 else col("g_kv")).then_inc(S["mla_tr_ev"], 1)
            act.wait_ge(S["h_back"], ND)
            for i in range(NT):
                act.wait_ge(S["mla_up"], i + 1)
                if i >= 2:
                    act.wait_ge(S["qk_tr"], 4 * (i - 1))
                nc.scalar.activation(qkt[:, i % 2, 0, :].rearrange("p (b c) -> p b c", b=2), pb[:, 0:2, 0:384], ACT.Copy,
                                     scale=QK_SCALE).then_inc(S["q_raw"], 1)
                for w, dst in ((0, qTm), (1, kTm)):
                    act.wait_ge(S["qk_tr"], 4 * i + 2 * w + 2)
                    nc.scalar.activation(dst[0:QK, 4:8, i * P:(i + 1) * P],
                                         pb[0:QK, 5 + 2 * w, :].rearrange("p (h c) -> p h c", h=4), ACT.Copy)\
                        .then_inc(S["qk_ev_act"], 1)
            act.wait_ge(S["cs_max"], 1)
            nc.scalar.activation(Pc[:, :, :, 0:31], Pc[:, :, :, 0:31], ACT.Exp).then_inc(S["cs_exp"], 1)

            def exps(u):
                i, kind, pr = UNITS[u]
                nk = (i + 1) * P
                act.wait_ge(S["at_max"], u + 1)
                for hh in range(2):
                    if u >= 2:
                        act.wait_ge(S["at_tr"], 2 * (u - 2) + hh + 1)
                    nc.scalar.activation(Pr[:, u % 2, hh, 0:nk], pb[:, 2 * (u % 2) + hh, 0:nk], ACT.Exp,
                                         bias=nm[:, u % 2, hh:hh + 1],
                                         accum_out=sums[:, u // 4, 2 * pr + hh:2 * pr + hh + 1]).then_inc(S["at_exp"], 1)

            def copy_turned(u):
                nk = (UNITS[u][0] + 1) * P
                act.wait_ge(S["at_tr"], 2 * u + 2)
                if u >= 2:
                    act.wait_ge(S["at_pv"], 2 * (u - 2) + 2)
                nc.scalar.activation(PTs[:, u % 2, 1, 0:nk], pb[:, 5, 0:nk], ACT.Copy).then_inc(S["at_ev_act"], 1)

            for u in range(len(UNITS)):
                exps(u)
                if u:
                    copy_turned(u - 1)
            copy_turned(len(UNITS) - 1)
            tr_act(act, "o_nsa", nsa_high, 4)
            tr_act(act, "o_mla", mla_high, 4, bank0=4)
            for m in range(2):
                high_act(act, "merge", m)
            for m in range(ND):
                b = 4 * (m % 2)
                for w in range(2):
                    high_at(act, W_CMP + 3 * m + w + 2)
                    act.wait_ge(S["w_used"], W_MERGE + 3 * m + w + 1)
                    if m >= 2:
                        act.wait_ge(S["mg_ev"], m - 1)
                    nc.scalar.activation(mgt[:, m % 2, w, :], pb[:, b + w, :], ACT.Sigmoid).then_inc(S["mg_sig"], 1)
                high_at(act, W_CMP + 3 * m + 4)
            for m in range(2, ND):
                high_act(act, "w_o", m)
            post_act(act, "p1", pair, W_UP - 1)
            norm_act(act, "n2", S["post_x"], 1 * NT)
            tr_act(act, "n2", hT_r, ND, "g_pre_ffn")
            for m in range(2):
                high_act(act, "up", m)

            def conv_last(j, w):
                m = w * NF + j
                t = 2 * j + w + 2
                high_act(act, "up" if t < 2 * NF else "down", t % (2 * NF))
                act.wait_ge(S["w_used"], W_UP + 2 * j + w + 1)
                if j >= 2:
                    act.wait_ge(S["up_g"], j - 1)
                nc.scalar.activation(cva[:, j % 2, w, :], pb[:, 2 * (j % 4) + w, :], ACT.Identity,
                                     scale=col("w_conv", 2 * 2 * NF + m), bias=col("b_conv", m)).then_inc(S["up_conv"], 1)

            for j in range(NF):
                for w in range(2):
                    conv_last(j, w)
                act.wait_ge(S["up_dve"], 2 * j + 1)
                nc.scalar.activation(ga[:, j % 2, :], cva[:, j % 2, 0, :], ACT.Gelu_apprx_tanh).then_inc(S["up_gelu"], 1)
            for m in range(2, NF):
                high_act(act, "down", m)
            post_act(act, "p2", pair, W_PLE - 1)
            for i in range(NT):
                product(act, S["ple_mm"], 0, i, W_PGATE - 1)
                nc.scalar.activation(E[:, i, :], pair(i), ACT.Copy).then_inc(S["ple_ev"], 1)
            for m in range(2):
                high_act(act, "pgate", m)
            tr_act(act, "x2", hT, ND)
            for m in range(2, ND):
                high_act(act, "pgate", m)
            for i in range(NT):
                product(act, S["pg_mm"], 0, i, W_IN2 - 1)
                nc.scalar.activation(Gs[:, i, :], pair(i), ACT.Sigmoid).then_inc(S["pg_sig"], 1)
            post_act(act, "p3", lambda i: E[:, i, :])
            second_act(act)

        @block.vector
        def _(dve):
            chain = [0]

            def L(ins):
                link(dve, chain, ins)

            norm_dve(dve, chain, "n1")
            dve.wait_ge(S["small_in"], 32)
            link(dve, chain, nc.vector.tensor_copy(tri16[:, :], cs("tri")))
            link(dve, chain, nc.vector.tensor_copy(ones16[:, :], cs("ones")))
            tr_split_dve(dve, "n1", hT_r, proj_low, S["hT_low"], gain="g_pre_mix")
            dve.wait_ge(S["pos_in"], 16)
            posf = ropet[:, 256:260]
            ang = ropet[:, 264:328]
            turns = ropet[:, 328:392]
            red = ropet[:, 128:192]
            redc = ropet[:, 192:256]
            L(nc.vector.tensor_copy(posf, posi[:, :]))
            L(nc.vector.tensor_tensor(ang.rearrange("p (i f) -> p i f", i=NT), posf.unsqueeze(2).broadcast_to([P, NT, 16]),
                                      cs("inv_freq").unsqueeze(1).broadcast_to([P, NT, 16]), ALU.mult))
            reduce_angle(L, nc, ang, turns, red)
            L(nc.vector.tensor_scalar(red, red, PI_LOW, -PI_LOW, ALU.min, ALU.max))
            L(nc.vector.scalar_tensor_tensor(out=redc, in0=red, scalar=-1.0, in1=red, op0=ALU.mult, op1=ALU.max))
            nc.vector.tensor_scalar(redc, redc, -1.0, PI_HALF, ALU.mult, ALU.add).then_inc(S["ang_ready"], 1)
            dve.wait_ge(S["proj_fm_ev"], 6)
            for w in range(2):
                src = kvT[:, w, :].rearrange("p (b l) -> p l b", l=16)
                for half in range(2):
                    nc.vector.tensor_tensor(
                        kb[:, w, 16 * half:16 * half + 16, :], src[:, :, half:half + 31],
                        col("pos_k" if w == 0 else "pos_v", 16 * half, 16).unsqueeze(2).broadcast_to([P, 16, 31]), ALU.add)\
                        .then_inc(S["cmp_blocks"], 1)
            nc.vector.memset(gv4, 0.0).then_inc(S["cmp_blocks"], 1)
            nc.vector.memset(ar(26304, 512), 0.0)
            dve.wait_ge(S["proj_mla_ev"], NT)
            L(nc.vector.tensor_tensor(chat[:, :, :], cqkv[:, :, 0:384], cqkv[:, :, 0:384], ALU.mult))
            L(nc.vector.tensor_reduce(mrs[:, 0:4], chat[:, :, 0:256], AX.X, ALU.add))
            L(nc.vector.tensor_reduce(mrs[:, 4:8], chat[:, :, 256:384], AX.X, ALU.add))
            nc.vector.tensor_scalar(mss[:, 0:4], mrs[:, 0:4], 1.0 / 256, EPS, ALU.mult, ALU.add)
            nc.vector.tensor_scalar(mss[:, 4:8], mrs[:, 4:8], 1.0 / 128, EPS, ALU.mult, ALU.add).then_inc(S["mla_ms"], 1)
            dve.wait_ge(S["mla_rt"], 1)
            L(nc.vector.reciprocal(mrs, mrt))
            nc.vector.tensor_tensor(chat[:, :, 0:256], cqkv[:, :, 0:256], mrs[:, 0:4].unsqueeze(2).broadcast_to([P, NT, 256]), ALU.mult)
            nc.vector.tensor_tensor(chat[:, :, 256:384], cqkv[:, :, 256:384], mrs[:, 4:8].unsqueeze(2).broadcast_to([P, NT, 128]), ALU.mult)\
                .then_inc(S["mla_norm"], 1)
            dve.wait_ge(S["sin_ready"], 1)
            sin, cos = ropet[:, 0:64], ropet[:, 64:128]

            def by_tile(t):
                return t.rearrange("p (i f) -> p i f", i=NT)

            krr = ropet[:, 520:648].rearrange("p (i c) -> p i c", i=NT)
            r1, r2 = ropet[:, 648:712], ropet[:, 712:776]
            x1, x2 = cqkv[:, :, 384:400], cqkv[:, :, 400:416]
            L(nc.vector.tensor_tensor(by_tile(r1), x1, by_tile(cos), ALU.mult))
            L(nc.vector.tensor_tensor(by_tile(r2), x2, by_tile(sin), ALU.mult))
            L(nc.vector.tensor_tensor(krr[:, :, 0:16], by_tile(r1), by_tile(r2), ALU.subtract))
            L(nc.vector.tensor_tensor(by_tile(r1), x2, by_tile(cos), ALU.mult))
            L(nc.vector.tensor_tensor(by_tile(r2), x1, by_tile(sin), ALU.mult))
            L(nc.vector.tensor_tensor(krr[:, :, 16:32], by_tile(r1), by_tile(r2), ALU.add))
            dve.wait_ge(S["cmp_kv"], 1)
            nc.vector.tensor_copy(kcT[:, 0:31], pb[:, 2, 0:31])
            for g in range(2):
                for q in range(4):
                    last = nc.vector.tensor_copy(Vbd[32 * q:32 * q + 32, g, q * DH:(q + 1) * DH],
                                                 pb[32 * q:32 * q + 32, 3 * (1 - g), 0:64])
            last.then_inc(S["cmp_ready"], 1)
            q1, q2, q3, q4 = [t.rearrange("p (h c) -> p h c", h=HEADS)
                              for t in (ropet[:, 776:904], ropet[:, 264:392], ropet[:, 392:520], ropet[:, 128:256])]
            dve.wait_ge(S["h_back"], ND)
            for i in range(NT):
                dve.wait_ge(S["mla_up"], i + 1)
                if i >= 2:
                    dve.wait_ge(S["qk_tr"], 4 * (i - 1))
                kvv = pb[:, 2:4, :].rearrange("p b (h c) -> p (b h) c", c=P)
                qd = qkt[:, i % 2, 0, :].rearrange("p (h c) -> p h c", c=QK)
                kd = qkt[:, i % 2, 1, :].rearrange("p (h c) -> p h c", c=QK)
                nc.vector.tensor_copy(kd[:, :, 64:96], krr[:, i, :].unsqueeze(1).broadcast_to([P, HEADS, 32]))
                nc.vector.tensor_copy(Vm[:, i, :].rearrange("p (h c) -> p h c", c=DH), kvv[:, :, 64:128])
                nc.vector.tensor_copy(kd[:, :, 0:64], kvv[:, :, 0:64]).then_inc(S["kv_ev"], 1)
                dve.wait_ge(S["q_raw"], i + 1)
                y1, y2 = qd[:, :, 64:80], qd[:, :, 80:96]
                ci = cos[:, 16 * i:16 * i + 16].unsqueeze(1).broadcast_to([P, HEADS, 16])
                si = sin[:, 16 * i:16 * i + 16].unsqueeze(1).broadcast_to([P, HEADS, 16])
                if i:
                    dve.wait_ge(S["q_ev"], i)
                nc.vector.tensor_tensor(q1, y1, ci, ALU.mult)
                nc.vector.tensor_tensor(q2, y2, si, ALU.mult)
                nc.vector.tensor_tensor(q3, y2, ci, ALU.mult)
                L(nc.vector.tensor_tensor(q4, y1, si, ALU.mult))
                nc.vector.tensor_tensor(y1, q1, q2, ALU.subtract)
                nc.vector.tensor_tensor(y2, q3, q4, ALU.add).then_inc(S["q_ev"], 1)
                for w, dst in ((0, qTm), (1, kTm)):
                    dve.wait_ge(S["qk_tr"], 4 * i + 2 * w + 1)
                    nc.vector.tensor_copy(dst[0:QK, 0:4, i * P:(i + 1) * P],
                                          pb[0:QK, 4 + 2 * w, :].rearrange("p (h c) -> p h c", h=4))\
                        .then_inc(S["qk_ev_dve"], 1)
            dve.wait_ge(S["tab_in"], 16)
            dve.wait_ge(S["cs_mm"], 1)
            L(nc.vector.memset(ar(21216, 1024), 0.0))
            for g in range(2):
                sc = pb[:, 4 * g:4 * g + 4, 0:128].rearrange("p i (h j) -> p i h j", j=32)
                ins = nc.vector.tensor_tensor(Pc[:, :, 4 * g:4 * g + 4, 0:31], sc[:, :, :, 0:31],
                                              cmpt.rearrange("p (i h j) -> p i h j", i=NT, j=31)[:, :, 4 * g:4 * g + 4, :],
                                              ALU.add)
            L(ins)
            L(nc.vector.tensor_reduce(cmaxn.rearrange("p (i h) -> p i h", i=NT), Pc[:, :, :, 0:31], AX.X, ALU.max))
            nc.vector.tensor_tensor(Pc[:, :, :, 0:31], Pc[:, :, :, 0:31],
                                    cmaxn.rearrange("p (i h) -> p i h", i=NT).unsqueeze(3).broadcast_to([P, NT, HEADS, 31]),
                                    ALU.subtract).then_inc(S["cs_max"], 1)
            dve.wait_ge(S["cs_exp"], 1)
            L(nc.vector.tensor_reduce(csum.rearrange("p (i h) -> p i h", i=NT), Pc[:, :, :, 0:31], AX.X, ALU.add))
            L(nc.vector.reciprocal(csum, csum))
            f3 = fac.rearrange("p (i h) -> p i h", i=NT)
            dve.wait_ge(S["proj_v_ev"], 2)
            L(nc.vector.tensor_tensor(f3, csum.rearrange("p (i h) -> p i h", i=NT), gates[:, :, 0:8], ALU.mult))
            L(nc.vector.tensor_scalar(fac[:, 0:8], fac[:, 0:8], cs("row_ok"), None, ALU.mult))
            dve.wait_ge(S["cs_tr"], 1)
            nc.vector.tensor_copy(PcT[:, :, :], pb[:, 4:8, 0:256]).then_inc(S["cs_tr_ev"], 1)
            dve.wait_ge(S["cs_pv"], 1)
            nc.vector.tensor_tensor(ar(17120, 2048).rearrange("p (a c) -> p a c", c=DH),
                                    pb[:, 0:4, :].rearrange("p i (h c) -> p (i h) c", c=DH),
                                    fac.unsqueeze(2).broadcast_to([P, 32, DH]), ALU.mult).then_inc(S["cs_o"], 1)
            dve.wait_ge(S["cs_o"], 1)

            alibi = cs("alibi")
            rinv = st[:, 428:436]
            otmp = junk[:, 0:512]

            def mask_max(u):
                i, kind, pr = UNITS[u]
                nk = (i + 1) * P
                b = 2 * (u % 2)
                dve.wait_ge(S["at_s"], u + 1)
                if kind == 2:
                    L(nc.vector.tensor_tensor(pb[:, b:b + 2, nk - P:nk], pb[:, b:b + 2, nk - P:nk],
                                              cs("diag").unsqueeze(1).broadcast_to([P, 2, P]), ALU.add))
                else:
                    for hh in range(2):
                        ins = nc.vector.scalar_tensor_tensor(out=pb[:, b + hh, 0:nk], in0=alibi[:, 512 - nk:512],
                                                             scalar=SLOPES[2 * pr + hh], in1=pb[:, b + hh, 0:nk],
                                                             op0=ALU.mult, op1=ALU.add)
                    L(ins)
                nc.vector.tensor_reduce(nm[:, u % 2, :], pb[:, b:b + 2, 0:nk], AX.X, ALU.max, negate=True)\
                    .then_inc(S["at_max"], 1)

            def copy_turned(u):
                nk = (UNITS[u][0] + 1) * P
                dve.wait_ge(S["at_tr"], 2 * u + 1)
                if u >= 2:
                    dve.wait_ge(S["at_pv"], 2 * (u - 2) + 1)
                nc.vector.tensor_copy(PTs[:, u % 2, 0, 0:nk], pb[:, 4, 0:nk]).then_inc(S["at_ev_dve"], 1)

            def combine(w):
                i, kind = w // 3, w % 3
                dve.wait_ge(S["at_pv"], 8 * (w + 1))
                L(nc.vector.reciprocal(rinv, sums[:, w, :]))
                if kind < 2:
                    L(nc.vector.tensor_tensor(rinv, rinv, gates[:, i, 8 * (kind + 1):8 * (kind + 2)], ALU.mult))
                dst = O_mla[:, i, :] if kind == 2 else otmp
                ins = nc.vector.tensor_tensor(dst.rearrange("p (h c) -> p h c", c=DH),
                                              pb[:, 6 + w % 2, :].rearrange("p (h c) -> p h c", c=DH),
                                              rinv.unsqueeze(2).broadcast_to([P, HEADS, DH]), ALU.mult)
                if kind < 2:
                    L(ins)
                    ins = nc.vector.tensor_tensor(O_nsa[:, i, :], O_nsa[:, i, :], otmp, ALU.add)
                ins.then_inc(S["at_o"], 1)
                dve.wait_ge(S["at_o"], w + 1)

            for u in range(len(UNITS)):
                mask_max(u)
                if u:
                    copy_turned(u - 1)
                if u % 4 == 1 and u >= 5:
                    combine((u - 5) // 4)
            copy_turned(len(UNITS) - 1)
            combine(11)
            for k in range(ND):
                L(nc.vector.tensor_copy(h_high[:, k, :], hT[:, k, :]))
                nc.vector.tensor_tensor(hT_r[:, k, :], hT[:, k, :], plain(h_high[:, k, :]), ALU.subtract)\
                    .then_inc(S["hT_low"], 1)
            tr_split_dve(dve, "o_nsa", nsa_high, nsa_low, S["oT_low"], B=4)
            tr_split_dve(dve, "o_mla", mla_high, mla_low, S["oT_low"], B=4, bank0=4)
            for m in range(ND):
                b = 4 * (m % 2)
                dve.wait_ge(S["mg_sig"], 2 * m + 2)
                dve.wait_ge(S["w_used"], W_MERGE + 3 * m + 3)
                for w in range(2):
                    ins = nc.vector.tensor_tensor(mgt[:, m % 2, 2 + w, :], mgt[:, m % 2, w, :], pb[:, b + 2 + w, :], ALU.mult)
                L(ins)
                nc.vector.tensor_tensor(mT[:, m, :], mgt[:, m % 2, 2, :], mgt[:, m % 2, 3, :], ALU.add).then_inc(S["mg_ev"], 1)
            dve.wait_ge(S["mg_ev"], ND)
            split_dve(dve, chain, "w_o", mT)
            post_dve(dve, chain, "p1", pair, 1)
            dve.wait_ge(S["post_x"], 1 * NT)
            norm_dve(dve, chain, "n2")
            tr_split_dve(dve, "n2", hT_r, up_low, S["hT_low"], gain="g_pre_ffn")
            for j in range(NF):
                for w in range(2):
                    m = w * NF + j
                    dve.wait_ge(S["up_conv"], 2 * j + w + 1)
                    c = cva[:, j % 2, w, :]
                    u = pb[:, 2 * (j % 4) + w, :]
                    L(nc.vector.scalar_tensor_tensor(out=c[:, 1:T], in0=u[:, 0:T - 1], scalar=col("w_conv", 2 * NF + m),
                                                     in1=c[:, 1:T], op0=ALU.mult, op1=ALU.add))
                    nc.vector.scalar_tensor_tensor(out=c[:, 2:T], in0=u[:, 0:T - 2], scalar=col("w_conv", m),
                                                   in1=c[:, 2:T], op0=ALU.mult, op1=ALU.add).then_inc(S["up_dve"], 1)
                dve.wait_ge(S["up_dve"], 2 * j + 2)
                dve.wait_ge(S["up_gelu"], j + 1)
                nc.vector.tensor_tensor(gT[:, j, :], ga[:, j % 2, :], cva[:, j % 2, 1, :], ALU.mult).then_inc(S["up_g"], 1)
            dve.wait_ge(S["up_g"], NF)
            split_dve(dve, chain, "down", gT)
            post_dve(dve, chain, "p2", pair, 2)
            dve.wait_ge(S["post_x"], 2 * NT)
            tr_dve(dve, "x2", hT, ND)
            tr_wait(dve, "x2")
            split_dve(dve, chain, "pgate", hT)
            for i in range(NT):
                dve.wait_ge(S["pg_sig"], i + 1)
                nc.vector.tensor_tensor(E[:, i, :], E[:, i, :], Gs[:, i, :], ALU.mult).then_inc(S["p3_prod"], 1)
            dve.wait_ge(S["p3_prod"], NT)
            post_dve(dve, chain, "p3", lambda i: E[:, i, :], 3)
            dve.wait_ge(S["post_x"], 3 * NT)
            second_dve(dve, chain)



TWO_PI = 6.283185307179586
PI_HALF = 1.5707963267948966
TWO_PI_A = 6.28125
TWO_PI_B = float(np.float32(np.round((TWO_PI - 6.28125) * 2.0 ** 21) / 2.0 ** 21))
TWO_PI_C = TWO_PI - TWO_PI_A - TWO_PI_B
ROUND = 12582912.0


def reduce_angle(L, nc, ang, turns, red):
    L(nc.vector.tensor_scalar(turns, ang, 1.0 / TWO_PI, ROUND, ALU.mult, ALU.add))
    L(nc.vector.tensor_scalar(turns, turns, ROUND, None, ALU.subtract))
    L(nc.vector.scalar_tensor_tensor(out=red, in0=turns, scalar=-TWO_PI_A, in1=ang, op0=ALU.mult, op1=ALU.add))
    L(nc.vector.scalar_tensor_tensor(out=red, in0=turns, scalar=-TWO_PI_B, in1=red, op0=ALU.mult, op1=ALU.add))
    L(nc.vector.scalar_tensor_tensor(out=red, in0=turns, scalar=-TWO_PI_C, in1=red, op0=ALU.mult, op1=ALU.add))


PI_LOW = 3.1415925025939941


def constants():
    f32 = np.float32
    p = np.arange(P)
    c = {"ident": np.eye(P), "ones": np.ones((P, P)), "diag": np.where(p[None, :] <= p[:, None], 0.0, NEG)}
    dist = p[:, None] - (np.arange(512)[None, :] - 384)
    c["alibi"] = np.where(dist >= 0, -dist, NEG)
    inv = (np.float32(10000.0) ** (-np.arange(0, 32, 2, dtype=f32) / f32(32))).astype(f32)
    c["inv_freq"] = np.broadcast_to(inv, (P, 16))
    c["row_ok"] = (p >= 31)[:, None]
    a = 2 * np.pi * np.outer(np.arange(64), np.arange(64)) / 64
    z = np.zeros((64, 64))
    c["dft64"] = np.block([[np.cos(a), z, -np.sin(a), z], [z, np.cos(a), z, -np.sin(a)]])
    c["giota"] = np.broadcast_to(np.arange(4), (P, 4))
    c["eiota"] = np.broadcast_to(np.arange(32), (P, 32))
    c["tri"] = p[:, None] < p[None, :]
    c["iota"] = np.broadcast_to(p, (P, P))
    c["choice"] = p[:, None] + P * np.arange(2 * NT)[None, :] - 2 * T
    c["empty"] = 2 * T + p[:, None]
    csts = np.concatenate([c[n].astype(f32) for n, _ in CSTS], axis=1)
    t = np.arange(T).reshape(NT, P).T
    dist = t[:, :, None] - (np.arange(N_CMP) * 16 + 31)[None, None, :]
    slopes = np.array(SLOPES)
    tab = np.where(dist[:, :, None, :] >= 0, -slopes[None, None, :, None] * dist[:, :, None, :], NEG)
    return csts, tab.astype(f32).reshape(P, -1)


def transforms():
    n = np.arange(T)
    a = 2 * np.pi * (np.outer(n, n) % (2 * T)) / (2 * T)
    C, Sn, alt = np.cos(a), np.sin(a), (-1.0) ** n

    def blocks(c, s, m):
        cols = slice(m * P, (m + 1) * P)
        return np.concatenate([by_rows(c[:, cols]), by_rows(s[:, cols])], axis=1).astype(np.float32)

    Cn, Sa = C.copy(), Sn.copy()
    Cn[:, 0] = alt
    Sa[:, 0] = alt
    forward = [blocks(Cn, Sa, 0)] + [blocks(C, Sn, m) for m in range(4)]
    Ci, Si = C.copy(), Sn.copy()
    Ci[0, :] = 0.5
    Si[0, :] = 0.5 * alt
    inverse = [blocks(Ci, Si, i) for i in range(NT)]
    b = 2 * np.pi * (np.outer(n, n) % T) / T
    scale = 1.0 / np.sqrt(64.0 * T)
    time = [blocks(np.cos(b) * scale, np.sin(b) * scale, i) for i in range(NT)]
    return (W_DFT, forward), (W_IDFT, inverse), (W_FFT, time)


def filter_tables():
    f32 = np.float32
    t = np.linspace(0.0, 1.0, T, dtype=f32)[:, None]
    w = (f32(2.0 * np.pi / T) * np.arange(T, dtype=f32))[:, None]
    f = np.linspace(1e-4, 15, 16, dtype=f32)[None, :]
    z = np.concatenate([t, np.cos(f * w), -np.sin(f * w)], axis=-1)
    deltas = np.abs(np.linspace(np.log(1e-2) / 1.5, np.log(1e-2) / 0.3, CH, dtype=f32))
    zp = np.zeros((P, T), f32)
    zp[:33] = z.T
    return zp, by_rows(np.exp(-t * deltas).astype(f32)).reshape(P, -1)


def by_rows(w):
    return w.reshape(-1, P, w.shape[-1]).transpose(1, 0, 2)


def pack(tiles, dest, at, m):
    flat = tiles.reshape(P, -1)
    dest[at + m, :, :flat.shape[1]] = flat


def kernel(**a):
    import concourse.bacc as bacc
    from concourse.bass_utils import run_bass_kernel_spmd

    a = {k: np.asarray(v) for k, v in a.items()}
    f32 = np.float32
    W = np.zeros((N_TILES, P, 1024), f32)
    w_in = a["w_in"][0]
    put = lambda tiles, at, m: pack(tiles, W, at, m)
    for m in range(4):
        cols = [*range(m * 64, m * 64 + 64), *range((m + 4) * 64, (m + 4) * 64 + 64)]
        put(by_rows(w_in[:, cols]), W_PROJ_FM, m)
    for m, part in enumerate((0, 1, 2, 4)):
        put(by_rows(w_in[:, 512 + part * 128:512 + part * 128 + 128]), W_PROJ_FM, 4 + m)
    mla = by_rows(w_in[:, 1304:1720])
    for m in range(4):
        put(mla[:, 2 * m:2 * m + 2], W_PROJ_MLA, m)
    vv = by_rows(np.concatenate([w_in[:, 896:1024], w_in[:, 1152:1304]], axis=1))
    for m in range(3):
        put(vv[:, 3 * m:3 * m + 3], W_PROJ_V, m)
    for w, name in enumerate(("nsa_ck_w1", "nsa_cv_w1")):
        w1 = a[name][0].reshape(32, 64, 64).transpose(1, 0, 2)
        w1 = np.concatenate([w1, w1], axis=0)
        for half in range(2):
            put(w1[:, 16 * half:16 * half + 16], W_CMP, 2 * w + half)
    uq = by_rows(a["mla_w_uq"][0])
    put(uq[:, 0], W_UQ, 0)
    put(uq[:, 1], W_UQ, 1)
    put(a["mla_w_ukv"][0], W_UKV, 0)
    for m in range(ND):
        s = slice(m * P, m * P + P)
        put(by_rows(w_in[:, 1720:2744][:, s]), W_MERGE, 3 * m)
        put(by_rows(w_in[:, 2744:3768][:, s]), W_MERGE, 3 * m + 1)
        put(np.concatenate([by_rows(a["w_br_nsa"][0][:, s]), by_rows(a["w_br_mla"][0][:, s])], axis=1), W_MERGE, 3 * m + 2)
    for name, at in (("w_o", W_O), ("w_down", W_DOWN), ("w_ple", W_PLE), ("w_ple_gate", W_PGATE), ("w_out_2", W_OUT2)):
        w = by_rows(a[name][0])
        for k in range(w.shape[1]):
            put(w[:, k], at, k)
    w_up = a["w_up"][0]
    for j in range(NF):
        for w in range(2):
            o = w * D_FF + j * P
            put(by_rows(w_up[:, o:o + P]), W_UP, 2 * j + w)
    w_in2 = a["w_in_2"][0]
    for m in range(16):
        put(by_rows(w_in2[:, m * P:(m + 1) * P]), W_IN2, m)
    for at, tiles in transforms():
        for m, t in enumerate(tiles):
            put(t, at, m)
    put(by_rows(np.concatenate([a["w_group_2"][0], a["w_router_2"][0].transpose(1, 0, 2).reshape(D, 32)], axis=1)), W_ROUTE, 0)
    experts = W[W_EXP:].reshape(N_EXP, 3, 4, P, 1024)
    for w, name in enumerate(("w_gate_2", "w_up_2")):
        experts[:, w] = a[name][0].reshape(N_EXP, 4, 2, P, 512).transpose(0, 1, 3, 2, 4).reshape(N_EXP, 4, P, 1024)
    experts[:, 2] = a["w_down_2"][0].reshape(N_EXP, 4, P, 1024)
    vec = lambda v: v.reshape(-1, P).T
    twice = lambda v: np.concatenate([v, v], axis=0)
    low = lambda v: np.concatenate([v, np.zeros((P - v.shape[0], v.shape[1]), f32)], axis=0)
    c = {"g_pre_mix": vec(a["g_pre_mix"][0]), "g_pre_ffn": vec(a["g_pre_ffn"][0]), "norm1": vec(a["norm1_g_2"][0]),
         "norm2": vec(a["norm2_g_2"][0]), "mix_g": vec(a["mix_g_2"][0]), "g_q": vec(a["mla_g_q"][0]),
         "g_kv": vec(a["mla_g_kv"][0]), "w_conv": vec(a["w_conv"][0].reshape(-1)), "b_conv": vec(a["b_conv"][0]),
         "conv_w": vec(a["conv_w_2"][0].reshape(-1)), "conv_b": vec(a["conv_b_2"][0]),
         "b1k": twice(a["nsa_ck_b1"][0][:, None]), "b1v": twice(a["nsa_cv_b1"][0][:, None]),
         "w2k": twice(a["nsa_ck_w2"][0]), "w2v": twice(a["nsa_cv_w2"][0]),
         "pos_k": twice(a["nsa_pos_k"][0].T), "pos_v": twice(a["nsa_pos_v"][0].T),
         "f_b_in": low(a["f_b_in_2"][0][:, None]), "f_freq": low(a["f_freq_2"][0].T), "f_b_mid": low(a["f_b_mid_2"][0].T),
         "f_w_in": low(a["f_w_in_2"][0]), "r_bias": np.broadcast_to(np.concatenate([a["b_group_2"][0], a["b_router_2"][0].reshape(-1)]), (P, 36)),
         "f_w_mid": low(a["f_w_mid_2"][0].transpose(1, 0, 2).reshape(64, 128))}
    cols = np.concatenate([c[n] for n, _ in COLS], axis=1)
    csts, cmp_tab = constants()
    ins = {"stream": W, "x": a["x"][0], "cols": cols, "csts": csts, "cmp_tab": cmp_tab,
           "pos": np.ascontiguousarray(a["positions"][0].reshape(NT, P).T),
           "grows": np.stack([np.broadcast_to(v, (P, D)) for v in (a["g_post_mix"][0], a["g_post_ffn"][0], a["g_ple"][0],
                                                             a["norm2_g_2"][0], a["final_g_2"])]),
           "pT": np.ascontiguousarray(by_rows(np.ascontiguousarray(a["p"][0, 0].T))).reshape(P, -1)}
    ins["fconst"], ins["decay"] = filter_tables()
    ins["fwout"] = a["f_w_out_2"][0]
    ins["frow"] = np.broadcast_to(a["f_bias_2"][0], (P, CH))
    nc = bacc.Bacc("TRN2", target_bir_lowering=False, num_devices=1)
    ap = {}
    for n, v in ins.items():
        v = ins[n] = np.ascontiguousarray(v)
        ap[n] = nc.dram_tensor(n, v.shape, mybir.dt.from_np(v.dtype), kind="ExternalInput").ap()
    out = nc.dram_tensor("out", (T, D), F32, kind="ExternalOutput").ap()
    build(nc, ap["stream"], ap["x"], ap["cols"], ap["csts"], ap["cmp_tab"], ap["pos"], ap["grows"],
          ap["pT"], ap["fconst"], ap["fwout"], ap["decay"], ap["frow"], out)
    r = run_bass_kernel_spmd(nc, [ins], core_ids=[0])
    return r.results[0]["out"].reshape(1, T, D)
```
